# Optimizing a Trainium2 kernel written in Bass

```python
import jax, jax.numpy as jnp
from jax import lax
import numpy as np
import math
import jax
import jax.numpy as jnp

D_MODEL = 1024
BATCH = 1
SEQ = 256
DEPTH = 1

D_MIX = D_MODEL
SSD_WIDTH = D_MIX // 2
SSD_HEAD_DIM = 64
SSD_HEADS = SSD_WIDTH // SSD_HEAD_DIM
SSD_GROUPS = 2
SSD_STATE = 128
SSD_CONV = 4
SSD_CHUNK = 128
ATTN_WIDTH = D_MIX // 4
ATTN_HEAD_DIM = 64
ATTN_HEADS = ATTN_WIDTH // ATTN_HEAD_DIM
ATTN_BLOCK = 128
CONV_WIDTH = D_MIX - SSD_WIDTH - ATTN_WIDTH
CONV_KERNEL = 31
XBC_WIDTH = SSD_WIDTH + 2 * SSD_GROUPS * SSD_STATE
D_IN = SSD_WIDTH + XBC_WIDTH + SSD_HEADS + 3 * ATTN_WIDTH + ATTN_HEADS + 2 * CONV_WIDTH
N_EXPERT_GROUPS = 4
EXPERTS_PER_GROUP = 8
N_EXPERTS = N_EXPERT_GROUPS * EXPERTS_PER_GROUP
TOP_K = 2
D_EXPERT = 512
MOE_BLOCK = 256
NORM_EPS = 1e-6


def _rms(x):
    xf = x.astype(jnp.float32)
    return xf * lax.rsqrt(jnp.mean(xf * xf, axis=-1, keepdims=True) + NORM_EPS)

def rms_norm(x, g):
    return (_rms(x) * g.astype(jnp.float32)).astype(x.dtype)

def layer_norm(x, g, b):
    xf = x.astype(jnp.float32)
    mu = jnp.mean(xf, axis=-1, keepdims=True)
    var = jnp.mean(jnp.square(xf - mu), axis=-1, keepdims=True)
    y = (xf - mu) * lax.rsqrt(var + NORM_EPS) * g.astype(jnp.float32) + b.astype(jnp.float32)
    return y.astype(x.dtype)

def causal_depthwise_conv(x, w, b):
    k = w.shape[0]
    y = lax.conv_general_dilated(
        x, w[:, None, :].astype(x.dtype), window_strides=(1,), padding=[(k - 1, 0)],
        dimension_numbers=('NWC', 'WIO', 'NWC'), feature_group_count=x.shape[-1])
    return y + b.astype(x.dtype)

def ssd_mixer(z, xbc, dt_raw, conv_w, conv_b, dt_bias, a_log, d_skip, norm_g):
    f32 = jnp.float32
    bsz, seq, _ = z.shape
    nc = seq // SSD_CHUNK
    r = SSD_HEADS // SSD_GROUPS
    gn = SSD_GROUPS * SSD_STATE
    xbc = jax.nn.silu(causal_depthwise_conv(xbc, conv_w, conv_b))
    xs, bmat, cmat = jnp.split(xbc, [SSD_WIDTH, SSD_WIDTH + gn], axis=-1)
    dt = jax.nn.softplus(dt_raw.astype(f32) + dt_bias.astype(f32))
    a = -jnp.exp(a_log.astype(f32))
    x_h = xs.reshape(bsz, nc, SSD_CHUNK, SSD_GROUPS, r, SSD_HEAD_DIM).astype(f32)
    dt_c = dt.reshape(bsz, nc, SSD_CHUNK, SSD_GROUPS, r)
    xdt = x_h * dt_c[..., None]
    bm = bmat.reshape(bsz, nc, SSD_CHUNK, SSD_GROUPS, SSD_STATE).astype(f32)
    cm = cmat.reshape(bsz, nc, SSD_CHUNK, SSD_GROUPS, SSD_STATE).astype(f32)
    acs = jnp.cumsum(dt_c * a.reshape(SSD_GROUPS, r), axis=2)
    acs = acs.transpose(0, 1, 3, 4, 2)
    causal = jnp.tril(jnp.ones((SSD_CHUNK, SSD_CHUNK), dtype=bool))
    decay_in = jnp.exp(jnp.where(causal, acs[..., :, None] - acs[..., None, :], -jnp.inf))
    cb = jnp.einsum('bclgn,bcsgn->bcgls', cm, bm)
    y_diag = jnp.einsum('bcgls,bcgrls,bcsgrp->bclgrp', cb, decay_in, xdt)
    decay_to_end = jnp.exp(acs[..., -1:] - acs)
    states = jnp.einsum('bclgn,bcgrl,bclgrp->bcgrpn', bm, decay_to_end, xdt)
    chunk_decay = jnp.exp(acs[..., -1])

    def step(h, inp):
        st, dec = inp
        return h * dec[..., None, None] + st, h

    h0 = jnp.zeros_like(states[:, 0])
    _, prev = lax.scan(step, h0, (states.swapaxes(0, 1), chunk_decay.swapaxes(0, 1)))
    prev = prev.swapaxes(0, 1)
    y_off = jnp.einsum('bclgn,bcgrpn,bcgrl->bclgrp', cm, prev, jnp.exp(acs))
    y = y_diag + y_off + x_h * d_skip.astype(f32).reshape(SSD_GROUPS, r, 1)
    y = y.reshape(bsz, seq, SSD_GROUPS, r * SSD_HEAD_DIM)
    y = y * jax.nn.silu(z.astype(f32)).reshape(bsz, seq, SSD_GROUPS, r * SSD_HEAD_DIM)
    y = _rms(y).reshape(bsz, seq, SSD_WIDTH) * norm_g.astype(f32)
    return y.astype(z.dtype)

def forgetting_attention(q, k, v, f_logit, f_bias, norm_g):
    f32 = jnp.float32
    bsz, seq, _ = q.shape
    nb = seq // ATTN_BLOCK
    scale = ATTN_HEAD_DIM ** -0.5
    qh = q.reshape(bsz, seq, ATTN_HEADS, ATTN_HEAD_DIM).transpose(0, 2, 1, 3)
    kh = k.reshape(bsz, seq, ATTN_HEADS, ATTN_HEAD_DIM).transpose(0, 2, 1, 3)
    vh = v.reshape(bsz, seq, ATTN_HEADS, ATTN_HEAD_DIM).transpose(0, 2, 1, 3)
    log_f = jax.nn.log_sigmoid(f_logit.astype(f32) + f_bias.astype(f32))
    cum = jnp.cumsum(log_f, axis=1).transpose(0, 2, 1)
    qb = qh.reshape(bsz, ATTN_HEADS, nb, ATTN_BLOCK, ATTN_HEAD_DIM).transpose(2, 0, 1, 3, 4)
    cb = cum.reshape(bsz, ATTN_HEADS, nb, ATTN_BLOCK).transpose(2, 0, 1, 3)
    k_pos = jnp.arange(seq)

    def block(args):
        qi, ci, i = args
        s = jnp.einsum('bhqd,bhkd->bhqk', qi, kh).astype(f32) * scale
        s = s + ci[..., :, None] - cum[:, :, None, :]
        q_pos = i * ATTN_BLOCK + jnp.arange(ATTN_BLOCK)
        s = jnp.where(k_pos[None, :] <= q_pos[:, None], s, -jnp.inf)
        p = jax.nn.softmax(s, axis=-1)
        return jnp.einsum('bhqk,bhkd->bhqd', p.astype(vh.dtype), vh)

    o = lax.map(block, (qb, cb, jnp.arange(nb)))
    o = o.transpose(1, 0, 3, 2, 4).reshape(bsz, seq, ATTN_WIDTH)
    return rms_norm(o, norm_g)

def conformer_conv(glu_a, glu_b, conv_w, conv_b, ln_g, ln_b):
    u = glu_a * jax.nn.sigmoid(glu_b)
    u = causal_depthwise_conv(u, conv_w, conv_b)
    u = layer_norm(u, ln_g, ln_b)
    return jax.nn.silu(u)

def hybrid_mixer(h, w_in, ssd_conv_w, ssd_conv_b, ssd_dt_bias, ssd_a_log, ssd_d, ssd_norm_g,
                 fox_f_bias, fox_norm_g, cm_conv_w, cm_conv_b, cm_ln_g, cm_ln_b, w_out):
    sizes = (SSD_WIDTH, XBC_WIDTH, SSD_HEADS, ATTN_WIDTH, ATTN_WIDTH, ATTN_WIDTH,
             ATTN_HEADS, CONV_WIDTH, CONV_WIDTH)
    splits = np.cumsum(sizes)[:-1].tolist()
    proj = h @ w_in
    z, xbc, dt_raw, q, k, v, f_logit, glu_a, glu_b = jnp.split(proj, splits, axis=-1)
    y_ssd = ssd_mixer(z, xbc, dt_raw, ssd_conv_w, ssd_conv_b, ssd_dt_bias, ssd_a_log, ssd_d, ssd_norm_g)
    y_att = forgetting_attention(q, k, v, f_logit, fox_f_bias, fox_norm_g)
    y_cnv = conformer_conv(glu_a, glu_b, cm_conv_w, cm_conv_b, cm_ln_g, cm_ln_b)
    y = jnp.concatenate([y_ssd.astype(h.dtype), y_att.astype(h.dtype), y_cnv.astype(h.dtype)], axis=-1)
    return y @ w_out

def hierarchical_moe(h, w_rg, b_rg, w_re, b_re, w_gate, w_up, w_down):
    f32 = jnp.float32
    bsz, seq, d = h.shape
    m = bsz * seq
    hf = h.reshape(m, d)
    p_g = jax.nn.softmax((hf @ w_rg + b_rg).astype(f32), axis=-1)
    g_sel = jnp.argmax(p_g, axis=-1).astype(jnp.int32)
    p_gsel = jnp.take_along_axis(p_g, g_sel[:, None], axis=-1)
    e_logits = (hf @ w_re + b_re).astype(f32).reshape(m, N_EXPERT_GROUPS, EXPERTS_PER_GROUP)
    e_logits = jnp.take_along_axis(e_logits, g_sel[:, None, None], axis=1)[:, 0]
    top_p, top_i = lax.top_k(jax.nn.softmax(e_logits, axis=-1), TOP_K)
    weights = top_p / jnp.sum(top_p, axis=-1, keepdims=True) * p_gsel
    expert = g_sel[:, None] * EXPERTS_PER_GROUP + top_i.astype(jnp.int32)
    n_assign = m * TOP_K
    flat_e = expert.reshape(-1)
    flat_w = weights.reshape(-1)
    flat_tok = jnp.arange(n_assign, dtype=jnp.int32) // TOP_K
    order = jnp.argsort(flat_e)
    se, stok, sw = flat_e[order], flat_tok[order], flat_w[order]
    counts = jnp.zeros((N_EXPERTS,), jnp.int32).at[flat_e].add(1)
    padded = (counts + MOE_BLOCK - 1) // MOE_BLOCK * MOE_BLOCK
    start = jnp.cumsum(counts) - counts
    pad_end = jnp.cumsum(padded)
    pad_start = pad_end - padded
    dest = pad_start[se] + jnp.arange(n_assign, dtype=jnp.int32) - start[se]
    n_blocks = (n_assign + MOE_BLOCK - 1) // MOE_BLOCK + N_EXPERTS
    rows = n_blocks * MOE_BLOCK
    xs = jnp.zeros((rows, d), h.dtype).at[dest].set(hf[stok])
    block_e = jnp.minimum(
        jnp.searchsorted(pad_end, jnp.arange(n_blocks, dtype=jnp.int32) * MOE_BLOCK, side='right'),
        N_EXPERTS - 1)

    def expert_block(args):
        xb, e = args
        hid = jax.nn.silu(xb @ w_gate[e]) * (xb @ w_up[e])
        return hid @ w_down[e]

    ys = lax.map(expert_block, (xs.reshape(n_blocks, MOE_BLOCK, d), block_e)).reshape(rows, d)
    contrib = (ys[dest] * sw[:, None]).astype(h.dtype)
    out = jnp.zeros((m, d), h.dtype).at[stok].add(contrib)
    return out.reshape(bsz, seq, d)

def first_inputs(seed: int = 0) -> dict:
    key = jax.random.key(seed)
    ks = jax.random.split(key, 32)
    nrm = jax.random.normal
    uni = jax.random.uniform
    f32 = jnp.float32
    dt0 = jnp.exp(uni(ks[8], (DEPTH, SSD_HEADS), f32, np.log(1e-3), np.log(1e-1)))
    return {
        'x': nrm(ks[0], (BATCH, SEQ, D_MODEL), f32),
        'c': nrm(ks[1], (BATCH, D_MODEL), f32),
        'ada_w': nrm(ks[2], (DEPTH, D_MODEL, 6 * D_MODEL), f32) * (0.5 * D_MODEL ** -0.5),
        'ada_b': 0.02 * nrm(ks[3], (DEPTH, 6 * D_MODEL), f32),
        'norm_mix_g': 1.0 + 0.02 * nrm(ks[4], (DEPTH, D_MODEL), f32),
        'w_in': nrm(ks[5], (DEPTH, D_MODEL, D_IN), f32) * D_MODEL ** -0.5,
        'ssd_conv_w': nrm(ks[6], (DEPTH, SSD_CONV, XBC_WIDTH), f32) * SSD_CONV ** -0.5,
        'ssd_conv_b': 0.02 * nrm(ks[7], (DEPTH, XBC_WIDTH), f32),
        'ssd_dt_bias': dt0 + jnp.log(-jnp.expm1(-dt0)),
        'ssd_a_log': jnp.log(uni(ks[9], (DEPTH, SSD_HEADS), f32, 1.0, 16.0)),
        'ssd_d': 1.0 + 0.02 * nrm(ks[10], (DEPTH, SSD_HEADS), f32),
        'ssd_norm_g': 1.0 + 0.02 * nrm(ks[11], (DEPTH, SSD_WIDTH), f32),
        'fox_f_bias': uni(ks[12], (DEPTH, ATTN_HEADS), f32, 1.0, 4.0),
        'fox_norm_g': 1.0 + 0.02 * nrm(ks[13], (DEPTH, ATTN_WIDTH), f32),
        'cm_conv_w': nrm(ks[14], (DEPTH, CONV_KERNEL, CONV_WIDTH), f32) * CONV_KERNEL ** -0.5,
        'cm_conv_b': 0.02 * nrm(ks[15], (DEPTH, CONV_WIDTH), f32),
        'cm_ln_g': 1.0 + 0.02 * nrm(ks[16], (DEPTH, CONV_WIDTH), f32),
        'cm_ln_b': 0.02 * nrm(ks[17], (DEPTH, CONV_WIDTH), f32),
        'w_out': nrm(ks[18], (DEPTH, D_MIX, D_MODEL), f32) * D_MIX ** -0.5,
        'norm_ffn_g': 1.0 + 0.02 * nrm(ks[19], (DEPTH, D_MODEL), f32),
        'w_router_group': nrm(ks[20], (DEPTH, D_MODEL, N_EXPERT_GROUPS), f32) * D_MODEL ** -0.5,
        'b_router_group': 0.01 * nrm(ks[21], (DEPTH, N_EXPERT_GROUPS), f32),
        'w_router_expert': nrm(ks[22], (DEPTH, D_MODEL, N_EXPERTS), f32) * D_MODEL ** -0.5,
        'b_router_expert': 0.01 * nrm(ks[23], (DEPTH, N_EXPERTS), f32),
        'w_gate': nrm(ks[24], (DEPTH, N_EXPERTS, D_MODEL, D_EXPERT), f32) * D_MODEL ** -0.5,
        'w_up': nrm(ks[25], (DEPTH, N_EXPERTS, D_MODEL, D_EXPERT), f32) * D_MODEL ** -0.5,
        'w_down': nrm(ks[26], (DEPTH, N_EXPERTS, D_EXPERT, D_MODEL), f32) * D_EXPERT ** -0.5,
        'final_norm_g': 1.0 + 0.02 * nrm(ks[27], (D_MODEL,), f32),
    }

def first_block(x, c, ada_w, ada_b, norm_mix_g, w_in, ssd_conv_w, ssd_conv_b, ssd_dt_bias,
              ssd_a_log, ssd_d, ssd_norm_g, fox_f_bias, fox_norm_g, cm_conv_w, cm_conv_b,
              cm_ln_g, cm_ln_b, w_out, norm_ffn_g, w_router_group, b_router_group,
              w_router_expert, b_router_expert, w_gate, w_up, w_down, final_norm_g):
    cond = jax.nn.silu(c)
    for l in range(DEPTH):
        mod = (cond @ ada_w[l] + ada_b[l])[:, None, :]
        sh_m, sc_m, g_m, sh_f, sc_f, g_f = jnp.split(mod, 6, axis=-1)
        h = rms_norm(x, norm_mix_g[l]) * (1.0 + sc_m) + sh_m
        y = hybrid_mixer(h, w_in[l], ssd_conv_w[l], ssd_conv_b[l], ssd_dt_bias[l], ssd_a_log[l],
                         ssd_d[l], ssd_norm_g[l], fox_f_bias[l], fox_norm_g[l], cm_conv_w[l],
                         cm_conv_b[l], cm_ln_g[l], cm_ln_b[l], w_out[l])
        x = x + g_m * y
        h = rms_norm(x, norm_ffn_g[l]) * (1.0 + sc_f) + sh_f
        y = hierarchical_moe(h, w_router_group[l], b_router_group[l], w_router_expert[l],
                             b_router_expert[l], w_gate[l], w_up[l], w_down[l])
        x = x + g_f * y
    return rms_norm(x, final_norm_g)


DEPTH_2 = 2

N_A = DEPTH_2 // 2
N_B = DEPTH_2 - N_A
PLE_DIM = 256
RWKV_HEAD = 64
RWKV_HEADS = D_MODEL // RWKV_HEAD
DECAY_LORA = 64
ICLR_LORA = 64
GN_EPS = 64e-5
DIFF_HEAD = 64
DIFF_HEADS = D_MODEL // (2 * DIFF_HEAD)
ROPE_DIMS = DIFF_HEAD // 4
ROPE_THETA = 500000.0
Q_BLOCK = 128
SUBLN_EPS = 1e-5


def rms_norm_2(x, g, eps=NORM_EPS):
    xf = x.astype(jnp.float32)
    y = xf * lax.rsqrt(jnp.mean(xf * xf, axis=-1, keepdims=True) + eps)
    return (y * g.astype(jnp.float32)).astype(x.dtype)

def rwkv7_time_mix(xn, mu, w_in, w0, w1, w2, a0, a1, a2, k_k, k_a, r_k, lnx_g, lnx_b, w_out):
    B, S, D = xn.shape
    H, N = RWKV_HEADS, RWKV_HEAD
    f32 = jnp.float32
    x_prev = jnp.pad(xn, ((0, 0), (1, 0), (0, 0)))[:, :-1]
    xmix = xn[None] + (x_prev - xn)[None] * mu[:, None, None, :]
    rkvg = jnp.einsum('cbsd,cde->cbse', xmix[:4], w_in)
    r, k, v, g = rkvg[0], rkvg[1], rkvg[2], rkvg[3]
    xw, xa = xmix[4], xmix[5]
    w_pre = (w0 + jnp.tanh(xw @ w1) @ w2).astype(f32)
    decay = jnp.exp(-jnp.exp(-jax.nn.softplus(-w_pre) - 0.5))
    a = jax.nn.sigmoid((a0 + (xa @ a1) @ a2).astype(f32))
    heads = lambda t: t.astype(f32).reshape(B, S, H, N)
    r, k, v, decay, a = heads(r), heads(k), heads(v), heads(decay), heads(a)
    kk = k * k_k.astype(f32).reshape(H, N)
    kk = kk / jnp.maximum(jnp.linalg.norm(kk, axis=-1, keepdims=True), 1e-12)
    k = k * (1.0 + (a - 1.0) * k_a.astype(f32).reshape(H, N))

    def step(state, inp):
        r_t, w_t, k_t, v_t, kk_t, a_t = inp
        s_kk = jnp.einsum('bhij,bhj->bhi', state, kk_t)
        state = (state * w_t[:, :, None, :]
                 - s_kk[..., None] * (kk_t * a_t)[:, :, None, :]
                 + v_t[..., None] * k_t[:, :, None, :])
        return state, jnp.einsum('bhij,bhj->bhi', state, r_t)

    seq_first = lambda t: jnp.swapaxes(t, 0, 1)
    state0 = jnp.zeros((B, H, N, N), f32)
    _, y = lax.scan(step, state0, (seq_first(r), seq_first(decay), seq_first(k),
                                   seq_first(v), seq_first(kk), seq_first(a)))
    y = jnp.swapaxes(y, 0, 1)
    mean = jnp.mean(y, axis=-1, keepdims=True)
    var = jnp.mean(jnp.square(y - mean), axis=-1, keepdims=True)
    y = ((y - mean) * lax.rsqrt(var + GN_EPS) * lnx_g.astype(f32).reshape(H, N)
         + lnx_b.astype(f32).reshape(H, N))
    y = y + jnp.sum(r * k * r_k.astype(f32), axis=-1, keepdims=True) * v
    y = y.reshape(B, S, D).astype(xn.dtype) * jax.nn.silu(g)
    return y @ w_out

def rope_tables(S):
    inv = ROPE_THETA ** (-jnp.arange(0, ROPE_DIMS, 2, dtype=jnp.float32) / ROPE_DIMS)
    ang = jnp.arange(S, dtype=jnp.float32)[:, None] * inv[None, :]
    return jnp.cos(ang), jnp.sin(ang)

def partial_rope(x, cos, sin):
    half = ROPE_DIMS // 2
    c = cos[None, :, None, None, :].astype(x.dtype)
    s = sin[None, :, None, None, :].astype(x.dtype)
    x1, x2 = x[..., :half], x[..., half:ROPE_DIMS]
    return jnp.concatenate([x1 * c - x2 * s, x2 * c + x1 * s, x[..., ROPE_DIMS:]], axis=-1)

def shared_kv(h, kv_norm, kv_w, cos, sin):
    B, S, D = h.shape
    kv = rms_norm_2(h, kv_norm) @ kv_w
    k = partial_rope(kv[..., :D].reshape(B, S, DIFF_HEADS, 2, DIFF_HEAD), cos, sin)
    v = kv[..., D:].reshape(B, S, DIFF_HEADS, 2 * DIFF_HEAD)
    return k.transpose(0, 2, 3, 1, 4), v.transpose(0, 2, 1, 3)

def diff_attention_mix(xn, k_sh, v_sh, w_in, lam_qk, subln_g, w_out, lam_init, cos, sin):
    B, S, D = xn.shape
    H, Dh = DIFF_HEADS, DIFF_HEAD
    f32 = jnp.float32
    proj = xn @ w_in
    q = partial_rope(proj[..., :D].reshape(B, S, H, 2, Dh), cos, sin) * (Dh ** -0.5)
    gate = proj[..., D:]
    lq = lam_qk.astype(f32)
    lam = jnp.exp(jnp.sum(lq[0] * lq[1])) - jnp.exp(jnp.sum(lq[2] * lq[3])) + lam_init
    nblk = S // Q_BLOCK
    qb = q.reshape(B, nblk, Q_BLOCK, H, 2, Dh).transpose(1, 0, 3, 4, 2, 5)
    kf = k_sh.astype(f32)
    vf = v_sh.astype(f32)
    k_pos = jnp.arange(S)

    def block(args):
        q_blk, blk = args
        s = jnp.einsum('bhcqd,bhckd->bhcqk', q_blk.astype(f32), kf)
        q_pos = blk * Q_BLOCK + jnp.arange(Q_BLOCK)
        s = jnp.where(k_pos[None, :] <= q_pos[:, None], s, -1e30)
        prob = jax.nn.softmax(s, axis=-1)
        attn = prob[:, :, 0] - lam * prob[:, :, 1]
        return jnp.einsum('bhqk,bhkv->bhqv', attn, vf)

    o = lax.map(block, (qb, jnp.arange(nblk)))
    o = o.transpose(1, 0, 3, 2, 4).reshape(B, S, H, 2 * Dh)
    o = rms_norm_2(o, subln_g, SUBLN_EPS) * (1.0 - lam_init)
    o = o.reshape(B, S, D).astype(xn.dtype) * jax.nn.silu(gate)
    return o @ w_out

def second_inputs(seed: int = 0) -> dict:
    key = jax.random.key(seed)
    ks = iter(jax.random.split(key, 32))
    D, f32 = D_MODEL, jnp.float32
    nrm = lambda shape, scale: jax.random.normal(next(ks), shape, f32) * scale
    gain = lambda shape: 1.0 + nrm(shape, 0.02)
    return {
        'x': nrm((BATCH, SEQ, D), 1.0),
        'p': nrm((DEPTH_2, BATCH, SEQ, PLE_DIM), 1.0),
        'norm_pre': gain((DEPTH_2, D)),
        'norm_post': gain((DEPTH_2, D)),
        'a_mu': jax.random.uniform(next(ks), (N_A, 6, D), f32),
        'a_w_in': nrm((N_A, 4, D, D), D ** -0.5),
        'a_w0': jax.random.uniform(next(ks), (N_A, D), f32, -6.0, 1.0),
        'a_w1': nrm((N_A, D, DECAY_LORA), D ** -0.5),
        'a_w2': nrm((N_A, DECAY_LORA, D), 0.1),
        'a_a0': nrm((N_A, D), 0.5),
        'a_a1': nrm((N_A, D, ICLR_LORA), D ** -0.5),
        'a_a2': nrm((N_A, ICLR_LORA, D), 0.5 * ICLR_LORA ** -0.5),
        'a_k_k': 1.0 + nrm((N_A, D), 0.1),
        'a_k_a': 1.0 + nrm((N_A, D), 0.1),
        'a_r_k': nrm((N_A, RWKV_HEADS, RWKV_HEAD), 0.1),
        'a_lnx_g': gain((N_A, D)),
        'a_lnx_b': nrm((N_A, D), 0.02),
        'a_w_out': nrm((N_A, D, D), D ** -0.5),
        'kv_norm': gain((D,)),
        'kv_w': nrm((D, 2 * D), D ** -0.5),
        'b_w_in': nrm((N_B, D, 2 * D), D ** -0.5),
        'b_lambda': nrm((N_B, 4, DIFF_HEAD), 0.1),
        'b_subln': gain((N_B, 2 * DIFF_HEAD)),
        'b_w_out': nrm((N_B, D, D), D ** -0.5),
        'ple_w': nrm((DEPTH_2, PLE_DIM, D), PLE_DIM ** -0.5),
        'ple_gate': nrm((DEPTH_2, D, D), D ** -0.5),
        'ple_norm': gain((DEPTH_2, D)),
    }

def second_block(x, p, norm_pre, norm_post, a_mu, a_w_in, a_w0, a_w1, a_w2, a_a0, a_a1, a_a2,
              a_k_k, a_k_a, a_r_k, a_lnx_g, a_lnx_b, a_w_out, kv_norm, kv_w, b_w_in, b_lambda,
              b_subln, b_w_out, ple_w, ple_gate, ple_norm):
    S = x.shape[1]
    cos, sin = rope_tables(S)
    h = x
    k_sh = None
    v_sh = None
    for i in range(DEPTH_2):
        xn = rms_norm_2(h, norm_pre[i])
        if i < N_A:
            y = rwkv7_time_mix(xn, a_mu[i], a_w_in[i], a_w0[i], a_w1[i], a_w2[i], a_a0[i],
                               a_a1[i], a_a2[i], a_k_k[i], a_k_a[i], a_r_k[i], a_lnx_g[i],
                               a_lnx_b[i], a_w_out[i])
        else:
            if i == N_A:
                k_sh, v_sh = shared_kv(h, kv_norm, kv_w, cos, sin)
            j = i - N_A
            lam_init = 0.8 - 0.6 * math.exp(-0.3 * i)
            y = diff_attention_mix(xn, k_sh, v_sh, b_w_in[j], b_lambda[j], b_subln[j],
                                   b_w_out[j], lam_init, cos, sin)
        h = h + rms_norm_2(y, norm_post[i])
        e = p[i] @ ple_w[i]
        g = jax.nn.sigmoid(h @ ple_gate[i])
        h = h + rms_norm_2(g * e, ple_norm[i])
    return h


def setup_inputs(seed=0):
    out = dict(first_inputs(seed))
    for name, value in second_inputs(seed + 1).items():
        if name != "x":
            out[name + "_2"] = value
    return out


def reference(
    x, c, ada_w, ada_b, norm_mix_g, w_in, ssd_conv_w, ssd_conv_b, ssd_dt_bias, ssd_a_log, ssd_d,
    ssd_norm_g, fox_f_bias, fox_norm_g, cm_conv_w, cm_conv_b, cm_ln_g, cm_ln_b, w_out,
    norm_ffn_g, w_router_group, b_router_group, w_router_expert, b_router_expert, w_gate, w_up,
    w_down, final_norm_g, p_2, norm_pre_2, norm_post_2, a_mu_2, a_w_in_2, a_w0_2, a_w1_2,
    a_w2_2, a_a0_2, a_a1_2, a_a2_2, a_k_k_2, a_k_a_2, a_r_k_2, a_lnx_g_2, a_lnx_b_2, a_w_out_2,
    kv_norm_2, kv_w_2, b_w_in_2, b_lambda_2, b_subln_2, b_w_out_2, ple_w_2, ple_gate_2,
    ple_norm_2,
):
    x = first_block(
        x, c, ada_w, ada_b, norm_mix_g, w_in, ssd_conv_w, ssd_conv_b, ssd_dt_bias, ssd_a_log,
        ssd_d, ssd_norm_g, fox_f_bias, fox_norm_g, cm_conv_w, cm_conv_b, cm_ln_g, cm_ln_b,
        w_out, norm_ffn_g, w_router_group, b_router_group, w_router_expert, b_router_expert,
        w_gate, w_up, w_down, final_norm_g,
    )
    return second_block(
        x, p_2, norm_pre_2, norm_post_2, a_mu_2, a_w_in_2, a_w0_2, a_w1_2, a_w2_2, a_a0_2,
        a_a1_2, a_a2_2, a_k_k_2, a_k_a_2, a_r_k_2, a_lnx_g_2, a_lnx_b_2, a_w_out_2, kv_norm_2,
        kv_w_2, b_w_in_2, b_lambda_2, b_subln_2, b_w_out_2, ple_w_2, ple_gate_2, ple_norm_2,
    )


_drawn_inputs = setup_inputs


def setup_inputs(seed=0):
    import zlib

    import numpy as np

    out = dict(_drawn_inputs(seed))
    spreads = {}
    factors = {'norm_mix_g': 3.856,
     'ssd_conv_b': 4.201,
     'ssd_d': 53.848,
     'ssd_norm_g': 5.031,
     'fox_norm_g': 5.761,
     'cm_conv_b': 2.853,
     'cm_ln_g': 7.196,
     'cm_ln_b': 8.0,
     'norm_ffn_g': 2.829,
     'b_router_group': 8.0,
     'b_router_expert': 6.051,
     'norm_post_2': 3.212,
     'a_lnx_g_2': 4.037,
     'a_lnx_b_2': 3.283,
     'kv_norm_2': 4.122,
     'b_subln_2': 42.22,
     'ple_norm_2': 3.374}
    for name, (base, spread) in spreads.items():
        noise = np.random.default_rng([zlib.crc32(name.encode()), seed]).standard_normal(out[name].shape)
        drawn = base * np.exp(spread * noise) if base else spread * noise
        out[name] = jnp.asarray(drawn.astype(out[name].dtype))
    for name, factor in factors.items():
        out[name] = (out[name] * factor).astype(out[name].dtype)
    return out
```

```python
from contextlib import ExitStack

import numpy as np

import concourse.bass as bass
from concourse import mybir

F32 = mybir.dt.float32
I32 = mybir.dt.int32
U32 = mybir.dt.uint32
ALU = mybir.AluOpType
ACT = mybir.ActivationFunctionType
AX = mybir.AxisListType

P = 128
T = 256
TT = T // P
D = 1024
DC = D // P
SLOT = 8 * 512
RING = 6
EPS = 1e-6
EXPERTS, TOP = 32, 2
SLOTS = 64
SPARE = (TOP * T - 1) // (SLOTS + 1)
LIST = 40

PARAM = [("c", 8), ("ada_b", 48), ("norm_mix_g", 8), ("ssd_conv_w", 32), ("ssd_conv_b", 8),
         ("ssd_norm_g", 4), ("ssd_d", 4), ("fox_norm_g", 2), ("cm_conv_w", 62), ("cm_conv_b", 2),
         ("cm_ln_g", 2), ("cm_ln_b", 2), ("norm_ffn_g", 8), ("final_norm_g", 8),
         ("norm_pre_2", 16), ("norm_post_2", 16), ("a_mu_2", 48), ("a_w0_2", 8), ("a_a0_2", 8),
         ("a_k_k_2", 8), ("a_k_a_2", 8), ("a_r_k_2", 8), ("a_lnx_g_2", 8), ("a_lnx_b_2", 8),
         ("kv_norm_2", 8), ("b_subln_2", 1), ("ple_norm_2", 16),
         ("ssd_dt_bias", 8), ("ssd_a_log", 8), ("fox_f_bias", 4), ("b_router", 36), ("b_lambda_2", 256)]
CONST = [("ident", 128), ("tri", 128), ("tri_strict", 128), ("ones", 128), ("block_ones", 128),
         ("rwkv_even", 128), ("rwkv_odd", 128), ("causal", 128), ("rot", 128),
         ("cos", 256), ("sin", 256), ("iota", 32), ("token", 2), ("half", 1), ("sign_even", 1), ("sign_odd", 1)]


def offsets(table):
    at, out = 0, {}
    for name, n in table:
        out[name] = (at, at + n)
        at += n
    return out, at


PAT, NPARAM = offsets(PARAM)
CAT, NCONST = offsets(CONST)


class Marks:

    def __init__(self, sem, *names):
        self.sem, self.value, self.next = sem, {n: i + 1 for i, n in enumerate(names)}, 0
        assert len(self.value) == len(names)

    def mark(self, name):
        self.next += 1
        assert self.value[name] == self.next, (name, self.value[name], self.next)
        return self.sem, 1

    def at(self, name):
        return self.sem, self.value[name]


class Chain:

    def __init__(self, sem):
        self.sem, self.n = sem, 0

    def step(self, ins):
        ins.then_inc(self.sem, 1)
        self.n += 1
        return self.n

    def link(self, eng, ins):
        eng.wait_ge(self.sem, self.step(ins))


class Banks:

    def __init__(self, tensors, full, free):
        self.tensors, self.full, self.free = tensors, full, free
        self.uses, self.count, self.where = 0, [0] * len(tensors), {}

    def open(self, pe, name):
        b = self.uses % len(self.tensors)
        if self.count[b]:
            pe.wait_ge(self.free[b], self.count[b])
        self.count[b] += 1
        self.uses += 1
        assert name not in self.where, name
        self.where[name] = (b, self.uses, self.count[b])
        return self.tensors[b]

    def __getitem__(self, name):
        return self.tensors[self.where[name][0]]

    def filled(self):
        return self.full, 1

    def ready(self, name):
        return self.full, self.where[name][1]

    def release(self, name):
        return self.free[self.where[name][0]], 1

    def emptied(self, name):
        return self.free[self.where[name][0]], self.where[name][2]


def mixer_weight_tiles(w_in):
    return [[(0, 512, 512)], [(0, 1024, 512)], [(0, 2056, 260), (260, 1536, 8)], [(0, 2316, 512)],
            [(0, 0, 512)], [(0, 1544, 512)]]


def program(nc, a):
    with ExitStack() as ctx:
        def sb(name, n, dt=F32, parts=P):
            return ctx.enter_context(nc.sbuf_tensor(name, [parts, n], dt))

        def sem(name):
            return ctx.enter_context(nc.semaphore(name))

        prm, cst = sb("prm", NPARAM), sb("cst", NCONST)
        xt = sb("xt", DC * T)
        ring = sb("ring", RING * SLOT)
        work_size = 21600
        work = sb("work", work_size)
        small = sb("small", 480)
        psum = [ctx.enter_context(nc.psum_tensor(f"bank{i}", [P, 512], F32)) for i in range(8)]

        def par(name, lo=0, n=None):
            s, e = PAT[name]
            return prm[:, s + lo:(s + lo + n if n is not None else e)]

        def con(name):
            s, e = CAT[name]
            return cst[:, s:e]

        ident, ones = con("ident"), con("ones")
        xv = xt[:].rearrange("p (c t) -> p c t", c=DC)

        def carve(sizes, tensor=work, at=0):
            out = {}
            for name, n in sizes:
                out[name] = tensor[:, at:at + n]
                at += n
            assert at <= tensor.shape[1], at
            return out

        def chunks(ap, c):
            return ap.rearrange("p (c t) -> p c t", c=c)

        params_loaded = sem("params_loaded")
        x_loaded = sem("x_loaded")
        slot_loaded = [sem(f"slot_loaded{s}") for s in range(RING)]
        weights_used = sem("weights_used")
        bank_full = sem("bank_full")
        bank_free = [sem(f"bank_free{b}") for b in range(7)]
        banks = Banks(psum[:7], bank_full, bank_free)
        mod_bank = psum[7]
        act_steps, dve_steps = Chain(sem("act_steps")), Chain(sem("dve_steps"))
        rms_squares, rms_root, rms_ready = sem("rms_squares"), sem("rms_root"), sem("rms_ready")
        rms_variance = sem("rms_variance")
        pe = nc.tensor
        act = nc.scalar
        dve = nc.vector

        def cols(w, c0, n, rows=D):
            return w.rearrange("(c p) n -> p c n", p=P)[:, :, c0:c0 + n]

        tiles = []

        def tile(name, *parts):
            tiles.append((name, parts))

        def ada(j):
            tile(f"ada{j}", (0, 512, cols(a["ada_w"][0], 512 * j, 512)))

        for j in range(4):
            ada(j)
        for j, pieces in enumerate(mixer_weight_tiles(None)):
            tile(f"win{j}", *[(o, 512 if len(pieces) == 1 else 268, cols(a["w_in"][0], c0, n)) for o, c0, n in pieces])
            ada(4 + j)
        ada(10)
        ada(11)
        for j in range(2):
            tile(f"wout{j}", (0, 512, cols(a["w_out"][0], 512 * j, 512)))
        tile("router", (0, 36, cols(a["w_router_group"][0], 0, 4)), (4, 36, cols(a["w_router_expert"][0], 0, 32)))
        MOE_TILE = len(tiles)
        assert MOE_TILE % 3 == 0
        slot_of, loaded_at = {}, {}
        total = [0] * RING
        for n, (name, parts) in enumerate(tiles):
            slot_of[name] = n % RING
            total[n % RING] += 16 * len(parts)
            loaded_at[name] = (slot_loaded[n % RING], total[n % RING])

        weights_used_after = {name: n + 1 for n, (name, _) in enumerate(tiles)}

        def slot(s, pitch=512, at=0, c=DC):
            return ring[:, s * SLOT + at:s * SLOT + at + pitch * c].rearrange("p (c n) -> p c n", c=c)

        m = carve([("h", 2048), ("xbc", 2072), ("conv", 2048), ("sq", 2048), ("e", 536), ("u", 572),
                   ("sg", 512), ("zs", 1024), ("qk", 1024), ("xdt", 1024), ("xde", 512), ("brow", 256),
                   ("cexp", 1024), ("cb", 512), ("st", 512), ("p", 1536), ("y", 2048),
                   ("lnx", 512)])
        m["decay"] = m["sq"]
        h, conv, sq = chunks(m["h"], 8), chunks(m["conv"], 8), chunks(m["sq"], 8)
        xbc = m["xbc"].rearrange("p (c t) -> p c t", c=8)
        ebuf = chunks(m["e"], 2)
        u = m["u"].rearrange("p (c t) -> p c t", c=2)
        zq = work[:, 2048 + 2072 + 2048 + 2048 + 536 + 572 + 512:][:, 0:2048].rearrange("p (c t) -> p c t", c=8)
        zs, qk, y = chunks(m["zs"], 4), chunks(m["qk"], 4), chunks(m["y"], 8)
        xdt = chunks(m["xdt"], 2)
        cb = m["cb"].rearrange("p (t g l) -> p t g l", t=2, g=2)
        decay = m["decay"].rearrange("p (t h l) -> p t h l", t=2, h=8)
        cexp = m["cexp"].rearrange("p (h l) -> p h l", h=8)
        prob = m["p"].rearrange("p (h k) -> p h k", h=4)
        ptr = m["xbc"][:, 0:1536].rearrange("p (h k) -> p h k", h=4)
        s = carve([("cond", 8), ("mod", 48), ("gmix", 8), ("spx", 24), ("spa", 24), ("spu", 24), ("spw", 24),
                   ("spl", 24), ("spd", 24), ("spr", 24), ("sp", 24), ("ea", 8), ("cumin", 24), ("nacs", 16), ("nq", 8),
                   ("dte", 8), ("mx", 16), ("sums", 8), ("rs", 8), ("spm", 24), ("gffn", 8), ("tdiff", 8), ("nmx", 8),
                   ], small)
        rst = sb("rst", 512)
        var = sb("var", 512)
        root = sb("root", 512)

        def pe_rms(k, chunks_of, n=T, weights=ones):
            pe.wait_ge(rms_squares, k + 1)
            bank = banks.open(pe, f"rms{k}")
            for g, group in enumerate(chunks_of):
                for i, ap in enumerate(group):
                    last = pe.matmul(bank[:, g * n:(g + 1) * n], weights, ap, start=(i == 0), stop=(i == len(group) - 1))
            last.then_inc(*banks.filled())

        def dve_rms(k, count, width, eps=EPS):
            dve.wait_ge(*banks.ready(f"rms{k}"))
            dve.tensor_scalar(var[:, 0:width], banks[f"rms{k}"][:, 0:width], 1.0 / count, eps, ALU.mult, ALU.add)\
               .then_inc(*banks.release(f"rms{k}"))
            dve.wait_ge(rms_root, k + 1)
            dve.reciprocal(rst[:, 0:width], root[:, 0:width]).then_inc(rms_ready, 1)
            dve.wait_ge(rms_ready, k + 1)

        def act_rms(k, width):
            act.wait_ge(*banks.emptied(f"rms{k}"))
            if k:
                act.wait_ge(rms_ready, k)
            act.activation(root[:, 0:width], var[:, 0:width], ACT.Sqrt).then_inc(rms_root, 1)

        V = Marks(sem("dve_mixer"), "zeros", "h", "xconv", "spa", "cumin", "u_gated", "tdiff", "args",
                  "xde", "decay", "cexp", "scores", "probs", "y_gated", "conv", "ln_centred", "ln_norm",
                  "y_ssd", "y_fox", "x1", "h2")
        A = Marks(sem("act_mixer"), "cond", "ea", "spu", "silu_conv", "dte", "cexp", "decay",
                  "exp", "silu_ln")


        mo = carve([("xg0", 512), ("xg1", 512), ("xet0", 512), ("xet1", 512), ("sg0", 256), ("sg1", 256),
                    ("hid0", 256), ("hid1", 256), ("ht0", 256), ("ht1", 256), ("ys0", 512), ("ys1", 512),
                    ("yg", 4096), ("comb", 2048),
                    ("rl", 72), ("gm", 2), ("gd", 8), ("ge", 8), ("gs", 2), ("pg", 2), ("gt", 8), ("gi", 2), ("ohg", 8),
                    ("ep", 64), ("el", 16), ("m1", 2), ("ed", 16), ("et", 16), ("ei", 2), ("oh8", 32), ("el2", 16),
                    ("m2", 2), ("md", 2), ("e2", 2), ("w", 4), ("oh", 128), ("hit", 64), ("x", 32), ("incl", 32),
                    ("excl", 32), ("prod", 128), ("pos", 4), ("e", 4), ("ov", 4), ("q", 4), ("slot", 4), ("g0", 4),
                    ("blk", 4), ("lst", 4), ("row", 4), ("cmp", 224), ("info", 8), ("listf", 40)], at=6168)
        list_at, row_at, token_id = sb("list_at", 4, U32), sb("row_at", 4, U32), sb("token_id", 2, I32)
        zero_list, list_in, gather_at = sb("zero_list", LIST, I32), sb("list_in", LIST, I32), sb("gather_at", LIST, U32)
        info = sb("info", 8, I32)
        xg, xet, sg_, hid, ht, ys = ([mo[f"{n}{p_}"] for p_ in range(2)] for n in ("xg", "xet", "sg", "hid", "ht", "ys"))
        R = Marks(sem("dve_routing"), "ids", "gd", "md", "hits", "lists", "info", "gather_at", "weights", "comb0", "comb1", "x2", "final")
        S = Marks(sem("act_routing"), "ge", "e2")
        list_cleared, list_scattered, list_loaded = sem("list_cleared"), sem("list_scattered"), sem("list_loaded")
        h_stored = sem("h_stored")
        yg_zero, yrow_cleared = sem("yg_zero"), sem("yrow_cleared")
        gathered = [sem("gathered0"), sem("gathered1")]
        xt_done, xt_copied, gu_done, silu_done, hid_done = (sem(n) for n in ("xt_done", "xt_copied", "gu_done", "silu_done", "hid_done"))
        ht_done, ht_copied, y_done, y_copied = (sem(n) for n in ("ht_done", "ht_copied", "y_done", "y_copied"))
        y_stored = [sem("y_stored0"), sem("y_stored1")]
        spare_loaded, spare_used, spare_gathered, spare_stored = (sem(n) for n in ("spare_loaded", "spare_used", "spare_gathered", "spare_stored"))
        rows_gathered = [sem(f"rows_gathered{t}") for t in range(TT)]
        expert_slots = [[(MOE_TILE + 3 * p_ + k) % RING for k in range(3)] for p_ in range(2)]

        def expert_loop(eng, body):
            body(0, 0)
            body(1, 1)
            with eng.Fori(1, EXPERTS // 2) as i:
                body(2 * i, 0)
                body(2 * i + 1, 1)

        def spare_loop(eng, body):
            spare = eng.value_load(info[0:1, 0:1], min_val=0, max_val=SPARE)
            with eng.If(spare > 0):
                with eng.Fori(0, SPARE) as j:
                    body(j)


        moe_base = list(total)
        post, POST_TILE = [], MOE_TILE + 3 * EXPERTS

        def post_tile(name, *parts):
            n = len(post)
            post.append((name, parts))
            slot_of[name] = n % 3
            total[n % 3] += 16 * len(parts) + (16 * (EXPERTS // 2) if n < 3 else 0)
            loaded_at[name] = (slot_loaded[n % 3], total[n % 3])

        def square(name, w, n):
            for j in range(n):
                post_tile(f"{name}{j}", (0, SLOT, P, DC, cols(w, 512 * j, 512)))

        def ple_tiles(l):
            post_tile(f"ple_w{l}", (0, 2 * D, P, 2, a["ple_w_2"][l].rearrange("(c p) n -> p c n", p=P)))
            square(f"ple_gate{l}_", a["ple_gate_2"][l], 2)

        post_tile("lora", (0, 512, P, DC, cols(a["a_w1_2"][0], 0, 64)), (512, 512, P, DC, cols(a["a_a1_2"][0], 0, 64)),
                  (1024, D, 64, 1, a["a_w2_2"][0].unsqueeze(1)), (2048, D, 64, 1, a["a_a2_2"][0].unsqueeze(1)))
        for i, name in enumerate("rkvg"):
            square(f"rwkv_{name}", a["a_w_in_2"][0, i], 2)
        square("rwkv_out", a["a_w_out_2"][0], 2)
        ple_tiles(0)
        square("kv", a["kv_w_2"], 4)
        square("b_in", a["b_w_in_2"][0], 4)
        square("b_out", a["b_w_out_2"][0], 2)
        ple_tiles(1)

        C, NC = 64, T // 64
        HP = 8
        w_ = carve([("xn", 2056), ("dx", 2048), ("mix", 4096), ("r", 2048), ("k", 2048), ("g", 2048), ("vu", 4096),
                    ("lw", 2048), ("hid", 1112)])
        ar = carve([("a", 2048), ("cum", 2048), ("e1", 2048), ("kk", 2048), ("e2", 2048), ("e3", 2048)], ring, 3 * SLOT)
        sc_ = ring[:, 3 * SLOT:3 * SLOT + 8192].rearrange("p (h c n) -> p h c n", h=16, c=NC)
        kbrow = ring[:, 3 * SLOT + 8192:6 * SLOT].rearrange("p (h c n) -> p h c n", h=HP, c=NC)
        kb = work[:, 0:4096].rearrange("p (h c k s) -> p h c k s", h=HP, c=NC, k=2)
        kr = w_["mix"].rearrange("p (h c k s) -> p h c k s", h=HP, c=NC, k=2)
        xm, xmt = (work[:, o:o + 2048].rearrange("p (h n) -> p h n", h=16) for o in (0, 2048))
        inv = w_["r"].rearrange("p (h n) -> p h n", h=16)
        wsb = work[:, 0:D]
        vu = w_["vu"].rearrange("p (c n) -> p c n", c=NC)
        state = w_["hid"][:, 0:D].rearrange("p (h n) -> p h n", h=HP)
        tmp = [ring[:, 3 * SLOT + 2048 * i:3 * SLOT + 2048 * (i + 1)] for i in range(6)]
        pc = sb("pc", 32)
        one_ka = sb("one_ka", 8)
        gn_eps = sb("gn_eps", 1)
        W = Marks(sem("dve_rwkv"), "vu_zero", "xn", *[f"mix{i}" for i in range(5)], "kk_sq", "bonus_in", "mix5", "args", "kb", "xmt0", "xmt1", "placed",
                  *[f"st{c}" for c in range(NC)], "centred", "y", "attn_in")
        X = Marks(sem("act_rwkv"), "tanh", "lora_a", "sigw", "siga", "r", "k", "kk_norm", "g", "exp", "centred_sq")

        z = carve([("pt", 1024), ("eb", 2048), ("gb", 2048), ("hkv", 2048), ("hq", 2048), ("kt", 2048), ("qt", 2048), ("gate", 2048),
                   ("v", 2048), ("ot", 2048), ("mask3", 384), ("mx", 32), ("nmx", 32), ("sums", 32), ("rs", 32), ("lp", 128), ("ls", 2),
                   ("le", 2), ("nlam", 1), ("sub", 1), ("eps", 1)])
        sq4 = tmp[0]
        dprob = ring[:, 3 * SLOT + 2048:3 * SLOT + 8192].rearrange("p (h c k) -> p h c k", h=8, c=2)
        dat = ring[:, 3 * SLOT + 8192:3 * SLOT + 8192 + 3072].rearrange("p (h k) -> p h k", h=8)
        lam_init = 0.8 - 0.6 * float(np.exp(-0.3))
        Y = Marks(sem("dve_diff"), "lam_sum", "ge0", "x3", "hkv", "hq", "kt", "qt", *[n for h_ in range(8) for n in ([f"ds{h_}"] + ([f"da{h_ - 1}"] if h_ else []))], "da7", "o", "x4", "ge1", "x5")
        Z = Marks(sem("act_diff"), "lam_exp", "k", "q", "gate", *[f"dx{h_}" for h_ in range(8)], "o_sq", "o_norm")
        out_written = sem("out_written")
        pt_loaded = sem("pt_loaded")

        block = ctx.enter_context(nc.Block())

        @block.tensor
        def _(pe):
            tri = con("tri")

            def use_tile(name):
                pe.wait_ge(*loaded_at[name])
                return slot_of[name]

            def ada_tile(j, bank, first):
                w = slot(use_tile(f"ada{j}"))
                for f in range(4):
                    col = 4 * (j - first) + f
                    for c in range(DC):
                        last = pe.matmul(bank[:, col:col + 1], w[:, c, f * P:(f + 1) * P], s["cond"][:, c:c + 1],
                                         start=(c == 0), stop=(c == DC - 1))
                last.then_inc(weights_used, 1)

            def project(w, rhs, names, fs=(0, 1, 2, 3), nc_=DC):
                for i in range(0, len(fs), 2):
                    bank = banks.open(pe, names[i // 2])
                    for j in range(2):
                        for c in range(nc_):
                            last = pe.matmul(bank[:, j * T:(j + 1) * T], w[:, c, fs[i + j] * P:(fs[i + j] + 1) * P],
                                             rhs[:, c, :], start=(c == 0), stop=(c == nc_ - 1))
                    last.then_inc(*banks.filled())
                return last

            def release_tile():
                pe.drain().then_inc(weights_used, 1)

            pe.wait_ge(params_loaded, 32)
            pe_rms(0, [[sq[:, c, :] for c in range(DC)]])
            pe.wait_ge(*A.at("cond"))
            bank = banks.open(pe, "mod")
            for j in range(4):
                ada_tile(j, bank, 0)
            pe.drain().then_inc(*banks.filled())
            pe.wait_ge(*V.at("h"))
            project(slot(use_tile("win0")), h, ("xbc0", "xbc1"))
            release_tile()
            ada_tile(4, mod_bank, 4)
            project(slot(use_tile("win1")), h, ("xbc2", "xbc3"))
            release_tile()
            ada_tile(5, mod_bank, 4)
            w = slot(use_tile("win2"), pitch=268)
            for t in range(TT):
                bank = banks.open(pe, f"e{t}")
                for c in range(DC):
                    last = pe.matmul(bank[:, 0:268], h[:, c, t * P:(t + 1) * P], w[:, c, :], start=(c == 0), stop=(c == DC - 1))
                last.then_inc(*banks.filled())
            release_tile()
            ada_tile(6, mod_bank, 4)
            project(slot(use_tile("win3")), h, ("glu_a", "glu_b"))
            release_tile()
            ada_tile(7, mod_bank, 4)
            pe.wait_ge(*V.at("cumin"))
            cumin = chunks(s["cumin"], 2)
            bank = banks.open(pe, "acs_rows")
            for t in range(TT):
                pe.matmul(bank[:, 8 * t:8 * t + 8], tri, cumin[:, t, 0:8], start=True, stop=True)
            pe.matmul(bank[:, 16:20], tri, cumin[:, 0, 8:12], start=True, stop=True)
            pe.matmul(bank[:, 20:24], ones, cumin[:, 0, 8:12], start=True, stop=False)
            pe.matmul(bank[:, 20:24], tri, cumin[:, 1, 8:12], start=False, stop=True).then_inc(*banks.filled())
            for t in range(TT):
                for half in range(2):
                    bank = banks.open(pe, f"acs{t}{half}")
                    for j in range(4):
                        col = cumin[:, t, 4 * half + j:4 * half + j + 1]
                        last = pe.matmul(bank[:, j * P:(j + 1) * P], col.to_broadcast([P, P]), tri, start=True, stop=True)
                    last.then_inc(*banks.filled())
            for half in range(2):
                bank = banks.open(pe, f"ncum{half}")
                for j in range(2):
                    c0, c1 = (cumin[:, t, 8 + 2 * half + j:9 + 2 * half + j].to_broadcast([P, P]) for t in range(2))
                    pe.matmul(bank[:, j * T:j * T + P], c0, tri, start=True, stop=True)
                    pe.matmul(bank[:, j * T + P:(j + 1) * T], c0, ones, start=True, stop=False)
                    last = pe.matmul(bank[:, j * T + P:(j + 1) * T], c1, tri, start=False, stop=True)
                last.then_inc(*banks.filled())
            project(slot(use_tile("win4")), h, ("z0", "z1"))
            release_tile()
            ada_tile(8, mod_bank, 4)
            pe.wait_ge(*A.at("silu_conv"))
            for t in range(TT):
                bank = banks.open(pe, f"xrow{t}")
                for c in range(4):
                    last = pe.transpose(bank[:, c * P:(c + 1) * P], conv[:, c, t * P:(t + 1) * P], ident)
                last.then_inc(*banks.filled())
            bank = banks.open(pe, "brow")
            for g in range(2):
                last = pe.transpose(bank[:, g * P:(g + 1) * P], conv[:, 4 + g, 0:P], ident)
            last.then_inc(*banks.filled())
            bank = banks.open(pe, "cb")
            for t in range(TT):
                for g in range(2):
                    at = (2 * t + g) * P
                    last = pe.matmul(bank[:, at:at + P], conv[:, 4 + g, t * P:(t + 1) * P], conv[:, 6 + g, t * P:(t + 1) * P],
                                     start=True, stop=True)
            last.then_inc(*banks.filled())
            project(slot(use_tile("win5")), h, ("q", "k"))
            release_tile()
            ada_tile(9, mod_bank, 4)
            pe.wait_ge(*banks.emptied("brow"))
            pe.wait_ge(*V.at("xde"))
            bank = banks.open(pe, "st")
            for g in range(2):
                last = pe.matmul(bank[:, g * T:(g + 1) * T], m["brow"][:, g * P:(g + 1) * P], m["xde"][:, g * T:(g + 1) * T],
                                 start=True, stop=True)
            last.then_inc(*banks.filled())
            pe.wait_ge(*banks.emptied("q"))
            pe.wait_ge(*banks.emptied("k"))
            for hd in range(4):
                r = slice(64 * (hd % 2), 64 * (hd % 2) + 64)
                bank = banks.open(pe, f"s{hd}")
                pe.matmul(bank[:, 0:P], qk[r, hd // 2, 0:P], qk[r, 2 + hd // 2, 0:P], start=True, stop=True)
                pe.matmul(bank[:, P:3 * P], qk[r, hd // 2, P:T], qk[r, 2 + hd // 2, :], start=True, stop=True)\
                  .then_inc(*banks.filled())
            pe.wait_ge(*V.at("decay"))
            pe.wait_ge(*V.at("cexp"))
            pe.wait_ge(*banks.emptied("st"))
            for half in range(2):
                bank = banks.open(pe, f"y{half}")
                for pair in range(2):
                    for hd in range(2):
                        hh = 4 * half + 2 * pair + hd
                        for t in range(TT):
                            out = bank[64 * hd:64 * hd + 64, pair * T + t * P:pair * T + (t + 1) * P]
                            last = pe.matmul(out, xdt[:, t, hh * 64:hh * 64 + 64], decay[:, t, hh, :], start=True, stop=(t == 0))
                            if t:
                                last = pe.matmul(out, m["st"][:, hh * 64:hh * 64 + 64], cexp[:, hh, :], start=False, stop=True)
                last.then_inc(*banks.filled())
            pe.wait_ge(*V.at("probs"))
            for hd in range(4):
                bank = banks.open(pe, f"pt{hd}")
                for j in range(3):
                    last = pe.transpose(bank[:, j * P:(j + 1) * P], prob[:, hd, j * P:(j + 1) * P], ident)
                last.then_inc(*banks.filled())
            bank = banks.open(pe, "o")
            for hd in range(4):
                pe.wait_ge(*banks.emptied(f"pt{hd}"))
                r = slice(64 * (hd % 2), 64 * (hd % 2) + 64)
                at = (hd // 2) * T
                v0, v1 = (ebuf[:, t, hd * 64:hd * 64 + 64] for t in range(2))
                pe.matmul(bank[r, at:at + P], v0, ptr[:, hd, 0:P], start=True, stop=True)
                pe.matmul(bank[r, at + P:at + T], v0, ptr[:, hd, P:2 * P], start=True, stop=False)
                last = pe.matmul(bank[r, at + P:at + T], v1, ptr[:, hd, 2 * P:3 * P], start=False, stop=True)
            last.then_inc(*banks.filled())
            pe.wait_ge(*V.at("conv"))
            bank = banks.open(pe, "ln_mean")
            for c in range(2):
                last = pe.matmul(bank[:, 0:T], ones, chunks(m["sg"], 2)[:, c, :], start=(c == 0), stop=(c == 1))
            last.then_inc(*banks.filled())
            pe_rms(1, [[sq[:, c, :] for c in (0, 1)]])
            pe_rms(2, [[sq[:, c, :] for c in (2, 3)], [sq[:, c, :] for c in (4, 5)]])
            pe_rms(3, [[sq[:, c, :] for c in (6, 7)]])
            ada_tile(10, mod_bank, 4)
            ada_tile(11, mod_bank, 4)
            pe.wait_ge(*V.at("y_ssd"))
            pe.wait_ge(*V.at("y_fox"))
            pe.wait_ge(*A.at("silu_ln"))
            for j in range(2):
                project(slot(use_tile(f"wout{j}")), y, (f"wo{2 * j}", f"wo{2 * j + 1}"))
                release_tile()
            pe_rms(4, [[sq[:, c, :] for c in range(DC)]])
            pe.wait_ge(*V.at("h2"))
            w = slot(use_tile("router"), pitch=36)
            bank = banks.open(pe, "router")
            for t in range(TT):
                for c in range(DC):
                    last = pe.matmul(bank[:, 36 * t:36 * t + 36], h[:, c, t * P:(t + 1) * P], w[:, c, :], start=(c == 0), stop=(c == DC - 1))
            last.then_inc(*banks.filled())
            release_tile()

            for t in range(TT):
                for half in range(2):
                    bank = banks.open(pe, f"hrow{t}{half}")
                    for c in range(4):
                        last = pe.transpose(bank[:, c * P:(c + 1) * P], h[:, 4 * half + c, t * P:(t + 1) * P], ident)
                    last.then_inc(*banks.filled())
            pe.wait_ge(*R.at("hits"))
            hit = chunks(mo["hit"], 2)
            bank = banks.open(pe, "pos")
            pe.matmul(bank[:, 0:32], con("tri_strict"), hit[:, 0, :], start=True, stop=True)
            pe.matmul(bank[:, 32:64], ones, hit[:, 0, :], start=True, stop=False)
            pe.matmul(bank[:, 32:64], con("tri_strict"), hit[:, 1, :], start=False, stop=True)
            pe.matmul(bank[:, 64:96], ones, hit[:, 0, :], start=True, stop=False)
            pe.matmul(bank[:, 64:96], ones, hit[:, 1, :], start=False, stop=True).then_inc(*banks.filled())

            def expert(e, p_, slots, gathered_at, loaded, used):
                gate_up = ring[:, slots[0] * SLOT:(slots[0] + 2) * SLOT].rearrange("p (k c n) -> p c k n", k=2, c=DC)
                down = ring[:, slots[2] * SLOT:(slots[2] + 1) * SLOT].rearrange("p (c n) -> p c n", c=4)
                pe.wait_ge(*gathered_at)
                for j in range(4):
                    last = pe.transpose(psum[p_][:, j * P:(j + 1) * P], xg[p_][:, j * P:(j + 1) * P], ident)
                last.then_inc(xt_done, 1)
                pe.wait_ge(xt_copied, e + 1)
                pe.wait_ge(*loaded[0])
                pe.wait_ge(*loaded[1])
                for c in range(DC):
                    x_c = xet[p_][:, (c % 4) * P + (c // 4) * 64:(c % 4) * P + (c // 4) * 64 + 64]
                    for half in range(2):
                        last = pe.matmul(psum[2 + p_][64 * half:64 * half + 64, :], x_c,
                                         gate_up[:, c, :, half * T:(half + 1) * T], start=(c == 0), stop=(c == DC - 1))
                last.then_inc(gu_done, 1)
                pe.wait_ge(gu_done, e + 1)
                pe.nop().then_inc(used, 2)
                pe.wait_ge(hid_done, e + 1)
                for c in range(2):
                    last = pe.transpose(psum[4][:, c * P:(c + 1) * P], hid[p_][:, c * P:(c + 1) * P], ident)
                last.then_inc(ht_done, 1)
                pe.wait_ge(ht_copied, e + 1)
                pe.wait_ge(*loaded[2])
                for c in range(4):
                    h_c = ht[p_][:, (c % 2) * P + (c // 2) * 64:(c % 2) * P + (c // 2) * 64 + 64]
                    for half in range(2):
                        last = pe.matmul(psum[5 + p_][64 * half:64 * half + 64, :], h_c,
                                         down[:, c, half * 512:(half + 1) * 512], start=(c == 0), stop=(c == 3))
                last.then_inc(y_done, 1)
                pe.wait_ge(y_done, e + 1)
                pe.nop().then_inc(used, 1)

            for b in range(7):
                if banks.count[b]:
                    pe.wait_ge(bank_free[b], banks.count[b])

            def main(e, p_):
                seen = e // 2 if isinstance(e, int) else (e - p_) // 2
                loaded = [(slot_loaded[k], moe_base[k] + 16 + 16 * seen) for k in expert_slots[p_]]
                expert(e, p_, expert_slots[p_], (gathered[p_], 16 + 16 * seen), loaded, weights_used)

            expert_loop(pe, main)
            pe.wait_ge(*R.at("info"))

            def spare(j):
                expert(EXPERTS + j, 0, (3, 4, 5), (spare_gathered, 16 + 16 * j), [(spare_loaded, 48 + 48 * j)] * 3, spare_used)

            spare_loop(pe, spare)
            for t in range(TT):
                pe.wait_ge(*R.at(f"comb{t}"))
                for half in range(2):
                    bank = banks.open(pe, f"moe{t}{half}")
                    for c in range(4):
                        at = t * D + (4 * half + c) * P
                        last = pe.transpose(bank[:, c * P:(c + 1) * P], mo["comb"][:, at:at + P], ident)
                    last.then_inc(*banks.filled())
            pe_rms(5, [[sq[:, c, :] for c in range(DC)]])
            xn = w_["xn"].rearrange("p (c t) -> p c t", c=DC)
            mix = [chunks(w_["mix"][:, 2048 * i:2048 * (i + 1)], 8) for i in range(2)]
            lora = ring[:, slot_of["lora"] * SLOT:(slot_of["lora"] + 1) * SLOT]
            pe_rms(6, [[sq[:, c, :] for c in range(DC)]])
            pe.wait_ge(*loaded_at["lora"])
            for i in range(2):
                pe.wait_ge(*W.at(f"mix{i}"))
                bank = banks.open(pe, f"lora{i}")
                for c in range(DC):
                    last = pe.matmul(bank[0:64, 0:T], lora[:, 512 * i + 64 * c:512 * i + 64 * c + 64], mix[i][:, c, :],
                                     start=(c == 0), stop=(c == DC - 1))
                last.then_inc(*banks.filled())
            for i in range(2):
                pe.wait_ge(*X.at(("tanh", "lora_a")[i]))
                for f in range(0, DC, 2):
                    bank = banks.open(pe, f"pre{i}{f}")
                    for j in range(2):
                        last = pe.matmul(bank[:, j * T:(j + 1) * T], lora[0:64, 1024 * (1 + i) + (f + j) * P:1024 * (1 + i) + (f + j + 1) * P],
                                         w_["hid"][0:64, i * T:(i + 1) * T], start=True, stop=True)
                    last.then_inc(*banks.filled())
            release_tile()

            def project_all(name, rhs, out, n=2):
                for j in range(n):
                    project(slot(use_tile(f"{name}{j}")), rhs, (f"{out}{2 * j}", f"{out}{2 * j + 1}"))
                    release_tile()

            pe.wait_ge(*W.at("mix2"))
            project_all("rwkv_r", mix[0], "r")
            pe.wait_ge(*W.at("mix3"))
            project_all("rwkv_k", mix[1], "k_")

            def project_rows(name, src, out, n=2):
                for j in range(n):
                    w = slot(use_tile(name(j)))
                    for t in range(TT):
                        bank = banks.open(pe, f"{out}{j}{t}")
                        for c in range(DC):
                            last = pe.matmul(bank[:, :], src[:, c, t * P:(t + 1) * P], w[:, c, :], start=(c == 0), stop=(c == DC - 1))
                        last.then_inc(*banks.filled())
                    release_tile()

            pe.wait_ge(*W.at("mix4"))
            project_rows(lambda j: f"rwkv_v{j}", mix[0], "v")
            for name, mark in (("kn", "kk_sq"), ("bonus", "bonus_in")):
                pe.wait_ge(*W.at(mark))
                src = ar["e1"] if name == "kn" else ar["e3"]
                for i in range(4):
                    bank = banks.open(pe, f"{name}{i}")
                    for j in range(2):
                        c = 2 * i + j
                        last = pe.matmul(bank[:, j * T:(j + 1) * T], con("block_ones"), src[:, c * T:(c + 1) * T], start=True, stop=True)
                    last.then_inc(*banks.filled())
            pe.wait_ge(*W.at("mix5"))
            project_all("rwkv_g", mix[1], "g")
            pe.wait_ge(*W.at("kb"))
            for c in range(NC):
                for half in range(2):
                    bank = banks.open(pe, f"kbt{c}{half}")
                    for j in range(4):
                        last = pe.transpose(bank[:, j * P:(j + 1) * P], kb[:, 4 * half + j, c, :, :].rearrange("p k s -> p (k s)"), ident)
                    last.then_inc(*banks.filled())
            for half in range(2):
                for c in range(NC):
                    for hd in range(2):
                        bank = banks.open(pe, f"sc{half}{c}{hd}")
                        r = slice(64 * hd, 64 * hd + 64)
                        for j in range(4):
                            last = pe.matmul(bank[:, j * P:(j + 1) * P], kb[r, 4 * half + j, c, :, :].rearrange("p k s -> p (k s)"),
                                             kr[r, 4 * half + j, c, :, :].rearrange("p k s -> p (k s)"), start=True, stop=True)
                        last.then_inc(*banks.filled())
            for q in range(2):
                pe.wait_ge(*W.at(f"xmt{q}"))
                for h4 in range(4):
                    bank = banks.open(pe, f"x{q}_0_{h4}")
                    for j in range(4):
                        last = pe.transpose(bank[:, j * P:(j + 1) * P], xmt[:, 4 * h4 + j, :], ident)
                    last.then_inc(*banks.filled())
                for level in range(1, 6):
                    for h4 in range(4):
                        pe.wait_ge(*banks.emptied(f"x{q}_{level - 1}_{h4}"))
                        if level > 1:
                            pe.wait_ge(*banks.emptied(f"xt{q}_{level - 1}_{h4}"))
                        bank = banks.open(pe, f"x{q}_{level}_{h4}")
                        for j in range(4):
                            hh = 4 * h4 + j
                            last = pe.matmul(bank[:, j * P:(j + 1) * P], xmt[:, hh, :], xm[:, hh, :], start=True, stop=True)
                        if level < 5:
                            last.then_inc(*banks.filled())
                            bank = banks.open(pe, f"xt{q}_{level}_{h4}")
                            for j in range(4):
                                hh = 4 * h4 + j
                                last = pe.matmul(bank[:, j * P:(j + 1) * P], xm[:, hh, :], xmt[:, hh, :], start=True, stop=True)
                        last.then_inc(*banks.filled())
                    for h4 in range(4):
                        pe.wait_ge(*banks.emptied(f"x{q}_{level}_{h4}"))
                        if level > 1:
                            pe.wait_ge(*banks.emptied(f"inv{q}_{level - 1}_{h4}"))
                        bank = banks.open(pe, f"inv{q}_{level}_{h4}")
                        for j in range(4):
                            hh = 4 * h4 + j
                            last = pe.matmul(bank[:, j * P:(j + 1) * P], xm[:, hh, :], inv[:, hh, :], start=True, stop=True)
                        last.then_inc(*banks.filled())
            pe.wait_ge(*W.at("placed"))
            for c in range(NC):
                rows = slice(64, 128) if c % 2 == 0 else slice(0, 64)
                if c:
                    pe.wait_ge(*W.at(f"st{c - 1}"))
                for half in range(2):
                    bank = banks.open(pe, f"w{c}{half}")
                    for j in range(4):
                        hp = 4 * half + j
                        for hd in range(2):
                            hh = 2 * hp + hd
                            out = bank[rows, j * P + 64 * hd:j * P + 64 * hd + 64]
                            if c:
                                pe.matmul(out, kr[:, hp, c, 0, :], state[:, hp, 64 * hd:64 * hd + 64], start=True, stop=False)
                            last = pe.matmul(out, sc_[:, hh, c, 0:64], vu[:, c, hh * 64:hh * 64 + 64], start=(c == 0), stop=True)
                    last.then_inc(*banks.filled())
                for half in range(2):
                    pe.wait_ge(*banks.emptied(f"w{c}{half}"))
                    bank = banks.open(pe, f"u{c}{half}")
                    for j in range(8):
                        hh = 8 * half + j
                        last = pe.matmul(bank[rows, j * 64:(j + 1) * 64], sc_[rows, hh, c, 0:64], wsb[rows, hh * 64:(hh + 1) * 64],
                                         start=True, stop=True)
                    last.then_inc(*banks.filled())
                for half in range(2):
                    pe.wait_ge(*banks.emptied(f"u{c}{half}"))
                    if c < NC - 1:
                        bank = banks.open(pe, f"ds{c}{half}")
                        for j in range(4):
                            hp = 4 * half + j
                            last = pe.matmul(bank[:, j * P:(j + 1) * P], kbrow[:, hp, c, :], vu[:, c, hp * P:(hp + 1) * P], start=True, stop=True)
                        last.then_inc(*banks.filled())
                bank = banks.open(pe, f"yr{c}")
                for hp in range(HP):
                    for hd in range(2):
                        hh = 2 * hp + hd
                        out = bank[64 * hd:64 * hd + 64, hp * 64:(hp + 1) * 64]
                        if c:
                            pe.matmul(out, state[:, hp, 64 * hd:64 * hd + 64], kr[:, hp, c, 1, :], start=True, stop=False)
                        last = pe.matmul(out, vu[:, c, hh * 64:(hh + 1) * 64], sc_[:, hh, c, 64:128], start=(c == 0), stop=True)
                last.then_inc(*banks.filled())
            for c in range(NC):
                rows = slice(0, 64) if c % 2 == 0 else slice(64, 128)
                bank = banks.open(pe, f"vt{c}")
                for hp in range(HP):
                    last = pe.transpose(bank[:, hp * 64:(hp + 1) * 64], vu[rows, c, hp * P:(hp + 1) * P], ident[rows, rows])
                last.then_inc(*banks.filled())
            for name in ("gmean", "gvar"):
                if name == "gvar":
                    pe.wait_ge(*X.at("centred_sq"))
                else:
                    for c in range(NC):
                        pe.wait_ge(*banks.emptied(f"yr{c}"))
                src = tmp[1] if name == "gvar" else w_["lw"]
                for i in range(4):
                    bank = banks.open(pe, f"{name}{i}")
                    for j in range(2):
                        c = 2 * i + j
                        last = pe.matmul(bank[:, j * T:(j + 1) * T], con("block_ones"), src[:, c * T:(c + 1) * T], start=True, stop=True)
                    last.then_inc(*banks.filled())
            pe.wait_ge(*W.at("y"))
            project_all("rwkv_out", chunks(w_["lw"], 8), "ro")
            pe_rms(7, [[chunks(tmp[1], 8)[:, c, :] for c in range(DC)]])

            def ple(l, x_ready):
                w = ring[:, slot_of[f"ple_w{l}"] * SLOT:slot_of[f"ple_w{l}"] * SLOT + 2 * D].rearrange("p (c n) -> p c n", c=2)
                pe.wait_ge(pt_loaded, 16)
                use_tile(f"ple_w{l}")
                project(w, z["pt"][:, 512 * l:512 * (l + 1)].rearrange("p (c t) -> p c t", c=2), [f"pe{l}_{i}" for i in range(4)],
                        fs=range(8), nc_=2)
                release_tile()
                pe.wait_ge(*x_ready)
                project_all(f"ple_gate{l}_", xv, f"pg{l}_")
                pe_rms((8, 11)[l], [[chunks(sq4, 8)[:, c, :] for c in range(DC)]])

            ple(0, W.at("attn_in"))
            pe_rms(9, [[chunks(sq4, 8)[:, c, :] for c in range(DC)]])
            pe.wait_ge(*Y.at("hkv"))
            hkv, hq = chunks(z["hkv"], 8), chunks(z["hq"], 8)
            project_all("kv", hkv, "kk")
            project_rows(lambda j: f"kv{2 + j}", hkv, "vv")

            def rotate(name, src, evac):
                pe.wait_ge(*evac)
                for i in range(4):
                    bank = banks.open(pe, f"{name}{i}")
                    pe.matmul(bank[:, :], con("rot"), src[:, 512 * i:512 * (i + 1)], start=True, stop=True).then_inc(*banks.filled())

            pe.wait_ge(*Y.at("hq"))
            project_all("b_in", hq, "qq")
            rotate("kr", z["kt"], Z.at("k"))
            rotate("qr", z["qt"], Z.at("q"))
            for j in range(2):
                project(slot(use_tile(f"b_in{2 + j}")), hq, (f"gg{2 * j}", f"gg{2 * j + 1}"))
                release_tile()
            pe.wait_ge(*Y.at("kt"))
            pe.wait_ge(*Y.at("qt"))
            kt, qt = chunks(z["kt"], 8), chunks(z["qt"], 8)

            def diff_scores(hh):
                for c in range(2):
                    r = slice(64 * c, 64 * c + 64)
                    bank = banks.open(pe, f"d{hh}{c}")
                    pe.matmul(bank[:, 0:P], qt[r, hh, 0:P], kt[r, hh, 0:P], start=True, stop=True)
                    pe.matmul(bank[:, P:3 * P], qt[r, hh, P:T], kt[r, hh, :], start=True, stop=True).then_inc(*banks.filled())

            def diff_turn(hh):
                pe.wait_ge(*Y.at(f"da{hh}"))
                bank = banks.open(pe, f"at{hh}")
                for j in range(3):
                    last = pe.transpose(bank[:, j * P:(j + 1) * P], dprob[:, hh, 0, j * P:(j + 1) * P], ident)
                last.then_inc(*banks.filled())

            def diff_values(h2):
                bank = banks.open(pe, f"do{h2}")
                for j in range(2):
                    hh = 2 * h2 + j
                    pe.wait_ge(*banks.emptied(f"at{hh}"))
                    v0, v1 = (z["v"][:, t * D + hh * P:t * D + (hh + 1) * P] for t in range(2))
                    pe.matmul(bank[:, j * T:j * T + P], v0, dat[:, hh, 0:P], start=True, stop=True)
                    pe.matmul(bank[:, j * T + P:(j + 1) * T], v0, dat[:, hh, P:2 * P], start=True, stop=False)
                    last = pe.matmul(bank[:, j * T + P:(j + 1) * T], v1, dat[:, hh, 2 * P:3 * P], start=False, stop=True)
                last.then_inc(*banks.filled())

            for hh in range(8):
                diff_scores(hh)
                if hh >= 2:
                    diff_turn(hh - 2)
            diff_turn(6)
            diff_turn(7)
            for h2 in range(4):
                diff_values(h2)
            pe.wait_ge(*Z.at("o_sq"))
            for i in range(4):
                bank = banks.open(pe, f"on{i}")
                pe.matmul(bank[:, :], ones, sq4[:, 512 * i:512 * (i + 1)], start=True, stop=True).then_inc(*banks.filled())
            pe.wait_ge(*Y.at("o"))
            project_all("b_out", chunks(z["ot"], 8), "bo")
            pe_rms(10, [[chunks(sq4, 8)[:, c, :] for c in range(DC)]])
            ple(1, Y.at("x4"))


        @block.scalar
        def _(act):
            act.wait_ge(params_loaded, 32)
            act.activation(s["cond"], par("c"), ACT.Silu).then_inc(*A.mark("cond"))
            act.wait_ge(x_loaded, 16)
            act.activation(m["sq"], xt[:], ACT.Square).then_inc(rms_squares, 1)
            act_rms(0, T)
            act.wait_ge(*V.at("zeros"))
            for i in range(4):
                act.wait_ge(*banks.ready(f"xbc{i}"))
                act.activation(xbc[:, 2 * i:2 * i + 2, 3:3 + T], chunks(banks[f"xbc{i}"][:, :], 2), ACT.Copy)\
                   .then_inc(*banks.release(f"xbc{i}"))
            for t in range(TT):
                act.wait_ge(*banks.ready(f"e{t}"))
                act.activation(ebuf[:, t, :], banks[f"e{t}"][:, 0:268], ACT.Copy).then_inc(*banks.release(f"e{t}"))
            act.activation(s["ea"], par("ssd_a_log"), ACT.Exp).then_inc(*A.mark("ea"))
            act.wait_ge(*V.at("spa"))
            act.activation(s["spu"], s["spa"], ACT.Exp, scale=-1.0).then_inc(*A.mark("spu"))
            act.wait_ge(*banks.ready("glu_b"))
            act.activation(m["sg"], banks["glu_b"][:, :], ACT.Sigmoid).then_inc(*banks.release("glu_b"))
            act.wait_ge(*V.at("xconv"))
            for c in range(DC):
                ins = act.activation(conv[:, c, :], conv[:, c, :], ACT.Silu, bias=par("ssd_conv_b", c, 1))
            ins.then_inc(*A.mark("silu_conv"))
            act.wait_ge(*V.at("tdiff"))
            act.activation(s["dte"], s["tdiff"], ACT.Exp).then_inc(*A.mark("dte"))
            for half in range(2):
                act.wait_ge(*banks.ready(f"acs1{half}"))
                ins = act.activation(cexp[:, 4 * half:4 * half + 4, :], chunks(banks[f"acs1{half}"][:, :], 4), ACT.Exp)
            ins.then_inc(*A.mark("cexp"))
            act.wait_ge(*V.at("args"))
            act.activation(m["decay"], m["decay"], ACT.Exp).then_inc(*A.mark("decay"))
            for i in range(2):
                act.wait_ge(*banks.ready(f"z{i}"))
                act.activation(m["zs"][:, 512 * i:512 * i + 512], banks[f"z{i}"][:, :], ACT.Silu)\
                   .then_inc(*banks.release(f"z{i}"))
            act.wait_ge(*banks.ready("brow"))
            act.activation(m["brow"], banks["brow"][:, 0:T], ACT.Copy).then_inc(*banks.release("brow"))
            for i, name in enumerate(("q", "k")):
                act.wait_ge(*banks.ready(name))
                act.activation(m["qk"][:, 512 * i:512 * i + 512], banks[name][:, :], ACT.Copy, scale=(0.125, 1.0)[i])\
                   .then_inc(*banks.release(name))
            act.wait_ge(*V.at("scores"))
            for hd in range(4):
                for q, (lo, hi) in enumerate(((0, P), (P, 3 * P))):
                    i = 2 * hd + q
                    ins = act.activation(prob[:, hd, lo:hi], prob[:, hd, lo:hi], ACT.Exp, bias=s["nmx"][:, i:i + 1],
                                         accum_out=s["sums"][:, i:i + 1])
            ins.then_inc(*A.mark("exp"))
            act.wait_ge(*V.at("ln_centred"))
            act.activation(m["sq"][:, 0:512], m["lnx"], ACT.Square).then_inc(rms_squares, 1)
            act_rms(1, T)
            act.wait_ge(*V.at("y_gated"))
            act.activation(m["sq"][:, 512:1536], m["y"][:, 0:1024], ACT.Square).then_inc(rms_squares, 1)
            act_rms(2, 2 * T)
            act.wait_ge(*banks.ready("o"))
            act.activation(m["y"][:, 1024:1536], banks["o"][:, :], ACT.Copy).then_inc(*banks.release("o"))
            act.wait_ge(*banks.emptied("o"))
            act.activation(m["sq"][:, 1536:2048], m["y"][:, 1024:1536], ACT.Square).then_inc(rms_squares, 1)
            act_rms(3, T)
            act.wait_ge(*V.at("ln_norm"))
            for c in range(2):
                ins = act.activation(y[:, 6 + c, :], m["lnx"][:, c * T:(c + 1) * T], ACT.Silu, scale=par("cm_ln_g", c, 1),
                                     bias=par("cm_ln_b", c, 1))
            ins.then_inc(*A.mark("silu_ln"))
            act.wait_ge(*V.at("x1"))
            act.activation(m["sq"], xt[:], ACT.Square).then_inc(rms_squares, 1)
            act_rms(4, T)
            for t in range(TT):
                for half in range(2):
                    act.wait_ge(*banks.ready(f"hrow{t}{half}"))
                    at = t * D + half * 512
                    act.activation(m["conv"][:, at:at + 512], banks[f"hrow{t}{half}"][:, :], ACT.Copy)\
                       .then_inc(*banks.release(f"hrow{t}{half}"))
            act.wait_ge(*R.at("gd"))
            act.activation(mo["ge"], mo["gd"], ACT.Exp).then_inc(*S.mark("ge"))
            act.wait_ge(*R.at("md"))
            act.activation(mo["e2"], mo["md"], ACT.Exp).then_inc(*S.mark("e2"))

            def expert(e, p_):
                act.wait_ge(xt_done, e + 1)
                act.activation(xet[p_], psum[p_][:, :], ACT.Copy).then_inc(xt_copied, 1)
                act.wait_ge(gu_done, e + 1)
                act.activation(sg_[p_], psum[2 + p_][:, 0:T], ACT.Silu).then_inc(silu_done, 1)

            expert_loop(act, expert)
            act.wait_ge(*R.at("info"))
            spare_loop(act, lambda j: expert(EXPERTS + j, 0))
            act.wait_ge(*R.at("x2"))
            act.activation(m["sq"], xt[:], ACT.Square).then_inc(rms_squares, 1)
            act_rms(5, T)
            act.wait_ge(*R.at("final"))
            act.activation(m["sq"], xt[:], ACT.Square).then_inc(rms_squares, 1)
            act_rms(6, T)
            act.wait_ge(*banks.ready("lora0"))
            act.activation(w_["hid"][0:64, 0:T], banks["lora0"][0:64, 0:T], ACT.Tanh).then_inc(*banks.release("lora0"))
            act.wait_ge(*banks.emptied("lora0"))
            act.nop().then_inc(*X.mark("tanh"))
            act.wait_ge(*banks.ready("lora1"))
            act.activation(w_["hid"][0:64, T:2 * T], banks["lora1"][0:64, 0:T], ACT.Copy).then_inc(*banks.release("lora1"))
            act.wait_ge(*banks.emptied("lora1"))
            act.nop().then_inc(*X.mark("lora_a"))
            for i, (out, bias, mark) in enumerate(((w_["lw"], "a_w0_2", "sigw"), (ar["a"], "a_a0_2", "siga"))):
                for f in range(0, DC, 2):
                    act.wait_ge(*banks.ready(f"pre{i}{f}"))
                    for j in range(2):
                        ins = act.activation(out[:, (f + j) * T:(f + j + 1) * T], banks[f"pre{i}{f}"][:, j * T:(j + 1) * T], ACT.Sigmoid,
                                             bias=par(bias, f + j, 1))
                    ins.then_inc(*banks.release(f"pre{i}{f}"))
                act.wait_ge(*banks.emptied(f"pre{i}6"))
                act.nop().then_inc(*X.mark(mark))

            def evacuate(name, out, func, mark=None):
                for i in range(4):
                    act.wait_ge(*banks.ready(f"{name}{i}"))
                    act.activation(out[:, 512 * i:512 * (i + 1)], banks[f"{name}{i}"][:, :], func).then_inc(*banks.release(f"{name}{i}"))
                if mark:
                    act.wait_ge(*banks.emptied(f"{name}3"))
                    act.nop().then_inc(*mark)

            evacuate("r", w_["r"], ACT.Copy, X.mark("r"))
            evacuate("k_", w_["k"], ACT.Copy, X.mark("k"))
            act.wait_ge(*W.at("vu_zero"))
            for j in range(2):
                for t in range(TT):
                    act.wait_ge(*banks.ready(f"v{j}{t}"))
                    for e in range(2):
                        r = slice(64 * e, 64 * e + 64)
                        ins = act.activation(vu[r, 2 * t + e, 512 * j:512 * (j + 1)], banks[f"v{j}{t}"][r, :], ACT.Copy)
                    ins.then_inc(*banks.release(f"v{j}{t}"))
            act.wait_ge(*W.at("bonus_in"))
            for i in range(4):
                act.wait_ge(*banks.ready(f"kn{i}"))
                act.activation(ar["kk"][:, 512 * i:512 * (i + 1)], banks[f"kn{i}"][:, :], ACT.Sqrt).then_inc(*banks.release(f"kn{i}"))
            act.wait_ge(*banks.emptied("kn3"))
            act.nop().then_inc(*X.mark("kk_norm"))
            evacuate("g", w_["g"], ACT.Silu, X.mark("g"))
            act.wait_ge(*W.at("args"))
            act.activation(ar["e1"], ar["cum"], ACT.Exp)
            act.activation(ar["e2"], ar["cum"], ACT.Exp, scale=-1.0)
            act.activation(ar["e3"], ar["e3"], ACT.Exp).then_inc(*X.mark("exp"))
            for c in range(NC):
                for half in range(2):
                    act.wait_ge(*banks.ready(f"kbt{c}{half}"))
                    act.activation(kbrow[:, 4 * half:4 * half + 4, c, :], chunks(banks[f"kbt{c}{half}"][:, :], 4), ACT.Copy,
                                   scale=con(("sign_even", "sign_odd")[c % 2])).then_inc(*banks.release(f"kbt{c}{half}"))
            for q in range(2):
                for level in range(6):
                    for h4 in range(4):
                        act.wait_ge(*banks.ready(f"x{q}_{level}_{h4}"))
                        if 0 < level < 5:
                            act.wait_ge(*banks.ready(f"xt{q}_{level}_{h4}"))
                        act.activation(xm[:, 4 * h4:4 * h4 + 4, :], chunks(banks[f"x{q}_{level}_{h4}"][:, :], 4), ACT.Copy)\
                           .then_inc(*banks.release(f"x{q}_{level}_{h4}"))
            for c in range(NC):
                rows = slice(64, 128) if c % 2 == 0 else slice(0, 64)
                act.wait_ge(*banks.ready(f"w{c}1"))
                act.activation(wsb[rows, 512:1024], banks[f"w{c}1"][rows, :], ACT.Copy).then_inc(*banks.release(f"w{c}1"))
                act.wait_ge(*banks.ready(f"u{c}1"))
                act.activation(vu[rows, c, 512:1024], banks[f"u{c}1"][rows, :], ACT.Copy).then_inc(*banks.release(f"u{c}1"))
                act.wait_ge(*banks.ready(f"yr{c}"))
                act.activation(chunks(w_["lw"], 8)[:, :, c * C:(c + 1) * C], chunks(banks[f"yr{c}"][:, :], 8), ACT.Copy)\
                   .then_inc(*banks.release(f"yr{c}"))
            act.wait_ge(*W.at("centred"))
            act.activation(tmp[1], tmp[0], ACT.Square).then_inc(*X.mark("centred_sq"))
            for i in range(4):
                act.wait_ge(*banks.ready(f"gvar{i}"))
                act.activation(tmp[2][:, 512 * i:512 * (i + 1)], banks[f"gvar{i}"][:, :], ACT.Sqrt, scale=1.0 / 64, bias=gn_eps[:, 0:1])\
                   .then_inc(*banks.release(f"gvar{i}"))
            evacuate("ro", tmp[0], ACT.Copy)
            act.wait_ge(*banks.emptied("ro3"))
            act.activation(tmp[1], tmp[0], ACT.Square).then_inc(rms_squares, 1)
            act_rms(7, T)
            act.wait_ge(*Y.at("lam_sum"))
            act.activation(z["le"], z["ls"], ACT.Exp).then_inc(*Z.mark("lam_exp"))

            def squares(src):
                act.activation(sq4, src, ACT.Square).then_inc(rms_squares, 1)

            def ple(l):
                evacuate(f"pe{l}_", z["eb"], ACT.Copy)
                evacuate(f"pg{l}_", z["gb"], ACT.Sigmoid)
                act.wait_ge(*Y.at(f"ge{l}"))
                squares(z["gb"])
                act_rms((8, 11)[l], T)

            ple(0)
            act.wait_ge(*Y.at("x3"))
            squares(xt[:])
            act_rms(9, T)
            evacuate("kk", z["kt"], ACT.Copy, Z.mark("k"))
            for j in range(2):
                for t in range(TT):
                    act.wait_ge(*banks.ready(f"vv{j}{t}"))
                    act.activation(z["v"][:, t * D + 512 * j:t * D + 512 * (j + 1)], banks[f"vv{j}{t}"][:, :], ACT.Copy)\
                       .then_inc(*banks.release(f"vv{j}{t}"))
            for i in range(4):
                act.wait_ge(*banks.ready(f"qq{i}"))
                act.activation(z["qt"][:, 512 * i:512 * (i + 1)], banks[f"qq{i}"][:, :], ACT.Copy, scale=0.125).then_inc(*banks.release(f"qq{i}"))
            act.wait_ge(*banks.emptied("qq3"))
            act.nop().then_inc(*Z.mark("q"))
            evacuate("gg", z["gate"], ACT.Silu, Z.mark("gate"))
            for hh in range(8):
                act.wait_ge(*Y.at(f"ds{hh}"))
                for c in range(2):
                    for q, (lo, hi) in enumerate(((0, P), (P, 3 * P))):
                        i = 4 * hh + 2 * c + q
                        ins = act.activation(dprob[:, hh, c, lo:hi], dprob[:, hh, c, lo:hi], ACT.Exp, bias=z["nmx"][:, i:i + 1],
                                             accum_out=z["sums"][:, i:i + 1])
                ins.then_inc(*Z.mark(f"dx{hh}"))
            evacuate("do", z["ot"], ACT.Copy)
            act.wait_ge(*banks.emptied("do3"))
            act.activation(sq4, z["ot"], ACT.Square).then_inc(*Z.mark("o_sq"))
            for i in range(4):
                act.wait_ge(*banks.ready(f"on{i}"))
                act.activation(z["eb"][:, 512 * i:512 * (i + 1)], banks[f"on{i}"][:, :], ACT.Sqrt, scale=1.0 / P, bias=z["eps"])\
                   .then_inc(*banks.release(f"on{i}"))
            act.wait_ge(*banks.emptied("on3"))
            act.nop().then_inc(*Z.mark("o_norm"))
            evacuate("bo", z["gb"], ACT.Copy)
            act.wait_ge(*banks.emptied("bo3"))
            squares(z["gb"])
            act_rms(10, T)
            ple(1)

        @block.vector
        def _(dve):
            link = lambda ins: dve_steps.link(dve, ins)

            def taps(out, src, weight, n, count):
                at = {}
                for k in range(n):
                    for c in range(count):
                        window = src[:, c, k:k + T]
                        if k == 0:
                            ins = dve.tensor_scalar(out[:, c, :], window, weight(c, k), None, ALU.mult)
                        else:
                            dve.wait_ge(dve_steps.sem, at[c])
                            ins = dve.scalar_tensor_tensor(out=out[:, c, :], in0=window, scalar=weight(c, k), in1=out[:, c, :],
                                                           op0=ALU.mult, op1=ALU.add)
                        if k == n - 1 and c == count - 1:
                            return ins
                        at[c] = dve_steps.step(ins)

            def modulate(out, src, scale, shift, buf):
                link(dve.tensor_tensor(buf, src, rst[:, 0:T].unsqueeze(1).to_broadcast([P, DC, T]), ALU.mult))
                for c in range(DC):
                    ins = dve.tensor_scalar(out[:, c, :], buf[:, c, :], scale[:, c:c + 1], shift[:, c:c + 1], ALU.mult, ALU.add)
                return ins

            dve.memset(xbc[:, :, 0:3], 0.0)
            dve.memset(u[:, :, 0:30], 0.0).then_inc(*V.mark("zeros"))
            dve_rms(0, D, T)
            dve.wait_ge(*banks.ready("mod"))
            mod = s["mod"]
            dve.tensor_tensor(mod[:, 0:16], banks["mod"][:, 0:16], par("ada_b", 0, 16), ALU.add).then_inc(*banks.release("mod"))
            dve.wait_ge(*banks.emptied("mod"))
            link(dve.scalar_tensor_tensor(out=s["gmix"], in0=mod[:, 8:16], scalar=1.0, in1=par("norm_mix_g"),
                                          op0=ALU.add, op1=ALU.mult))
            modulate(h, xv, s["gmix"], mod[:, 0:8], conv).then_inc(*V.mark("h"))
            for i in range(4):
                dve.wait_ge(*banks.emptied(f"xbc{i}"))
            dve.wait_ge(*V.at("h"))
            taps(conv, xbc, lambda c, k: par("ssd_conv_w", 4 * c + k, 1), 4, 8).then_inc(*V.mark("xconv"))
            spx = chunks(s["spx"], 2)
            for t in range(TT):
                dve.wait_ge(*banks.emptied(f"e{t}"))
                dve.tensor_tensor(spx[:, t, 0:8], ebuf[:, t, 260:268], par("ssd_dt_bias"), ALU.add)
                ins = dve.scalar_tensor_tensor(out=spx[:, t, 8:12], in0=ebuf[:, t, 256:260], scalar=-1.0, in1=par("fox_f_bias"),
                                               op0=ALU.mult, op1=ALU.subtract)
            link(ins)
            dve.scalar_tensor_tensor(out=s["spa"], in0=s["spx"], scalar=-1.0, in1=s["spx"], op0=ALU.mult, op1=ALU.max)\
               .then_inc(*V.mark("spa"))
            link(dve.tensor_scalar(s["spm"], s["spx"], 0.0, None, ALU.max))
            dve.wait_ge(*A.at("spu"))
            link(dve.tensor_scalar(s["spw"], s["spu"], 2.0, None, ALU.add))
            link(dve.reciprocal(s["spr"], s["spw"]))
            link(dve.tensor_tensor(s["spl"], s["spu"], s["spr"], ALU.mult))
            link(dve.tensor_tensor(s["spd"], s["spl"], s["spl"], ALU.mult))
            link(dve.tensor_scalar(s["spw"], s["spd"], 1.0 / 15, None, ALU.mult))
            for odd in (13, 11, 9, 7, 5, 3):
                link(dve.scalar_tensor_tensor(out=s["spw"], in0=s["spw"], scalar=1.0 / odd, in1=s["spd"], op0=ALU.add, op1=ALU.mult))
            link(dve.scalar_tensor_tensor(out=s["spr"], in0=s["spw"], scalar=1.0, in1=s["spl"], op0=ALU.add, op1=ALU.mult))
            link(dve.scalar_tensor_tensor(out=s["sp"], in0=s["spr"], scalar=2.0, in1=s["spm"], op0=ALU.mult, op1=ALU.add))
            dve.wait_ge(*A.at("ea"))
            sp, cumin = chunks(s["sp"], 2), chunks(s["cumin"], 2)
            dve.scalar_tensor_tensor(out=cumin[:, :, 0:8], in0=sp[:, :, 0:8], scalar=-1.0,
                                     in1=s["ea"].unsqueeze(1).to_broadcast([P, 2, 8]), op0=ALU.mult, op1=ALU.mult)
            dve.tensor_copy(cumin[:, :, 8:12], sp[:, :, 8:12]).then_inc(*V.mark("cumin"))
            dve.wait_ge(*banks.emptied("glu_b"))
            dve.wait_ge(*banks.ready("glu_a"))
            dve.tensor_tensor(u[:, :, 30:30 + T], chunks(banks["glu_a"][:, :], 2), chunks(m["sg"], 2), ALU.mult)\
               .then_inc(*banks.release("glu_a"))
            dve.wait_ge(*banks.emptied("glu_a"))
            dve.nop().then_inc(*V.mark("u_gated"))
            dve.wait_ge(*banks.ready("acs_rows"))
            link(dve.tensor_scalar(s["nacs"], banks["acs_rows"][:, 0:16], -1.0, None, ALU.mult))
            dve.tensor_copy(s["nq"], banks["acs_rows"][:, 16:24]).then_inc(*banks.release("acs_rows"))
            for half in range(2):
                dve.wait_ge(*banks.ready(f"acs0{half}"))
                end = chunks(banks[f"acs0{half}"][:, :], 4)[:, :, P - 1]
                ins = dve.tensor_tensor(s["tdiff"][:, 4 * half:4 * half + 4], end, s["nacs"][:, 4 * half:4 * half + 4], ALU.add)
            ins.then_inc(*V.mark("tdiff"))
            for t in range(TT):
                for half in range(2):
                    dve.wait_ge(*banks.ready(f"acs{t}{half}"))
                    if t:
                        dve.wait_ge(*A.at("cexp"))
                    for j in range(4):
                        hh = 4 * half + j
                        ins = dve.tensor_scalar(decay[:, t, hh, :], banks[f"acs{t}{half}"][:, j * P:(j + 1) * P],
                                                s["nacs"][:, 8 * t + hh:8 * t + hh + 1], 0.0, ALU.add, ALU.min)
                    ins.then_inc(*banks.release(f"acs{t}{half}"))
            dve.wait_ge(*banks.emptied("acs11"))
            dve.nop().then_inc(*V.mark("args"))
            for half in range(2):
                dve.wait_ge(*banks.ready(f"ncum{half}"))
                for j in range(2):
                    hd, b = 2 * half + j, banks[f"ncum{half}"][:, j * T:(j + 1) * T]
                    link(dve.tensor_tensor(prob[:, hd, 0:P], b[:, 0:P], con("causal"), ALU.add))
                    link(dve.tensor_copy(prob[:, hd, P:2 * P], b[:, 0:P]))
                    ins = dve.tensor_tensor(prob[:, hd, 2 * P:3 * P], b[:, P:T], con("causal"), ALU.add)
                    if j == 0:
                        link(ins)
                ins.then_inc(*banks.release(f"ncum{half}"))
            for t in range(TT):
                dve.wait_ge(*banks.ready(f"xrow{t}"))
                dve.tensor_tensor(xdt[:, t, :].rearrange("p (h i) -> p h i", h=8), chunks(banks[f"xrow{t}"][:, :], 8),
                                  sp[:, t, 0:8].unsqueeze(2).to_broadcast([P, 8, 64]), ALU.mult)\
                   .then_inc(*banks.release(f"xrow{t}"))
            dve.wait_ge(*banks.emptied("xrow0"))
            dve.wait_ge(*A.at("dte"))
            dve.tensor_tensor(chunks(m["xde"], 8), chunks(xdt[:, 0, :], 8),
                              s["dte"].unsqueeze(2).to_broadcast([P, 8, 64]), ALU.mult).then_inc(*V.mark("xde"))
            dve.wait_ge(*banks.ready("cb"))
            dve.tensor_tensor(chunks(m["cb"], 4), chunks(banks["cb"][:, :], 4),
                              con("tri").unsqueeze(1).to_broadcast([P, 4, P]), ALU.mult).then_inc(*banks.release("cb"))
            dve.wait_ge(*banks.emptied("cb"))
            dve.wait_ge(*A.at("decay"))
            for t in range(TT):
                for g in range(2):
                    block_ = decay[:, t, 4 * g:4 * g + 4, :]
                    ins = dve.tensor_tensor(block_, block_, cb[:, t, g, :].unsqueeze(1).to_broadcast([P, 4, P]), ALU.mult)
            ins.then_inc(*V.mark("decay"))
            dve.wait_ge(*A.at("silu_conv"))
            for g in range(2):
                block_ = cexp[:, 4 * g:4 * g + 4, :]
                ins = dve.tensor_tensor(block_, block_, conv[:, 6 + g, P:T].unsqueeze(1).to_broadcast([P, 4, P]), ALU.mult)
            ins.then_inc(*V.mark("cexp"))
            dve.wait_ge(*banks.ready("st"))
            dve.tensor_copy(m["st"], banks["st"][:, :]).then_inc(*banks.release("st"))
            for hd in range(4):
                dve.wait_ge(*banks.ready(f"s{hd}"))
                for q, (lo, hi) in enumerate(((0, P), (P, 3 * P))):
                    ins = dve.scalar_tensor_tensor(out=prob[:, hd, lo:hi], in0=banks[f"s{hd}"][:, lo:hi],
                                                   scalar=s["nq"][:, 4 * q + hd:4 * q + hd + 1], in1=prob[:, hd, lo:hi],
                                                   op0=ALU.subtract, op1=ALU.add)
                ins.then_inc(*banks.release(f"s{hd}"))
                dve.wait_ge(*banks.emptied(f"s{hd}"))
                for q, (lo, hi) in enumerate(((0, P), (P, 3 * P))):
                    ins = dve.reduce_max(s["mx"][:, 2 * hd + q:2 * hd + q + 1], prob[:, hd, lo:hi], AX.X)
            link(ins)
            dve.tensor_scalar(s["nmx"], s["mx"][:, 0:8], -1.0, None, ALU.mult).then_inc(*V.mark("scores"))
            dve.wait_ge(*A.at("exp"))
            link(dve.reciprocal(s["rs"], s["sums"]))
            for hd in range(4):
                for q, (lo, hi) in enumerate(((0, P), (P, 3 * P))):
                    i = 2 * hd + q
                    ins = dve.tensor_scalar(prob[:, hd, lo:hi], prob[:, hd, lo:hi], s["rs"][:, i:i + 1], None, ALU.mult)
            ins.then_inc(*V.mark("probs"))
            for hd in range(4):
                dve.wait_ge(*banks.ready(f"pt{hd}"))
                dve.tensor_copy(ptr[:, hd, :], banks[f"pt{hd}"][:, 0:3 * P]).then_inc(*banks.release(f"pt{hd}"))
            for i in range(2):
                dve.wait_ge(*banks.ready(f"y{i}"))
                for j in range(2):
                    c = 2 * i + j
                    ins = dve.scalar_tensor_tensor(out=y[:, c, :], in0=conv[:, c, :], scalar=par("ssd_d", c, 1),
                                                   in1=banks[f"y{i}"][:, j * T:(j + 1) * T], op0=ALU.mult, op1=ALU.add)
                ins.then_inc(*banks.release(f"y{i}"))
                dve.wait_ge(*banks.emptied(f"y{i}"))
                dve.wait_ge(*banks.emptied(f"z{i}"))
                half = slice(512 * i, 512 * i + 512)
                ins = dve.tensor_tensor(m["y"][:, half], m["y"][:, half], m["zs"][:, half], ALU.mult)
                if i == 0:
                    link(ins)
            ins.then_inc(*V.mark("y_gated"))
            lx = chunks(m["sg"], 2)
            link(taps(lx, u, lambda c, k: par("cm_conv_w", 31 * c + k, 1), 31, 2))
            for c in range(2):
                ins = dve.tensor_scalar(lx[:, c, :], lx[:, c, :], par("cm_conv_b", c, 1), None, ALU.add)
            ins.then_inc(*V.mark("conv"))
            dve.wait_ge(*banks.ready("ln_mean"))
            lnx = chunks(m["lnx"], 2)
            dve.tensor_scalar(var[:, 0:T], banks["ln_mean"][:, 0:T], 1.0 / 256, None, ALU.mult).then_inc(*banks.release("ln_mean"))
            dve.wait_ge(*banks.emptied("ln_mean"))
            dve.tensor_tensor(lnx, lx, var[:, 0:T].unsqueeze(1).to_broadcast([P, 2, T]), ALU.subtract)\
               .then_inc(*V.mark("ln_centred"))
            dve_rms(1, 256, T)
            dve.tensor_tensor(lnx, lnx, rst[:, 0:T].unsqueeze(1).to_broadcast([P, 2, T]), ALU.mult).then_inc(*V.mark("ln_norm"))
            dve_rms(2, 256, 2 * T)
            for c in range(4):
                ins = dve.scalar_tensor_tensor(out=y[:, c, :], in0=y[:, c, :], scalar=par("ssd_norm_g", c, 1),
                                               in1=rst[:, (c // 2) * T:(c // 2 + 1) * T], op0=ALU.mult, op1=ALU.mult)
            ins.then_inc(*V.mark("y_ssd"))
            dve_rms(3, 256, T)
            for c in range(2):
                ins = dve.scalar_tensor_tensor(out=y[:, 4 + c, :], in0=y[:, 4 + c, :], scalar=par("fox_norm_g", c, 1),
                                               in1=rst[:, 0:T], op0=ALU.mult, op1=ALU.mult)
            ins.then_inc(*V.mark("y_fox"))
            dve.wait_ge(weights_used, weights_used_after["ada11"])
            link(dve.tensor_tensor(mod[:, 16:48], mod_bank[:, 0:32], par("ada_b", 16, 32), ALU.add))
            for i in range(4):
                dve.wait_ge(*banks.ready(f"wo{i}"))
                for j in range(2):
                    c = 2 * i + j
                    ins = dve.scalar_tensor_tensor(out=xv[:, c, :], in0=banks[f"wo{i}"][:, j * T:(j + 1) * T],
                                                   scalar=mod[:, 16 + c:17 + c], in1=xv[:, c, :], op0=ALU.mult, op1=ALU.add)
                ins.then_inc(*banks.release(f"wo{i}"))
            for i in range(4):
                dve.wait_ge(*banks.emptied(f"wo{i}"))
            dve.scalar_tensor_tensor(out=s["gffn"], in0=mod[:, 32:40], scalar=1.0, in1=par("norm_ffn_g"),
                                     op0=ALU.add, op1=ALU.mult).then_inc(*V.mark("x1"))
            dve_rms(4, D, T)
            dve.wait_ge(*V.at("x1"))
            modulate(h, xv, s["gffn"], mod[:, 24:32], zq).then_inc(*V.mark("h2"))
            dve.wait_ge(*V.at("h2"))
            v = lambda n, k=2: mo[n].rearrange("p (t j) -> p t j", t=k)
            over = lambda ap, shape: ap.to_broadcast(shape)
            dve.memset(zero_list[:], 0)
            dve.tensor_copy(token_id[:], con("token")).then_inc(*R.mark("ids"))
            rl = v("rl")
            dve.wait_ge(*banks.ready("router"))
            dve.tensor_tensor(rl, chunks(banks["router"][:, 0:72], 2), par("b_router").unsqueeze(1).to_broadcast([P, 2, 36]),
                              ALU.add).then_inc(*banks.release("router"))
            dve.wait_ge(*banks.emptied("router"))
            iota = con("iota")

            def first_max(values, best, diff, index_, hot, n, mark=None):
                link(dve.tensor_reduce(mo[best], values, AX.X, ALU.max))
                ins = dve.tensor_tensor(v(diff), values, mo[best].unsqueeze(2).to_broadcast([P, 2, n]), ALU.subtract)
                if mark:
                    ins.then_inc(*R.mark(mark))
                    dve.wait_ge(*R.at(mark))
                else:
                    link(ins)
                t_ = "gt" if n == 4 else "et"
                link(dve.tensor_scalar(v(t_), v(diff), 0.0, 64.0, ALU.is_lt, ALU.mult))
                link(dve.tensor_tensor(v(t_), v(t_), iota[:, 0:n].unsqueeze(1).to_broadcast([P, 2, n]), ALU.add))
                link(dve.tensor_reduce(mo[index_], v(t_), AX.X, ALU.min))
                link(dve.tensor_tensor(hot, iota[:, 0:n].unsqueeze(1).to_broadcast([P, 2, n]),
                                       mo[index_].unsqueeze(2).to_broadcast([P, 2, n]), ALU.is_equal))

            first_max(rl[:, :, 0:4], "gm", "gd", "gi", v("ohg"), 4, "gd")
            ep = mo["ep"].rearrange("p (t g j) -> p t g j", t=2, g=4)
            for t in range(TT):
                ins = dve.tensor_tensor(ep[:, t], rl[:, t, 4:36].rearrange("p (g j) -> p g j", g=4),
                                        v("ohg")[:, t, :].unsqueeze(2).to_broadcast([P, 4, 8]), ALU.mult)
            link(ins)
            for t in range(TT):
                ins = dve.tensor_reduce(v("el")[:, t, :], ep[:, t].rearrange("p g j -> p j g"), AX.X, ALU.add)
            link(ins)
            oh8 = mo["oh8"].rearrange("p (k t j) -> p k t j", k=2, t=2)
            first_max(v("el"), "m1", "ed", "ei", oh8[:, 0], 8)
            link(dve.scalar_tensor_tensor(out=v("el2"), in0=oh8[:, 0], scalar=-1e30, in1=v("el"), op0=ALU.mult, op1=ALU.add))
            first_max(v("el2"), "m2", "ed", "ei", oh8[:, 1], 8)
            dve.tensor_tensor(mo["md"], mo["m2"], mo["m1"], ALU.subtract).then_inc(*R.mark("md"))
            oh = mo["oh"].rearrange("p (k t g j) -> p k t g j", k=2, t=2, g=4)
            for k in range(2):
                for t in range(TT):
                    ins = dve.tensor_tensor(oh[:, k, t], v("ohg")[:, t, :].unsqueeze(2).to_broadcast([P, 4, 8]),
                                            oh8[:, k, t, :].unsqueeze(1).to_broadcast([P, 4, 8]), ALU.mult)
            link(ins)
            ohk = mo["oh"].rearrange("p (k n) -> p k n", k=2)
            dve.tensor_tensor(mo["hit"], ohk[:, 0], ohk[:, 1], ALU.add).then_inc(*R.mark("hits"))
            dve.wait_ge(*banks.ready("pos"))
            cnt = banks["pos"][:, 64:96]
            link(dve.tensor_scalar(mo["x"], cnt, float(SLOTS), None, ALU.is_gt))
            for n in (2, 3):
                link(dve.scalar_tensor_tensor(out=mo["x"], in0=cnt, scalar=float(n * SLOTS), in1=mo["x"], op0=ALU.is_gt, op1=ALU.add))
            link(dve.tensor_tensor_scan(out=mo["incl"], data0=ones[:, 0:32], data1=mo["x"], initial=0.0, op0=ALU.mult, op1=ALU.add))
            link(dve.tensor_tensor(mo["excl"], mo["incl"], mo["x"], ALU.subtract))
            prod = v("prod")

            def pick(out, table, shape_over_kt=None):
                for k in range(2):
                    ins = dve.tensor_tensor(prod[:, k, :].rearrange("p (t n) -> p t n", t=2),
                                            ohk[:, k, :].rearrange("p (t n) -> p t n", t=2), table, ALU.mult)
                link(ins)
                return dve.tensor_reduce(mo[out], mo["prod"].rearrange("p (a n) -> p a n", a=4), AX.X, ALU.add)

            pick("pos", chunks(banks["pos"][:, 0:64], 2)).then_inc(*banks.release("pos"))
            dve.wait_ge(*banks.emptied("pos"))
            link(pick("e", iota.unsqueeze(1).to_broadcast([P, 2, 32])))
            link(pick("ov", mo["excl"].unsqueeze(1).to_broadcast([P, 2, 32])))
            link(dve.tensor_scalar(mo["q"], mo["pos"], float(SLOTS), None, ALU.is_ge))
            link(dve.tensor_copy(mo["g0"], mo["q"]))
            for n in (2, 3):
                link(dve.scalar_tensor_tensor(out=mo["q"], in0=mo["pos"], scalar=float(n * SLOTS), in1=mo["q"], op0=ALU.is_ge, op1=ALU.add))
            link(dve.scalar_tensor_tensor(out=mo["slot"], in0=mo["q"], scalar=-float(SLOTS), in1=mo["pos"], op0=ALU.mult, op1=ALU.add))
            link(dve.scalar_tensor_tensor(out=mo["blk"], in0=mo["ov"], scalar=float(EXPERTS - 1), in1=mo["q"], op0=ALU.add, op1=ALU.add))
            link(dve.tensor_tensor(mo["blk"], mo["blk"], mo["e"], ALU.subtract))
            link(dve.tensor_tensor(mo["blk"], mo["blk"], mo["g0"], ALU.mult))
            link(dve.tensor_tensor(mo["blk"], mo["blk"], mo["e"], ALU.add))
            link(dve.scalar_tensor_tensor(out=mo["lst"], in0=mo["slot"], scalar=float(LIST), in1=mo["blk"], op0=ALU.mult, op1=ALU.add))
            link(dve.scalar_tensor_tensor(out=mo["row"], in0=mo["blk"], scalar=float(SLOTS), in1=mo["slot"], op0=ALU.mult, op1=ALU.add))
            dve.tensor_copy(list_at[:], mo["lst"])
            dve.tensor_copy(row_at[:], mo["row"]).then_inc(*R.mark("lists"))
            cmp = mo["cmp"].rearrange("p (j n) -> p j n", j=7)
            for j in range(SPARE):
                ins = dve.tensor_scalar(cmp[:, j, :], mo["incl"], float(j), None, ALU.is_le)
            link(ins)
            link(dve.tensor_reduce(mo["info"][:, 1:8], cmp, AX.X, ALU.add))
            link(dve.tensor_scalar(mo["info"][:, 1:8], mo["info"][:, 1:8], float(EXPERTS - 1), None, ALU.min))
            link(dve.tensor_copy(mo["info"][:, 0:1], mo["incl"][:, 31:32]))
            dve.tensor_copy(info[:], mo["info"]).then_inc(*R.mark("info"))
            dve.wait_ge(list_loaded, 32)
            link(dve.tensor_copy(mo["listf"], list_in[:]))
            link(dve.tensor_scalar(mo["listf"], mo["listf"], 2.0, con("half"), ALU.mult, ALU.add))
            dve.tensor_copy(gather_at[:], mo["listf"]).then_inc(*R.mark("gather_at"))
            dve.wait_ge(*S.at("ge"))
            link(dve.tensor_reduce(mo["gs"], v("ge"), AX.X, ALU.add))
            dve.wait_ge(*S.at("e2"))
            link(dve.tensor_scalar(mo["md"], mo["e2"], 1.0, None, ALU.add))
            link(dve.tensor_tensor(mo["gs"], mo["gs"], mo["md"], ALU.mult))
            link(dve.reciprocal(mo["w"][:, 0:2], mo["gs"]))
            dve.tensor_tensor(mo["w"][:, 2:4], mo["w"][:, 0:2], mo["e2"], ALU.mult).then_inc(*R.mark("weights"))

            def expert(e, p_, stored=None):
                dve.wait_ge(silu_done, e + 1)
                dve.tensor_tensor(hid[p_], psum[2 + p_][:, T:2 * T], sg_[p_], ALU.mult).then_inc(hid_done, 1)
                dve.wait_ge(ht_done, e + 1)
                dve.tensor_copy(ht[p_], psum[4][:, 0:T]).then_inc(ht_copied, 1)
                dve.wait_ge(y_done, e + 1)
                if stored:
                    dve.wait_ge(*stored)
                dve.tensor_copy(ys[p_], psum[5 + p_][:, :]).then_inc(y_copied, 1)

            def main(e, p_):
                stored = None if isinstance(e, int) else (y_stored[p_], 16 * (e - p_))
                expert(e, p_, stored)

            expert_loop(dve, main)
            for p_ in range(2):
                dve.wait_ge(y_stored[p_], 16 * EXPERTS)
            spare_loop(dve, lambda j: expert(EXPERTS + j, 0))
            yg = mo["yg"].rearrange("p (k t n) -> p k t n", k=2, t=2)
            for t in range(TT):
                dve.wait_ge(rows_gathered[t], 32)
                link(dve.tensor_scalar(yg[:, 0, t, :], yg[:, 0, t, :], mo["w"][:, t:t + 1], None, ALU.mult))
                dve.scalar_tensor_tensor(out=mo["comb"][:, t * D:(t + 1) * D], in0=yg[:, 1, t, :], scalar=mo["w"][:, 2 + t:3 + t],
                                         in1=yg[:, 0, t, :], op0=ALU.mult, op1=ALU.add).then_inc(*R.mark(f"comb{t}"))
            for t in range(TT):
                for half in range(2):
                    dve.wait_ge(*banks.ready(f"moe{t}{half}"))
                    for c in range(4):
                        cc = 4 * half + c
                        ins = dve.scalar_tensor_tensor(out=xv[:, cc, t * P:(t + 1) * P], in0=banks[f"moe{t}{half}"][:, c * P:(c + 1) * P],
                                                       scalar=mod[:, 40 + cc:41 + cc], in1=xv[:, cc, t * P:(t + 1) * P],
                                                       op0=ALU.mult, op1=ALU.add)
                    ins.then_inc(*banks.release(f"moe{t}{half}"))
                    dve.wait_ge(*banks.emptied(f"moe{t}{half}"))
            dve.nop().then_inc(*R.mark("x2"))
            dve_rms(5, D, T)
            for c in range(DC):
                ins = dve.scalar_tensor_tensor(out=xv[:, c, :], in0=xv[:, c, :], scalar=par("final_norm_g", c, 1), in1=rst[:, 0:T],
                                               op0=ALU.mult, op1=ALU.mult)
            ins.then_inc(*R.mark("final"))
            dve.wait_ge(*R.at("final"))
            for c in range(NC):
                rows = slice(64, 128) if c % 2 == 0 else slice(0, 64)
                ins = dve.memset(vu[rows, c, :], 0.0)
            ins.then_inc(*W.mark("vu_zero"))
            dve.memset(gn_eps[:], 64e-5)
            full = work[:, 0:2056].rearrange("p (c t) -> p c t", c=DC)
            link(dve.memset(full[:, :, 0:1], 0.0))
            xn, dx = full[:, :, 1:T + 1], chunks(w_["dx"], 8)
            dve_rms(6, D, T)
            for c in range(DC):
                ins = dve.scalar_tensor_tensor(out=xn[:, c, :], in0=xv[:, c, :], scalar=par("norm_pre_2", c, 1), in1=rst[:, 0:T],
                                               op0=ALU.mult, op1=ALU.mult)
            ins.then_inc(*W.mark("xn"))
            dve.wait_ge(*W.at("xn"))
            link(dve.tensor_tensor(dx, full[:, :, 0:T], xn, ALU.subtract))
            link(dve.tensor_scalar(one_ka[:], par("a_k_a_2"), -1.0, 1.0, ALU.mult, ALU.add))
            mix = [chunks(w_["mix"][:, 2048 * i:2048 * (i + 1)], 8) for i in range(2)]

            def blend(i, which, after=None):
                if after:
                    dve.wait_ge(weights_used, POST_TILE + after)
                for c in range(DC):
                    ins = dve.scalar_tensor_tensor(out=mix[i % 2][:, c, :], in0=dx[:, c, :], scalar=par("a_mu_2", 8 * which + c, 1),
                                                   in1=xn[:, c, :], op0=ALU.mult, op1=ALU.add)
                ins.then_inc(*W.mark(f"mix{i}"))

            blend(0, 4)
            blend(1, 5)
            dve.wait_ge(*banks.ready("lora0"))
            blend(2, 0)
            dve.wait_ge(*banks.ready("lora1"))
            blend(3, 1)
            L, lw, kk = ar["cum"], w_["lw"], ar["kk"]
            dve.wait_ge(*X.at("sigw"))
            link(dve.tensor_scalar(lw, lw, -0.6065306597126334, None, ALU.mult))
            link(dve.memset(ar["e2"], 1.0))
            link(dve.memset(ar["e2"].rearrange("p (c s) -> p c s", s=C)[:, :, 0:1], 0.0))
            link(dve.tensor_tensor_scan(out=L, data0=ar["e2"], data1=lw, initial=0.0, op0=ALU.mult, op1=ALU.add))
            blend(4, 2, 3)
            rr, kk_, aa = chunks(w_["r"], 8), chunks(w_["k"], 8), chunks(ar["a"], 8)
            dve.wait_ge(*X.at("k"))
            dve.wait_ge(*X.at("siga"))
            kkr = chunks(ar["e2"], 8)
            for c in range(DC):
                ins = dve.tensor_scalar(kkr[:, c, :], kk_[:, c, :], par("a_k_k_2", c, 1), None, ALU.mult)
            link(ins)
            dve.tensor_tensor(ar["e1"], ar["e2"], ar["e2"], ALU.mult).then_inc(*W.mark("kk_sq"))
            ta = chunks(ar["kk"], 8)
            for c in range(DC):
                ins = dve.tensor_scalar(ta[:, c, :], aa[:, c, :], par("a_k_a_2", c, 1), one_ka[:, c:c + 1], ALU.mult, ALU.add)
            link(ins)
            link(dve.tensor_tensor(w_["k"], w_["k"], ar["kk"], ALU.mult))
            dve.wait_ge(*X.at("r"))
            for c in range(DC):
                ins = dve.scalar_tensor_tensor(out=chunks(ar["e3"], 8)[:, c, :], in0=rr[:, c, :], scalar=par("a_r_k_2", c, 1), in1=kk_[:, c, :],
                                               op0=ALU.mult, op1=ALU.mult)
            ins.then_inc(*W.mark("bonus_in"))
            blend(5, 3, 5)
            dve.wait_ge(*X.at("kk_norm"))
            link(dve.tensor_scalar(kk, kk, 1e-12, None, ALU.max))
            link(dve.reciprocal(kk, kk))
            link(dve.tensor_tensor(kk, kk, ar["e2"], ALU.mult))
            link(dve.tensor_tensor(ar["a"], ar["a"], kk, ALU.mult))
            for i in range(4):
                dve.wait_ge(*banks.ready(f"bonus{i}"))
                dve.tensor_copy(w_["dx"][:, 512 * i:512 * (i + 1)], banks[f"bonus{i}"][:, :]).then_inc(*banks.release(f"bonus{i}"))
            dve.tensor_tensor(ar["e3"], L, lw, ALU.subtract).then_inc(*W.mark("args"))
            dve.wait_ge(*X.at("exp"))
            four = lambda ap: ap.rearrange("p (h c s) -> p h c s", h=HP, c=NC)
            two = lambda ap, e: ap.rearrange("p (h c e s) -> p h c e s", h=HP, c=2, e=2)[:, :, :, e, :]
            kb2 = work[:, 0:4096].rearrange("p (h c e k s) -> p h c e k s", h=HP, c=2, e=2, k=2)
            dve.tensor_copy(pc[:].rearrange("p (h c) -> p h c", h=HP), four(ar["e1"])[:, :, :, C - 1])
            dve.wait_ge(weights_used, POST_TILE + 9)
            dve.tensor_tensor(kr[:, :, :, 0, :], four(kk), four(ar["e3"]), ALU.mult)
            ins = dve.tensor_tensor(kr[:, :, :, 1, :], four(w_["r"]), four(ar["e1"]), ALU.mult)
            link(ins)
            link(dve.tensor_copy(w_["r"], w_["dx"]))
            for e in range(2):
                dve.tensor_tensor(kb2[:, :, :, e, e, :], two(w_["k"], e), two(ar["e2"], e), ALU.mult)
                ins = dve.tensor_tensor(kb2[:, :, :, e, 1 - e, :], two(ar["a"], e), two(ar["e2"], e), ALU.mult)
            link(ins)
            dve.tensor_copy(w_["k"], w_["r"]).then_inc(*W.mark("kb"))
            for half in range(2):
                for c in range(NC):
                    for hd in range(2):
                        name = f"sc{half}{c}{hd}"
                        dve.wait_ge(*banks.ready(name))
                        out = sc_[:, 8 * half:8 * half + 8, c, :].rearrange("p (j e) n -> p j e n", e=2)[:, :, hd, :]
                        dve.tensor_tensor(out, chunks(banks[name][:, :], 4),
                                          con(("rwkv_even", "rwkv_odd")[c % 2]).unsqueeze(1).to_broadcast([P, 4, P]), ALU.mult)\
                           .then_inc(*banks.release(name))
            for half in range(2):
                for c in range(NC):
                    for hd in range(2):
                        dve.wait_ge(*banks.emptied(f"sc{half}{c}{hd}"))
            for q in range(2):
                if q:
                    for h4 in range(4):
                        dve.wait_ge(*banks.emptied(f"inv0_5_{h4}"))
                link(dve.memset(xmt[0:64, :, 64:128], 0.0))
                link(dve.memset(xmt[64:128, :, 0:64], 0.0))
                link(dve.tensor_copy(xmt[0:64, :, 0:64], sc_[0:64, :, 2 * q + 1, 0:64]))
                link(dve.tensor_copy(xmt[64:128, :, 64:128], sc_[64:128, :, 2 * q, 0:64]))
                dve.tensor_tensor(inv, xmt, ident.unsqueeze(1).to_broadcast([P, 16, P]), ALU.add).then_inc(*W.mark(f"xmt{q}"))
                dve.wait_ge(*W.at(f"xmt{q}"))
                for level in range(1, 6):
                    if level < 5:
                        for h4 in range(4):
                            dve.wait_ge(*banks.ready(f"xt{q}_{level}_{h4}"))
                            dve.tensor_copy(xmt[:, 4 * h4:4 * h4 + 4, :], chunks(banks[f"xt{q}_{level}_{h4}"][:, :], 4))\
                               .then_inc(*banks.release(f"xt{q}_{level}_{h4}"))
                    for h4 in range(4):
                        dve.wait_ge(*banks.ready(f"inv{q}_{level}_{h4}"))
                        block_ = inv[:, 4 * h4:4 * h4 + 4, :]
                        dve.tensor_tensor(block_, block_, chunks(banks[f"inv{q}_{level}_{h4}"][:, :], 4), ALU.add)\
                           .then_inc(*banks.release(f"inv{q}_{level}_{h4}"))
                for h4 in range(4):
                    dve.wait_ge(*banks.emptied(f"inv{q}_5_{h4}"))
                dve.tensor_copy(sc_[0:64, :, 2 * q + 1, 0:64], inv[0:64, :, 0:64])
                link(dve.tensor_copy(sc_[64:128, :, 2 * q, 0:64], inv[64:128, :, 64:128]))
            dve.memset(state, 0.0).then_inc(*W.mark("placed"))
            dve.wait_ge(*W.at("placed"))
            pcv = pc[:].rearrange("p (h c) -> p h c", h=HP)
            for c in range(NC):
                rows = slice(64, 128) if c % 2 == 0 else slice(0, 64)
                dve.wait_ge(*banks.ready(f"w{c}0"))
                dve.tensor_copy(wsb[rows, 0:512], banks[f"w{c}0"][rows, :]).then_inc(*banks.release(f"w{c}0"))
                dve.wait_ge(*banks.ready(f"u{c}0"))
                dve.tensor_copy(vu[rows, c, 0:512], banks[f"u{c}0"][rows, :]).then_inc(*banks.release(f"u{c}0"))
                if c < NC - 1:
                    dve.wait_ge(*banks.ready(f"yr{c}"))
                    for half in range(2):
                        for hd in range(2):
                            r = slice(64 * hd, 64 * hd + 64)
                            st = state[r, 4 * half:4 * half + 4, 64 * hd:64 * hd + 64]
                            new = chunks(banks[f"ds{c}{half}"][r, :], 4)[:, :, 64 * hd:64 * hd + 64]
                            ins = dve.tensor_tensor(st, st, new, ALU.add)
                            if hd == 0:
                                link(ins)
                        ins.then_inc(*banks.release(f"ds{c}{half}"))
                        dve.wait_ge(*banks.emptied(f"ds{c}{half}"))
                    for hd in range(2):
                        r = slice(64 * hd, 64 * hd + 64)
                        st = state[r, :, 64 * hd:64 * hd + 64]
                        ins = dve.tensor_tensor(st, st, pcv[r, :, c].unsqueeze(2).to_broadcast([64, HP, 64]), ALU.mult)
                    ins.then_inc(*W.mark(f"st{c}"))
                    dve.wait_ge(*W.at(f"st{c}"))
            dve.nop().then_inc(*W.mark(f"st{NC - 1}"))
            bonus = w_["k"]
            vt = w_["r"]
            for c in range(NC):
                dve.wait_ge(*banks.ready(f"vt{c}"))
                part = slice(c * C, (c + 1) * C)
                dve.tensor_tensor(chunks(vt, 8)[:, :, part], chunks(banks[f"vt{c}"][:, :], 8), chunks(bonus, 8)[:, :, part], ALU.mult)\
                   .then_inc(*banks.release(f"vt{c}"))
            yv = w_["lw"]
            for i in range(4):
                part = slice(512 * i, 512 * (i + 1))
                dve.wait_ge(*banks.ready(f"gmean{i}"))
                dve.scalar_tensor_tensor(out=tmp[0][:, part], in0=banks[f"gmean{i}"][:, :], scalar=-1.0 / 64, in1=yv[:, part],
                                         op0=ALU.mult, op1=ALU.add).then_inc(*banks.release(f"gmean{i}"))
            dve.wait_ge(*banks.emptied("gmean3"))
            dve.nop().then_inc(*W.mark("centred"))
            for i in range(4):
                dve.wait_ge(*banks.emptied(f"gvar{i}"))
            link(dve.reciprocal(tmp[2], tmp[2]))
            link(dve.tensor_tensor(tmp[0], tmp[0], tmp[2], ALU.mult))
            for c in range(DC):
                part = slice(c * T, (c + 1) * T)
                ins = dve.tensor_scalar(tmp[0][:, part], tmp[0][:, part], par("a_lnx_g_2", c, 1), par("a_lnx_b_2", c, 1), ALU.mult, ALU.add)
            link(ins)
            link(dve.tensor_tensor(tmp[0], tmp[0], vt, ALU.add))
            dve.wait_ge(*X.at("g"))
            dve.tensor_tensor(yv, tmp[0], w_["g"], ALU.mult).then_inc(*W.mark("y"))

            def add_normed(k, buf, gain, at):
                dve_rms(k, D, T)
                link(dve.tensor_tensor(chunks(buf, 8), chunks(buf, 8), rst[:, 0:T].unsqueeze(1).to_broadcast([P, DC, T]), ALU.mult))
                for c in range(DC):
                    ins = dve.scalar_tensor_tensor(out=xv[:, c, :], in0=buf[:, c * T:(c + 1) * T], scalar=par(gain, at + c, 1),
                                                   in1=xv[:, c, :], op0=ALU.mult, op1=ALU.add)
                return ins

            add_normed(7, tmp[0], "norm_post_2", 0).then_inc(*W.mark("attn_in"))
            dve.wait_ge(*W.at("attn_in"))
            lam = par("b_lambda_2").rearrange("p (a b n) -> p a b n", a=2, b=2)
            link(dve.tensor_tensor(chunks(z["lp"], 2), lam[:, :, 0, :], lam[:, :, 1, :], ALU.mult))
            dve.memset(z["eps"], 1e-5)
            dve.tensor_scalar(z["sub"], par("b_subln_2"), 1.0 - lam_init, None, ALU.mult)
            m3 = chunks(z["mask3"], 3)
            dve.memset(m3[:, 1, :], 0.0)
            dve.tensor_copy(m3[:, 0, :], con("causal"))
            link(dve.tensor_copy(m3[:, 2, :], con("causal")))

            def lam_sum():
                dve.tensor_reduce(z["ls"], chunks(z["lp"], 2), AX.X, ALU.add).then_inc(*Y.mark("lam_sum"))

            def ple(l, mark):
                for i in range(4):
                    dve.wait_ge(*banks.emptied(f"pe{l}_{i}"))
                    dve.wait_ge(*banks.emptied(f"pg{l}_{i}"))
                dve.tensor_tensor(z["gb"], z["gb"], z["eb"], ALU.mult).then_inc(*Y.mark(f"ge{l}"))
                add_normed((8, 11)[l], z["gb"], "ple_norm_2", 8 * l).then_inc(*Y.mark(mark))
                dve.wait_ge(*Y.at(mark))

            lam_sum()
            dve.wait_ge(*Z.at("lam_exp"))
            link(dve.tensor_tensor(z["nlam"], z["le"][:, 1:2], z["le"][:, 0:1], ALU.subtract))
            link(dve.tensor_scalar(z["nlam"], z["nlam"], -lam_init, None, ALU.add))
            ple(0, "x3")
            dve_rms(9, D, T)
            for name, gain, at in (("hkv", "kv_norm_2", 0), ("hq", "norm_pre_2", 8)):
                for c in range(DC):
                    ins = dve.scalar_tensor_tensor(out=z[name][:, c * T:(c + 1) * T], in0=xv[:, c, :], scalar=par(gain, at + c, 1),
                                                   in1=rst[:, 0:T], op0=ALU.mult, op1=ALU.mult)
                ins.then_inc(*Y.mark(name))
            for name, banks_of, ready in (("kt", "kr", "k"), ("qt", "qr", "q")):
                dve.wait_ge(*Z.at(ready))
                for i in range(4):
                    dve.wait_ge(*banks.ready(f"{banks_of}{i}"))
                    dve.tensor_tensor(chunks(z["eb"], 8)[:, 2 * i:2 * i + 2, :], chunks(banks[f"{banks_of}{i}"][:, :], 2),
                                      con("sin").unsqueeze(1).to_broadcast([P, 2, T]), ALU.mult).then_inc(*banks.release(f"{banks_of}{i}"))
                link(dve.tensor_tensor(chunks(z[name], 8), chunks(z[name], 8), con("cos").unsqueeze(1).to_broadcast([P, 8, T]), ALU.mult))
                for i in range(4):
                    dve.wait_ge(*banks.emptied(f"{banks_of}{i}"))
                dve.tensor_tensor(z[name], z[name], z["eb"], ALU.add).then_inc(*Y.mark(name))
                dve.wait_ge(*Y.at(name))

            def combine(hh):
                dve.wait_ge(*Z.at(f"dx{hh}"))
                link(dve.reciprocal(z["rs"][:, 4 * hh:4 * hh + 4], z["sums"][:, 4 * hh:4 * hh + 4]))
                link(dve.tensor_scalar(z["rs"][:, 4 * hh + 2:4 * hh + 4], z["rs"][:, 4 * hh + 2:4 * hh + 4], z["nlam"], None, ALU.mult))
                spans = ((0, P), (P, 3 * P))
                for q, (lo, hi) in enumerate(spans):
                    ins = dve.tensor_scalar(dprob[:, hh, 1, lo:hi], dprob[:, hh, 1, lo:hi], z["rs"][:, 4 * hh + 2 + q:4 * hh + 3 + q], None, ALU.mult)
                link(ins)
                for q, (lo, hi) in enumerate(spans):
                    ins = dve.scalar_tensor_tensor(out=dprob[:, hh, 0, lo:hi], in0=dprob[:, hh, 0, lo:hi],
                                                   scalar=z["rs"][:, 4 * hh + q:4 * hh + q + 1], in1=dprob[:, hh, 1, lo:hi],
                                                   op0=ALU.mult, op1=ALU.add)
                return ins

            def turned(hh):
                dve.wait_ge(*banks.ready(f"at{hh}"))
                dve.tensor_copy(dat[:, hh, :], banks[f"at{hh}"][:, 0:3 * P]).then_inc(*banks.release(f"at{hh}"))

            for hh in range(8):
                for c in range(2):
                    dve.wait_ge(*banks.ready(f"d{hh}{c}"))
                    dve.tensor_tensor(dprob[:, hh, c, :], banks[f"d{hh}{c}"][:, 0:3 * P], z["mask3"], ALU.add)\
                       .then_inc(*banks.release(f"d{hh}{c}"))
                for c in range(2):
                    dve.wait_ge(*banks.emptied(f"d{hh}{c}"))
                    for q, (lo, hi) in enumerate(((0, P), (P, 3 * P))):
                        i = 4 * hh + 2 * c + q
                        ins = dve.reduce_max(z["mx"][:, i:i + 1], dprob[:, hh, c, lo:hi], AX.X)
                link(ins)
                dve.tensor_scalar(z["nmx"][:, 4 * hh:4 * hh + 4], z["mx"][:, 4 * hh:4 * hh + 4], -1.0, None, ALU.mult).then_inc(*Y.mark(f"ds{hh}"))
                if hh:
                    combine(hh - 1).then_inc(*Y.mark(f"da{hh - 1}"))
                if hh > 1:
                    turned(hh - 2)
            combine(7).then_inc(*Y.mark("da7"))
            turned(6)
            turned(7)
            dve.wait_ge(*Z.at("o_norm"))
            link(dve.reciprocal(z["eb"], z["eb"]))
            link(dve.tensor_tensor(z["ot"], z["ot"], z["eb"], ALU.mult))
            dve.wait_ge(*Z.at("gate"))
            dve.scalar_tensor_tensor(out=z["ot"], in0=z["ot"], scalar=z["sub"], in1=z["gate"], op0=ALU.mult, op1=ALU.mult).then_inc(*Y.mark("o"))
            add_normed(10, z["gb"], "norm_post_2", 8).then_inc(*Y.mark("x4"))
            dve.wait_ge(*Y.at("x4"))
            ple(1, "x5")

        @block.gpsimd
        def _(pool):
            pool.wait_ge(*V.at("h2"))
            pool.memset(mo["yg"], 0.0).then_inc(yg_zero, 1)
            pool.wait_ge(*R.at("lists"))
            pool.wait_ge(list_cleared, 16)
            for i in range(TOP * TT):
                pool.indirect_dma_start(out=a["list"], out_offset=bass.IndirectOffsetOnAxis(ap=list_at[:, i:i + 1], axis=0),
                                        in_=token_id[:, i % TT:i % TT + 1], in_offset=None).then_inc(list_scattered, 16)

            def gather(block_, p_, done):
                pool.indirect_dma_start(out=xg[p_], out_offset=None, in_=a["hrow"],
                                        in_offset=bass.IndirectOffsetOnAxis(ap=gather_at[:, block_:block_ + 1], axis=0))\
                    .then_inc(done, 16)

            pool.wait_ge(*R.at("gather_at"))
            pool.wait_ge(h_stored, 16)
            for e in range(EXPERTS):
                if e >= 2:
                    pool.wait_ge(xt_done, e - 1)
                gather(e, e % 2, gathered[e % 2])
            for p_ in range(2):
                pool.wait_ge(y_stored[p_], 16 * EXPERTS)
            spare = pool.value_load(info[0:1, 0:1], min_val=0, max_val=SPARE)
            with pool.If(spare > 0):
                for j in range(SPARE):
                    if j:
                        pool.wait_ge(spare_stored, 32 * j)
                    gather(EXPERTS + j, 0, spare_gathered)
                pool.wait_ge(spare_stored, 32 * SPARE)
            pool.wait_ge(yrow_cleared, 16)
            for t in range(TT):
                for k in range(TOP):
                    out = mo["yg"][:, (k * TT + t) * D:(k * TT + t + 1) * D]
                    pool.indirect_dma_start(out=out, out_offset=None, in_=a["yrow"],
                                            in_offset=bass.IndirectOffsetOnAxis(ap=row_at[:, k * TT + t:k * TT + t + 1], axis=0))\
                        .then_inc(rows_gathered[t], 16)

        @block.sync
        def _(sp):
            sp.dma_start(prm[:], a["params"]).then_inc(params_loaded, 16)
            sp.dma_start(cst[:], a["tables"]).then_inc(params_loaded, 16)
            sp.dma_start(xt[:], a["x"]).then_inc(x_loaded, 16)
            for n, (name, parts) in enumerate(tiles):
                if n >= RING:
                    sp.wait_ge(weights_used, n - RING + 1)
                for at, pitch, view in parts:
                    width = view.shape[2]
                    dst = ring[:, slot_of[name] * SLOT:slot_of[name] * SLOT + pitch * DC].rearrange("p (c n) -> p c n", c=DC)[:, :, at:at + width]
                    sp.dma_start(dst, view).then_inc(slot_loaded[slot_of[name]], 16)
            sp.wait_ge(*R.at("ids"))
            list_rows = a["list"].rearrange("(s b) o -> s (b o)", b=LIST)
            sp.dma_start(list_rows, zero_list[0:SLOTS, :]).then_inc(list_cleared, 16)
            sp.wait_ge(yg_zero, 1)
            spare_rows = a["yrow"].rearrange("(b p) n -> b (p n)", p=SLOTS)[EXPERTS:EXPERTS + SPARE].rearrange("b (q n) -> q b n", q=P)
            sp.dma_start(spare_rows, mo["yg"][:, 0:SPARE * 512].rearrange("p (b n) -> p b n", b=SPARE)).then_inc(yrow_cleared, 16)

            def load_expert(e, p_):
                for k, name in enumerate(("w_gate", "w_up", "w_down")):
                    dst = ring[:, expert_slots[p_][k] * SLOT:(expert_slots[p_][k] + 1) * SLOT]
                    sp.wait_ge(weights_used, 3 * e + (MOE_TILE + k - RING + 1))
                    load_matrix(name, e, dst, slot_loaded[expert_slots[p_][k]])

            def load_matrix(name, e, dst, done):
                w = a[name][0][bass.ds(e, 1)].rearrange("e (c p) n -> p (e c) n", p=P)
                sp.dma_start(dst.rearrange("p (c n) -> p c n", n=w.shape[2]), w).then_inc(done, 16)

            def store_rows(e, p_, done):
                rows = a["yrow"].rearrange("(b s) n -> b s n", s=SLOTS)[bass.ds(e, 1)].rearrange("b s n -> (b s) n")
                for half in range(2):
                    sp.dma_start(rows[:, half * 512:(half + 1) * 512], ys[p_][64 * half:64 * half + 64, :]).then_inc(done, 16)

            for p_ in range(2):
                load_expert(p_, p_)
            for t in range(TT):
                for half in range(2):
                    sp.wait_ge(*banks.emptied(f"hrow{t}{half}"))
            sp.dma_start(a["hrow"].rearrange("(t p two) n -> p t (two n)", t=TT, two=2), chunks(m["conv"], 2)).then_inc(h_stored, 16)
            sp.wait_ge(list_scattered, 16 * TOP * TT)
            for half in range(2):
                sp.dma_start(list_in[64 * half:64 * half + 64, :], list_rows).then_inc(list_loaded, 16)
            with sp.Fori(0, EXPERTS // 2 - 1) as i:
                for p_ in range(2):
                    load_expert(2 * i + 2 + p_, p_)
                    sp.wait_ge(y_copied, 2 * i + p_ + 1)
                    store_rows(2 * i + p_, p_, y_stored[p_])
            for p_ in range(2):
                sp.wait_ge(y_copied, EXPERTS - 1 + p_)
                store_rows(EXPERTS - 2 + p_, p_, y_stored[p_])
            for p_ in range(2):
                sp.wait_ge(y_stored[p_], 16 * EXPERTS)
            sp.wait_ge(*R.at("info"))
            spare = sp.value_load(info[0:1, 0:1], min_val=0, max_val=SPARE)
            with sp.If(spare > 0):
                sp.wait_ge(yrow_cleared, 16)
                sp.wait_ge(weights_used, MOE_TILE + 3 * EXPERTS)
                for j in range(SPARE):
                    if j:
                        sp.wait_ge(spare_used, 3 * j)
                    owner = sp.value_load(info[0:1, 1 + j:2 + j], min_val=0, max_val=EXPERTS - 1)
                    for k, name in enumerate(("w_gate", "w_up", "w_down")):
                        load_matrix(name, owner, ring[:, (3 + k) * SLOT:(4 + k) * SLOT], spare_loaded)
                    sp.wait_ge(y_copied, EXPERTS + j + 1)
                    store_rows(EXPERTS + j, 0, spare_stored)
                sp.wait_ge(spare_stored, 32 * SPARE)
            for n, (name, parts) in enumerate(post):
                if name == "ple_w0":
                    sp.wait_ge(*W.at("centred"))
                    sp.dma_start(z["pt"], a["p"]).then_inc(pt_loaded, 16)
                sp.wait_ge(weights_used, POST_TILE + n - 2)
                for at, size, rows, c, view in parts:
                    base = slot_of[name] * SLOT + at
                    dst = ring[0:rows, base:base + size].rearrange("p (c n) -> p c n", c=c)
                    sp.dma_start(dst, view).then_inc(slot_loaded[slot_of[name]], 16)
            sp.wait_ge(*Y.at("x5"))
            sp.dma_start(a["out"], xt[:]).then_inc(out_written, 16)
            sp.wait_ge(out_written, 16)


def tables():
    p, q = np.arange(P)[:, None], np.arange(P)[None, :]
    t = {}
    t["ident"] = p == q
    t["tri"] = p <= q
    t["tri_strict"] = p < q
    t["ones"] = np.ones((P, P))
    t["block_ones"] = (p // 64) == (q // 64)
    mask = np.where(q < 64, (p % 64) < (q % 64), (p % 64) <= (q % 64))
    t["rwkv_even"] = mask * np.where(p < 64, 1.0, -1.0)
    t["rwkv_odd"] = mask * np.where(p < 64, -1.0, 1.0)
    t["causal"] = np.where(q <= p, 0.0, -1e30)
    rot = np.zeros((P, P))
    for i in range(P):
        if i % 64 < 8:
            rot[i + 8, i] = -1.0
        elif i % 64 < 16:
            rot[i - 8, i] = 1.0
    t["rot"] = rot
    inv = (np.float32(500000.0) ** (-np.arange(0, 16, 2, dtype=np.float32) / np.float32(16))).astype(np.float32)
    ang = (np.arange(T, dtype=np.float32)[None, :] * inv[np.arange(P) % 8][:, None]).astype(np.float32)
    turned = (p % 64) < 16
    t["cos"] = np.where(turned, np.cos(ang), 1.0)
    t["sin"] = np.where(turned, np.sin(ang), 0.0)
    t["iota"] = np.broadcast_to(np.arange(32)[None, :], (P, 32))
    t["token"] = p + P * np.arange(2)[None, :]
    t["half"] = p // 64
    t["sign_even"] = np.where(p < 64, 1.0, -1.0)
    t["sign_odd"] = np.where(p < 64, -1.0, 1.0)
    return np.ascontiguousarray(np.concatenate([np.asarray(t[n], np.float32) for n, _ in CONST], 1))


def parameters(i):
    def col(a):
        a = a.reshape(-1, P)
        return a.T

    def taps(w):
        k, n = w.shape
        return w.reshape(k, n // P, P).transpose(2, 1, 0).reshape(P, -1)

    def row(a):
        return np.broadcast_to(a.reshape(1, -1), (P, a.size))

    one = {"ssd_conv_w": taps(i["ssd_conv_w"][0]), "cm_conv_w": taps(i["cm_conv_w"][0]),
           "ssd_d": col(np.repeat(i["ssd_d"][0], 64)),
           "ssd_dt_bias": row(i["ssd_dt_bias"]), "ssd_a_log": row(i["ssd_a_log"]), "fox_f_bias": row(i["fox_f_bias"]),
           "b_router": row(np.concatenate([i["b_router_group"][0], i["b_router_expert"][0]])),
           "b_lambda_2": row(i["b_lambda_2"])}
    return np.ascontiguousarray(np.concatenate([one[n] if n in one else col(i[n]) for n, _ in PARAM], 1))


def transposed(x):
    return np.ascontiguousarray(x.reshape(T, -1, P).transpose(2, 1, 0).reshape(P, -1))


WEIGHTS = ["ada_w", "w_in", "w_out", "w_router_group", "w_router_expert", "w_gate", "w_up", "w_down",
           "a_w_in_2", "a_w1_2", "a_w2_2", "a_a1_2", "a_a2_2", "a_w_out_2", "kv_w_2", "b_w_in_2", "b_w_out_2",
           "ple_w_2", "ple_gate_2"]


def scratch(nc):
    return {"list": nc.dram_tensor("list_scratch", (SLOTS * LIST, 1), I32).ap(),
            "hrow": nc.dram_tensor("hrow_scratch", (2 * T, D // 2), F32).ap(),
            "yrow": nc.dram_tensor("yrow_scratch", ((EXPERTS + SPARE) * SLOTS, D), F32).ap()}


def kernel(**inputs):
    import concourse.bacc as _bacc
    from concourse.bass_utils import run_bass_kernel_spmd as _run

    i = {n: np.asarray(v) for n, v in inputs.items()}
    nc = _bacc.Bacc("TRN2", target_bir_lowering=False, num_devices=1)
    given = {"params": parameters(i), "tables": tables(), "x": transposed(i["x"][0]),
             "p": np.concatenate([transposed(i["p_2"][0, 0]), transposed(i["p_2"][1, 0])], 1)}
    given.update({n: np.ascontiguousarray(i[n]) for n in WEIGHTS})
    a = {n: nc.dram_tensor(f"in_{n}", v.shape, F32, kind="ExternalInput").ap() for n, v in given.items()}
    a["out"] = nc.dram_tensor("out_x", (P, DC * T), F32, kind="ExternalOutput").ap()
    a.update(scratch(nc))
    program(nc, a)
    r = _run(nc, [{f"in_{n}": v for n, v in given.items()}], core_ids=[0])
    return np.ascontiguousarray(r.results[0]["out_x"].reshape(P, DC, T).transpose(2, 1, 0).reshape(1, T, D))
```

```python
from contextlib import ExitStack

import numpy as np

import concourse.bass as bass
from concourse import mybir

F32 = mybir.dt.float32
I32 = mybir.dt.int32
U32 = mybir.dt.uint32
ALU = mybir.AluOpType
ACT = mybir.ActivationFunctionType
AX = mybir.AxisListType

P = 128
T = 256
TT = T // P
D = 1024
DC = D // P
SLOT = 8 * 512
RING = 6
EPS = 1e-6
EXPERTS, TOP = 32, 2
SLOTS = 64
SPARE = (TOP * T - 1) // (SLOTS + 1)
LIST = 40

PARAM = [("c", 8), ("ada_b", 48), ("norm_mix_g", 8), ("ssd_conv_w", 32), ("ssd_conv_b", 8),
         ("ssd_norm_g", 4), ("ssd_d", 4), ("fox_norm_g", 2), ("cm_conv_w", 62), ("cm_conv_b", 2),
         ("cm_ln_g", 2), ("cm_ln_b", 2), ("norm_ffn_g", 8), ("final_norm_g", 8),
         ("norm_pre_2", 16), ("norm_post_2", 16), ("a_mu_2", 48), ("a_w0_2", 8), ("a_a0_2", 8),
         ("a_k_k_2", 8), ("a_k_a_2", 8), ("a_r_k_2", 8), ("a_lnx_g_2", 8), ("a_lnx_b_2", 8),
         ("kv_norm_2", 8), ("b_subln_2", 1), ("ple_norm_2", 16),
         ("ssd_dt_bias", 8), ("ssd_a_log", 8), ("fox_f_bias", 4), ("b_router", 36), ("b_lambda_2", 256)]
CONST = [("ident", 128), ("tri", 128), ("tri_strict", 128), ("ones", 128), ("block_ones", 128),
         ("rwkv_even", 128), ("rwkv_odd", 128), ("causal", 128), ("rot", 128),
         ("cos", 256), ("sin", 256), ("iota", 32), ("token", 2), ("half", 1), ("sign_even", 1), ("sign_odd", 1), ("eps", 1),
         ("slot_no", 128), ("block_no", LIST)]


def offsets(table):
    at, out = 0, {}
    for name, n in table:
        out[name] = (at, at + n)
        at += n
    return out, at


PAT, NPARAM = offsets(PARAM)
CAT, NCONST = offsets(CONST)


class Marks:

    def __init__(self, sem, *names):
        self.sem, self.value, self.next = sem, {n: i + 1 for i, n in enumerate(names)}, 0
        assert len(self.value) == len(names)

    def mark(self, name):
        self.next += 1
        assert self.value[name] == self.next, (name, self.value[name], self.next)
        return self.sem, 1

    def at(self, name):
        return self.sem, self.value[name]


class Chain:

    def __init__(self, sem):
        self.sem, self.n = sem, 0

    def step(self, ins):
        ins.then_inc(self.sem, 1)
        self.n += 1
        return self.n

    def link(self, eng, ins):
        eng.wait_ge(self.sem, self.step(ins))


class Banks:

    def __init__(self, tensors, full, free):
        self.tensors, self.full, self.free = tensors, full, free
        self.uses, self.count, self.where = 0, [0] * len(tensors), {}

    def open(self, pe, name):
        b = self.uses % len(self.tensors)
        if self.count[b]:
            pe.wait_ge(self.free[b], self.count[b])
        self.count[b] += 1
        self.uses += 1
        assert name not in self.where, name
        self.where[name] = (b, self.uses, self.count[b])
        return self.tensors[b]

    def __getitem__(self, name):
        return self.tensors[self.where[name][0]]

    def filled(self):
        return self.full, 1

    def ready(self, name):
        return self.full, self.where[name][1]

    def release(self, name):
        return self.free[self.where[name][0]], 1

    def emptied(self, name):
        return self.free[self.where[name][0]], self.where[name][2]


def mixer_weight_tiles(w_in):
    return [[(0, 512, 512)], [(0, 1024, 512)], [(0, 2056, 260), (260, 1536, 8)], [(0, 2316, 512)],
            [(0, 0, 512)], [(0, 1544, 512)]]


def program(nc, a):
    with ExitStack() as ctx:
        def sb(name, n, dt=F32, parts=P):
            return ctx.enter_context(nc.sbuf_tensor(name, [parts, n], dt))

        def sem(name):
            return ctx.enter_context(nc.semaphore(name))

        prm, cst = sb("prm", NPARAM), sb("cst", NCONST)
        xt = sb("xt", DC * T)
        ring = sb("ring", RING * SLOT)
        work_size = 21600
        work = sb("work", work_size)
        small = sb("small", 480)
        psum = [ctx.enter_context(nc.psum_tensor(f"bank{i}", [P, 512], F32)) for i in range(8)]

        def par(name, lo=0, n=None):
            s, e = PAT[name]
            return prm[:, s + lo:(s + lo + n if n is not None else e)]

        def con(name):
            s, e = CAT[name]
            return cst[:, s:e]

        ident, ones = con("ident"), con("ones")
        xv = xt[:].rearrange("p (c t) -> p c t", c=DC)

        def carve(sizes, tensor=work, at=0):
            out = {}
            for name, n in sizes:
                out[name] = tensor[:, at:at + n]
                at += n
            assert at <= tensor.shape[1], at
            return out

        def chunks(ap, c):
            return ap.rearrange("p (c t) -> p c t", c=c)

        params_loaded = sem("params_loaded")
        x_loaded = sem("x_loaded")
        slot_loaded = [sem(f"slot_loaded{s}") for s in range(RING)]
        weights_used = sem("weights_used")
        ada_summed = sem("ada_summed")
        ada_reduced = sem("ada_reduced")
        bank_full = sem("bank_full")
        bank_free = [sem(f"bank_free{b}") for b in range(7)]
        banks = Banks(psum[:7], bank_full, bank_free)
        mod_bank = psum[7]
        dve_steps, pool_steps = (Chain(sem(f"{n}_steps")) for n in ("dve", "pool"))
        rms_squares, rms_root, rms_ready = sem("rms_squares"), sem("rms_root"), sem("rms_ready")
        pe = nc.tensor
        act = nc.scalar
        dve = nc.vector

        def cols(w, c0, n, rows=D):
            return w.rearrange("(c p) n -> p c n", p=P)[:, :, c0:c0 + n]

        tiles = []

        def tile(name, *parts):
            tiles.append((name, parts))

        def ada(j):
            tile(f"ada{j}", (0, 512, cols(a["ada_w"][0], 512 * j, 512)))

        for j in range(4):
            ada(j)
        for j, pieces in enumerate(mixer_weight_tiles(None)):
            tile(f"win{j}", *[(o, 512 if len(pieces) == 1 else 268, cols(a["w_in"][0], c0, n)) for o, c0, n in pieces])
            ada(4 + j)
        ada(10)
        ada(11)
        for j in range(2):
            tile(f"wout{j}", (0, 512, cols(a["w_out"][0], 512 * j, 512)))
        tile("router", (0, 36, cols(a["w_router_group"][0], 0, 4)), (4, 36, cols(a["w_router_expert"][0], 0, 32)))
        MOE_TILE = len(tiles)
        assert MOE_TILE % 3 == 0
        slot_of, loaded_at = {}, {}
        total = [0] * RING
        for n, (name, parts) in enumerate(tiles):
            slot_of[name] = n % RING
            total[n % RING] += 16 * len(parts)
            loaded_at[name] = (slot_loaded[n % RING], total[n % RING])

        is_ada = [name.startswith("ada") for name, _ in tiles]
        ADA = sum(is_ada)
        ADA_DVE = 6
        MOE_USED = MOE_TILE - ADA

        def tile_used(n):
            count = sum(f == is_ada[n] for f in is_ada[:n + 1])
            return (ada_summed if is_ada[n] else weights_used), count

        def slot(s, pitch=512, at=0, c=DC):
            return ring[:, s * SLOT + at:s * SLOT + at + pitch * c].rearrange("p (c n) -> p c n", c=c)

        m = carve([("h", 2048), ("xbc", 2072), ("conv", 2048), ("sq", 2048), ("e", 536), ("u", 572),
                   ("sg", 512), ("zs", 1024), ("qk", 1024), ("xdt", 1024), ("xde", 512), ("brow", 256),
                   ("cexp", 1024), ("cb", 512), ("st", 512), ("p", 1536), ("y", 2048),
                   ("lnx", 512), ("ada0", 512), ("ada1", 512)])
        m["decay"] = m["sq"]
        h, conv, sq = chunks(m["h"], 8), chunks(m["conv"], 8), chunks(m["sq"], 8)
        xbc = m["xbc"].rearrange("p (c t) -> p c t", c=8)
        ebuf = chunks(m["e"], 2)
        u = m["u"].rearrange("p (c t) -> p c t", c=2)
        zq = work[:, 2048 + 2072 + 2048 + 2048 + 536 + 572 + 512:][:, 0:2048].rearrange("p (c t) -> p c t", c=8)
        zs, qk, y = chunks(m["zs"], 4), chunks(m["qk"], 4), chunks(m["y"], 8)
        xdt = chunks(m["xdt"], 2)
        cb = m["cb"].rearrange("p (t g l) -> p t g l", t=2, g=2)
        decay = m["decay"].rearrange("p (t h l) -> p t h l", t=2, h=8)
        cexp = m["cexp"].rearrange("p (h l) -> p h l", h=8)
        prob = m["p"].rearrange("p (h k) -> p h k", h=4)
        ptr = m["xbc"][:, 0:1536].rearrange("p (h k) -> p h k", h=4)
        s = carve([("cond", 8), ("mod", 48), ("gmix", 8), ("spx", 24), ("spa", 24), ("spu", 24), ("spw", 24),
                   ("spl", 24), ("spd", 24), ("spr", 24), ("sp", 24), ("ea", 8), ("cumin", 24), ("nacs", 16), ("nq", 8),
                   ("dte", 8), ("mx", 16), ("sums", 8), ("rs", 8), ("spm", 24), ("gffn", 8), ("tdiff", 8), ("nmx", 8),
                   ], small)
        rst = sb("rst", 512)
        var = sb("var", 512)
        root = sb("root", 512)

        def pe_rms(k, chunks_of, n=T, weights=ones):
            before = sum(RMS_PARTS[:k])
            pe.wait_ge(rms_squares, before + 1)
            bank = banks.open(pe, f"rms{k}")
            for g, group in enumerate(chunks_of):
                for i, ap in enumerate(group):
                    if RMS_PARTS[k] == 2 and i == DC // 2:
                        pe.wait_ge(rms_squares, before + 2)
                    last = pe.matmul(bank[:, g * n:(g + 1) * n], weights, ap, start=(i == 0), stop=(i == len(group) - 1))
            last.then_inc(*banks.filled())

        RMS_COUNT = [D, D // 4, D // 4, D // 4] + [D] * 8
        RMS_PARTS = [2, 1, 1, 1] + [2] * 8

        def act_squares(out, src):
            for half in range(2):
                part = slice(half * D, (half + 1) * D)
                act.activation(out[:, part], src[:, part], ACT.Square).then_inc(rms_squares, 1)

        def dve_rms(k, width, used=None):
            if used:
                dve.wait_ge(*used)
            dve.wait_ge(rms_root, k + 1)
            dve.reciprocal(rst[:, 0:width], root[:, 0:width]).then_inc(rms_ready, 1)
            dve.wait_ge(rms_ready, k + 1)

        def act_rms(k, width):
            act.wait_ge(*banks.ready(f"rms{k}"))
            if k:
                act.wait_ge(rms_ready, k)
            act.activation(root[:, 0:width], banks[f"rms{k}"][:, 0:width], ACT.Sqrt, scale=1.0 / RMS_COUNT[k], bias=con("eps"))\
               .then_inc(*banks.release(f"rms{k}"))
            act.wait_ge(*banks.emptied(f"rms{k}"))
            act.nop().then_inc(rms_root, 1)

        def ada_sum(eng, steps, j):
            w, out = slot(slot_of[f"ada{j}"]), m[f"ada{j % 2}"]
            eng.wait_ge(*loaded_at[f"ada{j}"])
            if j >= 2:
                eng.wait_ge(ada_reduced, j - 1)
            if eng is dve:
                steps.link(eng, eng.tensor_scalar(out, w[:, 0, :], s["cond"][:, 0:1], None, ALU.mult))
                for c in range(1, DC):
                    ins = eng.scalar_tensor_tensor(out=out, in0=w[:, c, :], scalar=s["cond"][:, c:c + 1], in1=out,
                                                   op0=ALU.mult, op1=ALU.add)
                    if c < DC - 1:
                        steps.link(eng, ins)
            else:
                steps.link(eng, eng.tensor_tensor(w, w, s["cond"].unsqueeze(2).to_broadcast([P, DC, 512]), ALU.mult))
                for n in (4, 2):
                    steps.link(eng, eng.tensor_tensor(w[:, 0:n, :], w[:, 0:n, :], w[:, n:2 * n, :], ALU.add))
                ins = eng.tensor_tensor(out, w[:, 0, :], w[:, 1, :], ALU.add)
            ins.then_inc(ada_summed, 1)

        V = Marks(sem("dve_mixer"), "zeros", "h", "xconv", "spa", "cumin", "u_gated", "tdiff", "args",
                  "conv", "xde", "decay", "cexp", "scores", "probs", "y_gated", "ln_centred", "ln_norm",
                  "y_ssd", "y_fox", "x1", "h2")
        A = Marks(sem("act_mixer"), "cond", "ea", "spu", "silu_conv", "dte", "cexp", "decay",
                  "exp", "silu_ln")


        mo = carve([("xg0", 512), ("xg1", 512), ("xet0", 512), ("xet1", 512), ("sg0", 256), ("sg1", 256),
                    ("hid0", 256), ("hid1", 256), ("ht0", 256), ("ht1", 256), ("ys0", 512), ("ys1", 512),
                    ("yg", 4096), ("comb", 2048),
                    ("rl", 72), ("gm", 2), ("gd", 8), ("ge", 8), ("gs", 2), ("pg", 2), ("gt", 8), ("gi", 2), ("ohg", 8),
                    ("ep", 64), ("el", 16), ("m1", 2), ("ed", 16), ("et", 16), ("ei", 2), ("oh8", 32), ("el2", 16),
                    ("m2", 2), ("md", 2), ("e2", 2), ("w", 4), ("oh", 128), ("hit", 64), ("x", 32), ("incl", 32),
                    ("excl", 32), ("prod", 128), ("pos", 4), ("e", 4), ("ov", 4), ("q", 4), ("slot", 4), ("g0", 4),
                    ("blk", 4), ("row", 4), ("cmp", 224), ("info", 8), ("listf", 40), ("hot_slot", 512),
                    ("hot_block", 4 * LIST)], at=6168)
        row_at = sb("row_at", 4, U32)
        gather_at = sb("gather_at", LIST, U32)
        info = sb("info", 8, I32)
        xg, xet, sg_, hid, ht, ys = ([mo[f"{n}{p_}"] for p_ in range(2)] for n in ("xg", "xet", "sg", "hid", "ht", "ys"))
        R = Marks(sem("dve_routing"), "gd", "md", "hits", "lists", "gather_at", "info", "weights", "comb0", "comb1", "x2", "final")
        S = Marks(sem("act_routing"), "ge", "e2")
        h_stored = sem("h_stored")
        yg_zero, yrow_cleared = sem("yg_zero"), sem("yrow_cleared")
        gathered = [sem("gathered0"), sem("gathered1")]
        xt_done, xt_copied, gu_done, silu_done, hid_done = (sem(n) for n in ("xt_done", "xt_copied", "gu_done", "silu_done", "hid_done"))
        ht_done, ht_copied, y_done, y_copied = (sem(n) for n in ("ht_done", "ht_copied", "y_done", "y_copied"))
        y_stored = [sem("y_stored0"), sem("y_stored1")]
        spare_loaded, spare_used, spare_gathered, spare_stored = (sem(n) for n in ("spare_loaded", "spare_used", "spare_gathered", "spare_stored"))
        rows_gathered = [sem(f"rows_gathered{t}") for t in range(TT)]
        expert_slots = [[(MOE_TILE + 3 * p_ + k) % RING for k in range(3)] for p_ in range(2)]

        def expert_loop(eng, body):
            body(0, 0)
            body(1, 1)
            with eng.Fori(1, EXPERTS // 2) as i:
                body(2 * i, 0)
                body(2 * i + 1, 1)

        def spare_loop(eng, body):
            spare = eng.value_load(info[0:1, 0:1], min_val=0, max_val=SPARE)
            with eng.If(spare > 0):
                with eng.Fori(0, SPARE) as j:
                    body(j)


        moe_base = list(total)
        post, POST_USED = [], MOE_USED + 3 * EXPERTS

        def post_tile(name, *parts):
            n = len(post)
            post.append((name, parts))
            slot_of[name] = n % 3
            total[n % 3] += 16 * len(parts) + (16 * (EXPERTS // 2) if n < 3 else 0)
            loaded_at[name] = (slot_loaded[n % 3], total[n % 3])

        def square(name, w, n):
            for j in range(n):
                post_tile(f"{name}{j}", (0, SLOT, P, DC, cols(w, 512 * j, 512)))

        def ple_tiles(l):
            post_tile(f"ple_w{l}", (0, 2 * D, P, 2, a["ple_w_2"][l].rearrange("(c p) n -> p c n", p=P)))
            square(f"ple_gate{l}_", a["ple_gate_2"][l], 2)

        post_tile("lora", (0, 512, P, DC, cols(a["a_w1_2"][0], 0, 64)), (512, 512, P, DC, cols(a["a_a1_2"][0], 0, 64)),
                  (1024, D, 64, 1, a["a_w2_2"][0].unsqueeze(1)), (2048, D, 64, 1, a["a_a2_2"][0].unsqueeze(1)))
        for i, name in enumerate("rkvg"):
            square(f"rwkv_{name}", a["a_w_in_2"][0, i], 2)
        square("rwkv_out", a["a_w_out_2"][0], 2)
        ple_tiles(0)
        square("kv", a["kv_w_2"], 4)
        square("b_in", a["b_w_in_2"][0], 4)
        square("b_out", a["b_w_out_2"][0], 2)
        ple_tiles(1)

        C, NC = 64, T // 64
        HP = 8
        w_ = carve([("xn", 2056), ("dx", 2048), ("mix", 4096), ("r", 2048), ("k", 2048), ("g", 2048), ("vu", 4096),
                    ("lw", 2048), ("hid", 1112)])
        ar = carve([("a", 2048), ("cum", 2048), ("e1", 2048), ("kk", 2048), ("e2", 2048), ("e3", 2048)], ring, 3 * SLOT)
        sc_ = ring[:, 3 * SLOT:3 * SLOT + 8192].rearrange("p (h c n) -> p h c n", h=16, c=NC)
        kbrow = ring[:, 3 * SLOT + 8192:6 * SLOT].rearrange("p (h c n) -> p h c n", h=HP, c=NC)
        kb = work[:, 0:4096].rearrange("p (h c k s) -> p h c k s", h=HP, c=NC, k=2)
        kr = w_["mix"].rearrange("p (h c k s) -> p h c k s", h=HP, c=NC, k=2)
        xm, xmt = (work[:, o:o + 2048].rearrange("p (h n) -> p h n", h=16) for o in (0, 2048))
        inv = w_["r"].rearrange("p (h n) -> p h n", h=16)
        wsb = work[:, 0:D]
        vu = w_["vu"].rearrange("p (c n) -> p c n", c=NC)
        state = w_["hid"][:, 0:D].rearrange("p (h n) -> p h n", h=HP)
        tmp = [ring[:, 3 * SLOT + 2048 * i:3 * SLOT + 2048 * (i + 1)] for i in range(6)]
        pc = sb("pc", 32)
        vu_zero, corners_zero = sem("vu_zero"), sem("corners_zero")
        gn_root, gn_rstd = sb("gn_root", 32), sb("gn_rstd", 32)
        one_ka = sb("one_ka", 8)
        gn_eps = sb("gn_eps", 1)
        W = Marks(sem("dve_rwkv"), "xn", *[f"mix{i}" for i in range(5)], "kk_sq", "bonus_in", "mix5", "args", "kk", "kb", "e3_used", "kr", "xmt0", "inv0", "xmt1", "inv1", "placed",
                  *[f"st{c}" for c in range(NC)], "centred", "gn_rstd", "y", "attn_in")
        X = Marks(sem("act_rwkv"), "tanh", "lora_a", "sigw", "siga", "r", "k", "kk_norm", "exp", "exp2", "g", "centred_sq")

        z = carve([("pt", 1024), ("eb", 2048), ("gb", 2048), ("hkv", 2048), ("hq", 2048), ("kt", 2048), ("qt", 2048), ("gate", 2048),
                   ("v", 2048), ("ot", 2048), ("mask3", 384), ("mx", 32), ("nmx", 32), ("sums", 32), ("rs", 32), ("lp", 128), ("ls", 2),
                   ("le", 2), ("nlam", 1), ("sub", 1), ("eps", 1), ("ort", 16), ("ors", 16)])
        sq4 = tmp[0]
        dprob = ring[:, 3 * SLOT + 2048:3 * SLOT + 8192].rearrange("p (h c k) -> p h c k", h=8, c=2)
        dat = ring[:, 3 * SLOT + 8192:3 * SLOT + 8192 + 3072].rearrange("p (h k) -> p h k", h=8)
        lam_init = 0.8 - 0.6 * float(np.exp(-0.3))
        Y = Marks(sem("dve_diff"), "lam_sum", "ge0", "x3", "hkv", "hq", "kt", "qt", *[n for h_ in range(8) for n in ([f"ds{h_}"] + ([f"da{h_ - 1}"] if h_ else []))], "da7", "o_rstd", "x4", "ge1", "x5")
        Z = Marks(sem("act_diff"), "lam_exp", "k", "q", *[f"dx{h_}" for h_ in range(8)], "o_sq")
        out_written = sem("out_written")
        pt_loaded = sem("pt_loaded")

        block = ctx.enter_context(nc.Block())

        @block.tensor
        def _(pe):
            tri = con("tri")

            def use_tile(name):
                pe.wait_ge(*loaded_at[name])
                return slot_of[name]

            def ada_tile(j, bank, first):
                pe.wait_ge(ada_summed, j + 1)
                for f in range(4):
                    col = 4 * (j - first) + f
                    last = pe.matmul(bank[:, col:col + 1], m[f"ada{j % 2}"][:, f * P:(f + 1) * P], ones[:, 0:1], start=True, stop=True)
                last.then_inc(ada_reduced, 1)

            def project(w, rhs, names, fs=(0, 1, 2, 3), nc_=DC):
                for i in range(0, len(fs), 2):
                    bank = banks.open(pe, names[i // 2])
                    for j in range(2):
                        for c in range(nc_):
                            last = pe.matmul(bank[:, j * T:(j + 1) * T], w[:, c, fs[i + j] * P:(fs[i + j] + 1) * P],
                                             rhs[:, c, :], start=(c == 0), stop=(c == nc_ - 1))
                    last.then_inc(*banks.filled())
                return last

            def release_tile():
                pe.drain().then_inc(weights_used, 1)

            pe.wait_ge(params_loaded, 32)
            pe_rms(0, [[sq[:, c, :] for c in range(DC)]])
            bank = banks.open(pe, "mod")
            for j in range(4):
                ada_tile(j, bank, 0)
            pe.drain().then_inc(*banks.filled())
            pe.wait_ge(*V.at("h"))
            project(slot(use_tile("win0")), h, ("xbc0", "xbc1"))
            release_tile()
            ada_tile(4, mod_bank, 4)
            project(slot(use_tile("win1")), h, ("xbc2", "xbc3"))
            release_tile()
            ada_tile(5, mod_bank, 4)
            w = slot(use_tile("win2"), pitch=268)
            for t in range(TT):
                bank = banks.open(pe, f"e{t}")
                for c in range(DC):
                    last = pe.matmul(bank[:, 0:268], h[:, c, t * P:(t + 1) * P], w[:, c, :], start=(c == 0), stop=(c == DC - 1))
                last.then_inc(*banks.filled())
            release_tile()
            project(slot(use_tile("win3")), h, ("glu_a", "glu_b"))
            release_tile()
            pe.wait_ge(*V.at("cumin"))
            cumin = chunks(s["cumin"], 2)
            bank = banks.open(pe, "acs_rows")
            for t in range(TT):
                pe.matmul(bank[:, 8 * t:8 * t + 8], tri, cumin[:, t, 0:8], start=True, stop=True)
            pe.matmul(bank[:, 16:20], tri, cumin[:, 0, 8:12], start=True, stop=True)
            pe.matmul(bank[:, 20:24], ones, cumin[:, 0, 8:12], start=True, stop=False)
            pe.matmul(bank[:, 20:24], tri, cumin[:, 1, 8:12], start=False, stop=True).then_inc(*banks.filled())
            for t in range(TT):
                for half in range(2):
                    bank = banks.open(pe, f"acs{t}{half}")
                    for j in range(4):
                        col = cumin[:, t, 4 * half + j:4 * half + j + 1]
                        last = pe.matmul(bank[:, j * P:(j + 1) * P], col.to_broadcast([P, P]), tri, start=True, stop=True)
                    last.then_inc(*banks.filled())
            for half in range(2):
                bank = banks.open(pe, f"ncum{half}")
                for j in range(2):
                    c0, c1 = (cumin[:, t, 8 + 2 * half + j:9 + 2 * half + j].to_broadcast([P, P]) for t in range(2))
                    pe.matmul(bank[:, j * T:j * T + P], c0, tri, start=True, stop=True)
                    pe.matmul(bank[:, j * T + P:(j + 1) * T], c0, ones, start=True, stop=False)
                    last = pe.matmul(bank[:, j * T + P:(j + 1) * T], c1, tri, start=False, stop=True)
                last.then_inc(*banks.filled())
            ada_tile(6, mod_bank, 4)
            project(slot(use_tile("win4")), h, ("z0", "z1"))
            release_tile()
            ada_tile(7, mod_bank, 4)
            pe.wait_ge(*A.at("silu_conv"))
            for t in range(TT):
                bank = banks.open(pe, f"xrow{t}")
                for c in range(4):
                    last = pe.transpose(bank[:, c * P:(c + 1) * P], conv[:, c, t * P:(t + 1) * P], ident)
                last.then_inc(*banks.filled())
            bank = banks.open(pe, "brow")
            for g in range(2):
                last = pe.transpose(bank[:, g * P:(g + 1) * P], conv[:, 4 + g, 0:P], ident)
            last.then_inc(*banks.filled())
            bank = banks.open(pe, "cb")
            for t in range(TT):
                for g in range(2):
                    at = (2 * t + g) * P
                    last = pe.matmul(bank[:, at:at + P], conv[:, 4 + g, t * P:(t + 1) * P], conv[:, 6 + g, t * P:(t + 1) * P],
                                     start=True, stop=True)
            last.then_inc(*banks.filled())
            project(slot(use_tile("win5")), h, ("q", "k"))
            release_tile()
            pe.wait_ge(*banks.emptied("brow"))
            pe.wait_ge(*V.at("xde"))
            bank = banks.open(pe, "st")
            for g in range(2):
                last = pe.matmul(bank[:, g * T:(g + 1) * T], m["brow"][:, g * P:(g + 1) * P], m["xde"][:, g * T:(g + 1) * T],
                                 start=True, stop=True)
            last.then_inc(*banks.filled())
            pe.wait_ge(*banks.emptied("q"))
            pe.wait_ge(*banks.emptied("k"))
            for hd in range(4):
                r = slice(64 * (hd % 2), 64 * (hd % 2) + 64)
                bank = banks.open(pe, f"s{hd}")
                pe.matmul(bank[:, 0:P], qk[r, hd // 2, 0:P], qk[r, 2 + hd // 2, 0:P], start=True, stop=True)
                pe.matmul(bank[:, P:3 * P], qk[r, hd // 2, P:T], qk[r, 2 + hd // 2, :], start=True, stop=True)\
                  .then_inc(*banks.filled())
            pe.wait_ge(*V.at("decay"))
            pe.wait_ge(*V.at("cexp"))
            pe.wait_ge(*banks.emptied("st"))
            for half in range(2):
                bank = banks.open(pe, f"y{half}")
                for pair in range(2):
                    for hd in range(2):
                        hh = 4 * half + 2 * pair + hd
                        for t in range(TT):
                            out = bank[64 * hd:64 * hd + 64, pair * T + t * P:pair * T + (t + 1) * P]
                            last = pe.matmul(out, xdt[:, t, hh * 64:hh * 64 + 64], decay[:, t, hh, :], start=True, stop=(t == 0))
                            if t:
                                last = pe.matmul(out, m["st"][:, hh * 64:hh * 64 + 64], cexp[:, hh, :], start=False, stop=True)
                last.then_inc(*banks.filled())
            ada_tile(8, mod_bank, 4)
            pe.wait_ge(*V.at("probs"))
            for hd in range(4):
                bank = banks.open(pe, f"pt{hd}")
                for j in range(3):
                    last = pe.transpose(bank[:, j * P:(j + 1) * P], prob[:, hd, j * P:(j + 1) * P], ident)
                last.then_inc(*banks.filled())
            bank = banks.open(pe, "o")
            for hd in range(4):
                pe.wait_ge(*banks.emptied(f"pt{hd}"))
                r = slice(64 * (hd % 2), 64 * (hd % 2) + 64)
                at = (hd // 2) * T
                v0, v1 = (ebuf[:, t, hd * 64:hd * 64 + 64] for t in range(2))
                pe.matmul(bank[r, at:at + P], v0, ptr[:, hd, 0:P], start=True, stop=True)
                pe.matmul(bank[r, at + P:at + T], v0, ptr[:, hd, P:2 * P], start=True, stop=False)
                last = pe.matmul(bank[r, at + P:at + T], v1, ptr[:, hd, 2 * P:3 * P], start=False, stop=True)
            last.then_inc(*banks.filled())
            ada_tile(9, mod_bank, 4)
            pe.wait_ge(*V.at("conv"))
            bank = banks.open(pe, "ln_mean")
            for c in range(2):
                last = pe.matmul(bank[:, 0:T], ones, chunks(m["sg"], 2)[:, c, :], start=(c == 0), stop=(c == 1))
            last.then_inc(*banks.filled())
            pe_rms(1, [[sq[:, c, :] for c in (0, 1)]])
            pe_rms(2, [[sq[:, c, :] for c in (2, 3)], [sq[:, c, :] for c in (4, 5)]])
            pe_rms(3, [[sq[:, c, :] for c in (6, 7)]])
            ada_tile(10, mod_bank, 4)
            ada_tile(11, mod_bank, 4)
            pe.wait_ge(*V.at("y_ssd"))
            pe.wait_ge(*V.at("y_fox"))
            pe.wait_ge(*A.at("silu_ln"))
            for j in range(2):
                project(slot(use_tile(f"wout{j}")), y, (f"wo{2 * j}", f"wo{2 * j + 1}"))
                release_tile()
            pe_rms(4, [[sq[:, c, :] for c in range(DC)]])
            pe.wait_ge(*V.at("h2"))
            w = slot(use_tile("router"), pitch=36)
            bank = banks.open(pe, "router")
            for t in range(TT):
                for c in range(DC):
                    last = pe.matmul(bank[:, 36 * t:36 * t + 36], h[:, c, t * P:(t + 1) * P], w[:, c, :], start=(c == 0), stop=(c == DC - 1))
            last.then_inc(*banks.filled())
            release_tile()

            for t in range(TT):
                for half in range(2):
                    bank = banks.open(pe, f"hrow{t}{half}")
                    for c in range(4):
                        last = pe.transpose(bank[:, c * P:(c + 1) * P], h[:, 4 * half + c, t * P:(t + 1) * P], ident)
                    last.then_inc(*banks.filled())
            pe.wait_ge(*R.at("hits"))
            hit = chunks(mo["hit"], 2)
            bank = banks.open(pe, "pos")
            pe.matmul(bank[:, 0:32], con("tri_strict"), hit[:, 0, :], start=True, stop=True)
            pe.matmul(bank[:, 32:64], ones, hit[:, 0, :], start=True, stop=False)
            pe.matmul(bank[:, 32:64], con("tri_strict"), hit[:, 1, :], start=False, stop=True)
            pe.matmul(bank[:, 64:96], ones, hit[:, 0, :], start=True, stop=False)
            pe.matmul(bank[:, 64:96], ones, hit[:, 1, :], start=False, stop=True).then_inc(*banks.filled())
            pe.wait_ge(*R.at("lists"))
            bank = banks.open(pe, "lists")
            for i in range(TOP * TT):
                last = pe.matmul(bank[:, 0:LIST], chunks(mo["hot_slot"], 4)[:, i, :], chunks(mo["hot_block"], 4)[:, i, :],
                                 start=(i == 0), stop=(i == TOP * TT - 1))
            last.then_inc(*banks.filled())

            def expert(e, p_, slots, gathered_at, loaded, used):
                gate_up = ring[:, slots[0] * SLOT:(slots[0] + 2) * SLOT].rearrange("p (k c n) -> p c k n", k=2, c=DC)
                down = ring[:, slots[2] * SLOT:(slots[2] + 1) * SLOT].rearrange("p (c n) -> p c n", c=4)
                pe.wait_ge(*gathered_at)
                for j in range(4):
                    last = pe.transpose(psum[p_][:, j * P:(j + 1) * P], xg[p_][:, j * P:(j + 1) * P], ident)
                last.then_inc(xt_done, 1)
                pe.wait_ge(xt_copied, e + 1)
                pe.wait_ge(*loaded[0])
                pe.wait_ge(*loaded[1])
                for c in range(DC):
                    x_c = xet[p_][:, (c % 4) * P + (c // 4) * 64:(c % 4) * P + (c // 4) * 64 + 64]
                    for half in range(2):
                        last = pe.matmul(psum[2 + p_][64 * half:64 * half + 64, :], x_c,
                                         gate_up[:, c, :, half * T:(half + 1) * T], start=(c == 0), stop=(c == DC - 1))
                last.then_inc(gu_done, 1)
                pe.wait_ge(gu_done, e + 1)
                pe.nop().then_inc(used, 2)
                pe.wait_ge(hid_done, e + 1)
                for c in range(2):
                    last = pe.transpose(psum[4][:, c * P:(c + 1) * P], hid[p_][:, c * P:(c + 1) * P], ident)
                last.then_inc(ht_done, 1)
                pe.wait_ge(ht_copied, e + 1)
                pe.wait_ge(*loaded[2])
                for c in range(4):
                    h_c = ht[p_][:, (c % 2) * P + (c // 2) * 64:(c % 2) * P + (c // 2) * 64 + 64]
                    for half in range(2):
                        last = pe.matmul(psum[5 + p_][64 * half:64 * half + 64, :], h_c,
                                         down[:, c, half * 512:(half + 1) * 512], start=(c == 0), stop=(c == 3))
                last.then_inc(y_done, 1)
                pe.wait_ge(y_done, e + 1)
                pe.nop().then_inc(used, 1)

            for b in range(7):
                if banks.count[b]:
                    pe.wait_ge(bank_free[b], banks.count[b])

            def main(e, p_):
                seen = e // 2 if isinstance(e, int) else (e - p_) // 2
                loaded = [(slot_loaded[k], moe_base[k] + 16 + 16 * seen) for k in expert_slots[p_]]
                expert(e, p_, expert_slots[p_], (gathered[p_], 16 + 16 * seen), loaded, weights_used)

            expert_loop(pe, main)
            pe.wait_ge(*R.at("info"))

            def spare(j):
                expert(EXPERTS + j, 0, (3, 4, 5), (spare_gathered, 16 + 16 * j), [(spare_loaded, 48 + 48 * j)] * 3, spare_used)

            spare_loop(pe, spare)
            for t in range(TT):
                pe.wait_ge(*R.at(f"comb{t}"))
                for half in range(2):
                    bank = banks.open(pe, f"moe{t}{half}")
                    for c in range(4):
                        at = t * D + (4 * half + c) * P
                        last = pe.transpose(bank[:, c * P:(c + 1) * P], mo["comb"][:, at:at + P], ident)
                    last.then_inc(*banks.filled())
            pe_rms(5, [[sq[:, c, :] for c in range(DC)]])
            xn = w_["xn"].rearrange("p (c t) -> p c t", c=DC)
            mix = [chunks(w_["mix"][:, 2048 * i:2048 * (i + 1)], 8) for i in range(2)]
            lora = ring[:, slot_of["lora"] * SLOT:(slot_of["lora"] + 1) * SLOT]
            pe_rms(6, [[sq[:, c, :] for c in range(DC)]])
            pe.wait_ge(*loaded_at["lora"])
            for i in range(2):
                pe.wait_ge(*W.at(f"mix{i}"))
                bank = banks.open(pe, f"lora{i}")
                for c in range(DC):
                    last = pe.matmul(bank[0:64, 0:T], lora[:, 512 * i + 64 * c:512 * i + 64 * c + 64], mix[i][:, c, :],
                                     start=(c == 0), stop=(c == DC - 1))
                last.then_inc(*banks.filled())
            for i in range(2):
                pe.wait_ge(*X.at(("tanh", "lora_a")[i]))
                for f in range(0, DC, 2):
                    bank = banks.open(pe, f"pre{i}{f}")
                    for j in range(2):
                        last = pe.matmul(bank[:, j * T:(j + 1) * T], lora[0:64, 1024 * (1 + i) + (f + j) * P:1024 * (1 + i) + (f + j + 1) * P],
                                         w_["hid"][0:64, i * T:(i + 1) * T], start=True, stop=True)
                    last.then_inc(*banks.filled())
            release_tile()

            def project_all(name, rhs, out, n=2):
                for j in range(n):
                    project(slot(use_tile(f"{name}{j}")), rhs, (f"{out}{2 * j}", f"{out}{2 * j + 1}"))
                    release_tile()

            pe.wait_ge(*W.at("mix2"))
            project_all("rwkv_r", mix[0], "r")
            pe.wait_ge(*W.at("mix3"))
            project_all("rwkv_k", mix[1], "k_")

            def project_rows(name, src, out, tiles_=range(2)):
                for j in tiles_:
                    w = slot(use_tile(name(j)))
                    for t in range(TT):
                        bank = banks.open(pe, f"{out}{j}{t}")
                        for c in range(DC):
                            last = pe.matmul(bank[:, :], src[:, c, t * P:(t + 1) * P], w[:, c, :], start=(c == 0), stop=(c == DC - 1))
                        last.then_inc(*banks.filled())
                    release_tile()

            pe.wait_ge(*W.at("mix4"))
            project_rows(lambda j: f"rwkv_v{j}", mix[0], "v", (0,))
            for name, mark in (("kn", "kk_sq"), ("bonus", "bonus_in")):
                pe.wait_ge(*W.at(mark))
                src = ar["e1"] if name == "kn" else ar["e3"]
                for i in range(4):
                    bank = banks.open(pe, f"{name}{i}")
                    for j in range(2):
                        c = 2 * i + j
                        last = pe.matmul(bank[:, j * T:(j + 1) * T], con("block_ones"), src[:, c * T:(c + 1) * T], start=True, stop=True)
                    last.then_inc(*banks.filled())
            project_rows(lambda j: f"rwkv_v{j}", mix[0], "v", (1,))
            pe.wait_ge(*W.at("mix5"))
            project_all("rwkv_g", mix[1], "g")
            pe.wait_ge(*W.at("kb"))
            for c in range(NC):
                for half in range(2):
                    bank = banks.open(pe, f"kbt{c}{half}")
                    for j in range(4):
                        last = pe.transpose(bank[:, j * P:(j + 1) * P], kb[:, 4 * half + j, c, :, :].rearrange("p k s -> p (k s)"), ident)
                    last.then_inc(*banks.filled())
            pe.wait_ge(*W.at("kr"))
            for half in range(2):
                for c in range(NC):
                    for hd in range(2):
                        bank = banks.open(pe, f"sc{half}{c}{hd}")
                        r = slice(64 * hd, 64 * hd + 64)
                        for j in range(4):
                            last = pe.matmul(bank[:, j * P:(j + 1) * P], kb[r, 4 * half + j, c, :, :].rearrange("p k s -> p (k s)"),
                                             kr[r, 4 * half + j, c, :, :].rearrange("p k s -> p (k s)"), start=True, stop=True)
                        last.then_inc(*banks.filled())
            for q in range(2):
                pe.wait_ge(*W.at(f"xmt{q}"))
                for h4 in range(4):
                    bank = banks.open(pe, f"x{q}_0_{h4}")
                    for j in range(4):
                        last = pe.transpose(bank[:, j * P:(j + 1) * P], xmt[:, 4 * h4 + j, :], ident)
                    last.then_inc(*banks.filled())
                for level in range(1, 6):
                    for h4 in range(4):
                        pe.wait_ge(*banks.emptied(f"x{q}_{level - 1}_{h4}"))
                        if level > 1:
                            pe.wait_ge(*banks.emptied(f"xt{q}_{level - 1}_{h4}"))
                        bank = banks.open(pe, f"x{q}_{level}_{h4}")
                        for j in range(4):
                            hh = 4 * h4 + j
                            last = pe.matmul(bank[:, j * P:(j + 1) * P], xmt[:, hh, :], xm[:, hh, :], start=True, stop=True)
                        if level < 5:
                            last.then_inc(*banks.filled())
                            bank = banks.open(pe, f"xt{q}_{level}_{h4}")
                            for j in range(4):
                                hh = 4 * h4 + j
                                last = pe.matmul(bank[:, j * P:(j + 1) * P], xm[:, hh, :], xmt[:, hh, :], start=True, stop=True)
                        last.then_inc(*banks.filled())
                    for h4 in range(4):
                        pe.wait_ge(*banks.emptied(f"x{q}_{level}_{h4}"))
                        if level == 1:
                            pe.wait_ge(*W.at(f"inv{q}"))
                        if level > 1:
                            pe.wait_ge(*banks.emptied(f"inv{q}_{level - 1}_{h4}"))
                        bank = banks.open(pe, f"inv{q}_{level}_{h4}")
                        for j in range(4):
                            hh = 4 * h4 + j
                            last = pe.matmul(bank[:, j * P:(j + 1) * P], xm[:, hh, :], inv[:, hh, :], start=True, stop=True)
                        last.then_inc(*banks.filled())
            pe.wait_ge(*W.at("placed"))
            for c in range(NC):
                rows = slice(64, 128) if c % 2 == 0 else slice(0, 64)
                if c:
                    pe.wait_ge(*W.at(f"st{c - 1}"))
                for half in range(2):
                    bank = banks.open(pe, f"w{c}{half}")
                    for j in range(4):
                        hp = 4 * half + j
                        for hd in range(2):
                            hh = 2 * hp + hd
                            out = bank[rows, j * P + 64 * hd:j * P + 64 * hd + 64]
                            if c:
                                pe.matmul(out, kr[:, hp, c, 0, :], state[:, hp, 64 * hd:64 * hd + 64], start=True, stop=False)
                            last = pe.matmul(out, sc_[:, hh, c, 0:64], vu[:, c, hh * 64:hh * 64 + 64], start=(c == 0), stop=True)
                    last.then_inc(*banks.filled())
                for half in range(2):
                    pe.wait_ge(*banks.emptied(f"w{c}{half}"))
                    bank = banks.open(pe, f"u{c}{half}")
                    for j in range(8):
                        hh = 8 * half + j
                        last = pe.matmul(bank[rows, j * 64:(j + 1) * 64], sc_[rows, hh, c, 0:64], wsb[rows, hh * 64:(hh + 1) * 64],
                                         start=True, stop=True)
                    last.then_inc(*banks.filled())
                for half in range(2):
                    pe.wait_ge(*banks.emptied(f"u{c}{half}"))
                    if c < NC - 1:
                        bank = banks.open(pe, f"ds{c}{half}")
                        for j in range(4):
                            hp = 4 * half + j
                            last = pe.matmul(bank[:, j * P:(j + 1) * P], kbrow[:, hp, c, :], vu[:, c, hp * P:(hp + 1) * P], start=True, stop=True)
                        last.then_inc(*banks.filled())
                bank = banks.open(pe, f"yr{c}")
                for hp in range(HP):
                    for hd in range(2):
                        hh = 2 * hp + hd
                        out = bank[64 * hd:64 * hd + 64, hp * 64:(hp + 1) * 64]
                        if c:
                            pe.matmul(out, state[:, hp, 64 * hd:64 * hd + 64], kr[:, hp, c, 1, :], start=True, stop=False)
                        last = pe.matmul(out, vu[:, c, hh * 64:(hh + 1) * 64], sc_[:, hh, c, 64:128], start=(c == 0), stop=True)
                last.then_inc(*banks.filled())
            for c in range(NC):
                rows = slice(0, 64) if c % 2 == 0 else slice(64, 128)
                bank = banks.open(pe, f"vt{c}")
                for hp in range(HP):
                    last = pe.transpose(bank[:, hp * 64:(hp + 1) * 64], vu[rows, c, hp * P:(hp + 1) * P], ident[rows, rows])
                last.then_inc(*banks.filled())
            for c in range(NC):
                pe.wait_ge(*banks.emptied(f"yr{c}"))
            for i in range(4):
                bank = banks.open(pe, f"gmean{i}")
                for j in range(2):
                    c = 2 * i + j
                    last = pe.matmul(bank[:, j * T:(j + 1) * T], con("block_ones"), w_["lw"][:, c * T:(c + 1) * T], start=True, stop=True)
                last.then_inc(*banks.filled())
            pe.wait_ge(*X.at("centred_sq"))
            bank = banks.open(pe, "gvar")
            for t in range(TT):
                for c in range(DC):
                    at = 2 * (t * DC + c)
                    last = pe.matmul(bank[:, at:at + 2], tmp[1][:, c * T + t * P:c * T + (t + 1) * P], con("block_ones")[:, 0:P:64],
                                     start=True, stop=True)
            last.then_inc(*banks.filled())
            pe.wait_ge(*W.at("gn_rstd"))
            for i in range(4):
                bank = banks.open(pe, f"gb{i}")
                for j in range(2):
                    for t in range(TT):
                        at = 2 * (t * DC + 2 * i + j)
                        last = pe.matmul(bank[:, j * T + t * P:j * T + (t + 1) * P],
                                         tmp[0][:, 64 * at:64 * at + P], ident, start=True, stop=True)
                last.then_inc(*banks.filled())
            pe.wait_ge(*W.at("y"))
            project_all("rwkv_out", chunks(w_["lw"], 8), "ro")
            pe_rms(7, [[chunks(tmp[1], 8)[:, c, :] for c in range(DC)]])

            def ple(l, x_ready):
                w = ring[:, slot_of[f"ple_w{l}"] * SLOT:slot_of[f"ple_w{l}"] * SLOT + 2 * D].rearrange("p (c n) -> p c n", c=2)
                pe.wait_ge(pt_loaded, 16)
                use_tile(f"ple_w{l}")
                project(w, z["pt"][:, 512 * l:512 * (l + 1)].rearrange("p (c t) -> p c t", c=2), [f"pe{l}_{i}" for i in range(4)],
                        fs=range(8), nc_=2)
                release_tile()
                pe.wait_ge(*x_ready)
                project_all(f"ple_gate{l}_", xv, f"pg{l}_")
                pe_rms((8, 11)[l], [[chunks(sq4, 8)[:, c, :] for c in range(DC)]])

            ple(0, W.at("attn_in"))
            pe_rms(9, [[chunks(sq4, 8)[:, c, :] for c in range(DC)]])
            pe.wait_ge(*Y.at("hkv"))
            hkv, hq = chunks(z["hkv"], 8), chunks(z["hq"], 8)
            project_all("kv", hkv, "kk")
            project_rows(lambda j: f"kv{2 + j}", hkv, "vv")

            def rotate(name, src, evac):
                pe.wait_ge(*evac)
                for i in range(4):
                    bank = banks.open(pe, f"{name}{i}")
                    pe.matmul(bank[:, :], con("rot"), src[:, 512 * i:512 * (i + 1)], start=True, stop=True).then_inc(*banks.filled())

            rotate("kr", z["kt"], Z.at("k"))
            pe.wait_ge(*Y.at("hq"))
            project_all("b_in", hq, "qq")
            rotate("qr", z["qt"], Z.at("q"))

            def gate(i):
                w = slot(use_tile(f"b_in{2 + i // 2}") if i % 2 == 0 else slot_of[f"b_in{2 + i // 2}"])
                project(w, hq, (f"gg{i}",), fs=(2 * (i % 2), 2 * (i % 2) + 1))
                if i % 2:
                    release_tile()

            gate(0)
            pe.wait_ge(*Y.at("kt"))
            pe.wait_ge(*Y.at("qt"))
            kt, qt = chunks(z["kt"], 8), chunks(z["qt"], 8)

            def diff_scores(hh):
                for c in range(2):
                    r = slice(64 * c, 64 * c + 64)
                    bank = banks.open(pe, f"d{hh}{c}")
                    pe.matmul(bank[:, 0:P], qt[r, hh, 0:P], kt[r, hh, 0:P], start=True, stop=True)
                    pe.matmul(bank[:, P:3 * P], qt[r, hh, P:T], kt[r, hh, :], start=True, stop=True).then_inc(*banks.filled())

            def diff_turn(hh):
                pe.wait_ge(*Y.at(f"da{hh}"))
                bank = banks.open(pe, f"at{hh}")
                for j in range(3):
                    last = pe.transpose(bank[:, j * P:(j + 1) * P], dprob[:, hh, 0, j * P:(j + 1) * P], ident)
                last.then_inc(*banks.filled())

            def diff_values(h2):
                bank = banks.open(pe, f"do{h2}")
                for j in range(2):
                    hh = 2 * h2 + j
                    pe.wait_ge(*banks.emptied(f"at{hh}"))
                    v0, v1 = (z["v"][:, t * D + hh * P:t * D + (hh + 1) * P] for t in range(2))
                    pe.matmul(bank[:, j * T:j * T + P], v0, dat[:, hh, 0:P], start=True, stop=True)
                    pe.matmul(bank[:, j * T + P:(j + 1) * T], v0, dat[:, hh, P:2 * P], start=True, stop=False)
                    last = pe.matmul(bank[:, j * T + P:(j + 1) * T], v1, dat[:, hh, 2 * P:3 * P], start=False, stop=True)
                last.then_inc(*banks.filled())

            for hh in range(8):
                diff_scores(hh)
                if hh in (2, 4, 6):
                    gate(hh // 2)
                if hh >= 2:
                    diff_turn(hh - 2)
            diff_turn(6)
            diff_turn(7)
            for h2 in range(4):
                diff_values(h2)
            pe.wait_ge(*Z.at("o_sq"))
            bank = banks.open(pe, "on")
            for t in range(TT):
                for hh in range(8):
                    last = pe.matmul(bank[:, 8 * t + hh:8 * t + hh + 1], sq4[:, hh * T + t * P:hh * T + (t + 1) * P], ones[:, 0:1], start=True, stop=True)
            last.then_inc(*banks.filled())
            pe.wait_ge(*Y.at("o_rstd"))
            for i in range(4):
                bank = banks.open(pe, f"ob{i}")
                for j in range(2):
                    for t in range(TT):
                        at = 8 * t + 2 * i + j
                        last = pe.matmul(bank[:, j * T + t * P:j * T + (t + 1) * P], z["ors"][:, at:at + 1].to_broadcast([P, P]), ident,
                                         start=True, stop=True)
                last.then_inc(*banks.filled())
            for i in range(4):
                pe.wait_ge(*banks.emptied(f"ob{i}"))
            project_all("b_out", chunks(z["ot"], 8), "bo")
            pe_rms(10, [[chunks(sq4, 8)[:, c, :] for c in range(DC)]])
            ple(1, Y.at("x4"))


        @block.scalar
        def _(act):
            act.wait_ge(params_loaded, 32)
            act.activation(s["cond"], par("c"), ACT.Silu).then_inc(*A.mark("cond"))
            act.wait_ge(x_loaded, 16)
            act_squares(m["sq"], xt[:])
            act_rms(0, T)
            act.wait_ge(*V.at("zeros"))
            for i in range(4):
                act.wait_ge(*banks.ready(f"xbc{i}"))
                act.activation(xbc[:, 2 * i:2 * i + 2, 3:3 + T], chunks(banks[f"xbc{i}"][:, :], 2), ACT.Copy)\
                   .then_inc(*banks.release(f"xbc{i}"))
            for t in range(TT):
                act.wait_ge(*banks.ready(f"e{t}"))
                act.activation(ebuf[:, t, :], banks[f"e{t}"][:, 0:268], ACT.Copy).then_inc(*banks.release(f"e{t}"))
            act.activation(s["ea"], par("ssd_a_log"), ACT.Exp).then_inc(*A.mark("ea"))
            act.wait_ge(*V.at("spa"))
            act.activation(s["spu"], s["spa"], ACT.Exp, scale=-1.0).then_inc(*A.mark("spu"))
            act.wait_ge(*banks.ready("glu_b"))
            act.activation(m["sg"], banks["glu_b"][:, :], ACT.Sigmoid).then_inc(*banks.release("glu_b"))
            act.wait_ge(*V.at("xconv"))
            for c in range(DC):
                ins = act.activation(conv[:, c, :], conv[:, c, :], ACT.Silu, bias=par("ssd_conv_b", c, 1))
            ins.then_inc(*A.mark("silu_conv"))
            act.wait_ge(*V.at("tdiff"))
            act.activation(s["dte"], s["tdiff"], ACT.Exp).then_inc(*A.mark("dte"))
            for half in range(2):
                act.wait_ge(*banks.ready(f"acs1{half}"))
                ins = act.activation(cexp[:, 4 * half:4 * half + 4, :], chunks(banks[f"acs1{half}"][:, :], 4), ACT.Exp)
            ins.then_inc(*A.mark("cexp"))
            act.wait_ge(*V.at("args"))
            act.activation(m["decay"], m["decay"], ACT.Exp).then_inc(*A.mark("decay"))
            for i in range(2):
                act.wait_ge(*banks.ready(f"z{i}"))
                act.activation(m["zs"][:, 512 * i:512 * i + 512], banks[f"z{i}"][:, :], ACT.Silu)\
                   .then_inc(*banks.release(f"z{i}"))
            act.wait_ge(*banks.ready("brow"))
            act.activation(m["brow"], banks["brow"][:, 0:T], ACT.Copy).then_inc(*banks.release("brow"))
            for i, name in enumerate(("q", "k")):
                act.wait_ge(*banks.ready(name))
                act.activation(m["qk"][:, 512 * i:512 * i + 512], banks[name][:, :], ACT.Copy, scale=(0.125, 1.0)[i])\
                   .then_inc(*banks.release(name))
            act.wait_ge(*V.at("scores"))
            for hd in range(4):
                for q, (lo, hi) in enumerate(((0, P), (P, 3 * P))):
                    i = 2 * hd + q
                    ins = act.activation(prob[:, hd, lo:hi], prob[:, hd, lo:hi], ACT.Exp, bias=s["nmx"][:, i:i + 1],
                                         accum_out=s["sums"][:, i:i + 1])
            ins.then_inc(*A.mark("exp"))
            act.wait_ge(*V.at("ln_centred"))
            act.activation(m["sq"][:, 0:512], m["lnx"], ACT.Square).then_inc(rms_squares, 1)
            act_rms(1, T)
            act.wait_ge(*V.at("y_gated"))
            act.activation(m["sq"][:, 512:1536], m["y"][:, 0:1024], ACT.Square).then_inc(rms_squares, 1)
            act_rms(2, 2 * T)
            act.wait_ge(*banks.ready("o"))
            act.activation(m["y"][:, 1024:1536], banks["o"][:, :], ACT.Copy).then_inc(*banks.release("o"))
            act.wait_ge(*banks.emptied("o"))
            act.activation(m["sq"][:, 1536:2048], m["y"][:, 1024:1536], ACT.Square).then_inc(rms_squares, 1)
            act_rms(3, T)
            act.wait_ge(*V.at("ln_norm"))
            for c in range(2):
                ins = act.activation(y[:, 6 + c, :], m["lnx"][:, c * T:(c + 1) * T], ACT.Silu, scale=par("cm_ln_g", c, 1),
                                     bias=par("cm_ln_b", c, 1))
            ins.then_inc(*A.mark("silu_ln"))
            act.wait_ge(*V.at("x1"))
            act_squares(m["sq"], xt[:])
            act_rms(4, T)
            for t in range(TT):
                for half in range(2):
                    act.wait_ge(*banks.ready(f"hrow{t}{half}"))
                    at = t * D + half * 512
                    act.activation(m["conv"][:, at:at + 512], banks[f"hrow{t}{half}"][:, :], ACT.Copy)\
                       .then_inc(*banks.release(f"hrow{t}{half}"))
            act.wait_ge(*R.at("gd"))
            act.activation(mo["ge"], mo["gd"], ACT.Exp).then_inc(*S.mark("ge"))
            act.wait_ge(*R.at("md"))
            act.activation(mo["e2"], mo["md"], ACT.Exp).then_inc(*S.mark("e2"))

            def expert(e, p_):
                act.wait_ge(xt_done, e + 1)
                act.activation(xet[p_], psum[p_][:, :], ACT.Copy).then_inc(xt_copied, 1)
                act.wait_ge(gu_done, e + 1)
                act.activation(sg_[p_], psum[2 + p_][:, 0:T], ACT.Silu).then_inc(silu_done, 1)

            expert_loop(act, expert)
            act.wait_ge(*R.at("info"))
            spare_loop(act, lambda j: expert(EXPERTS + j, 0))
            act.wait_ge(*R.at("x2"))
            act_squares(m["sq"], xt[:])
            act_rms(5, T)
            act.wait_ge(*R.at("final"))
            act_squares(m["sq"], xt[:])
            act_rms(6, T)
            act.wait_ge(*banks.ready("lora0"))
            act.activation(w_["hid"][0:64, 0:T], banks["lora0"][0:64, 0:T], ACT.Tanh).then_inc(*banks.release("lora0"))
            act.wait_ge(*banks.emptied("lora0"))
            act.nop().then_inc(*X.mark("tanh"))
            act.wait_ge(*banks.ready("lora1"))
            act.activation(w_["hid"][0:64, T:2 * T], banks["lora1"][0:64, 0:T], ACT.Copy).then_inc(*banks.release("lora1"))
            act.wait_ge(*banks.emptied("lora1"))
            act.nop().then_inc(*X.mark("lora_a"))
            for i, (out, bias, mark) in enumerate(((w_["lw"], "a_w0_2", "sigw"), (ar["a"], "a_a0_2", "siga"))):
                for f in range(0, DC, 2):
                    act.wait_ge(*banks.ready(f"pre{i}{f}"))
                    for j in range(2):
                        ins = act.activation(out[:, (f + j) * T:(f + j + 1) * T], banks[f"pre{i}{f}"][:, j * T:(j + 1) * T], ACT.Sigmoid,
                                             bias=par(bias, f + j, 1))
                    ins.then_inc(*banks.release(f"pre{i}{f}"))
                act.wait_ge(*banks.emptied(f"pre{i}6"))
                act.nop().then_inc(*X.mark(mark))

            def evacuate(name, out, func, mark=None):
                for i in range(4):
                    act.wait_ge(*banks.ready(f"{name}{i}"))
                    act.activation(out[:, 512 * i:512 * (i + 1)], banks[f"{name}{i}"][:, :], func).then_inc(*banks.release(f"{name}{i}"))
                if mark:
                    act.wait_ge(*banks.emptied(f"{name}3"))
                    act.nop().then_inc(*mark)

            evacuate("r", w_["r"], ACT.Copy, X.mark("r"))
            evacuate("k_", w_["k"], ACT.Copy, X.mark("k"))
            act.wait_ge(vu_zero, 1)

            def rows_of_v(j):
                for t in range(TT):
                    act.wait_ge(*banks.ready(f"v{j}{t}"))
                    for e in range(2):
                        r = slice(64 * e, 64 * e + 64)
                        ins = act.activation(vu[r, 2 * t + e, 512 * j:512 * (j + 1)], banks[f"v{j}{t}"][r, :], ACT.Copy)
                    ins.then_inc(*banks.release(f"v{j}{t}"))

            rows_of_v(0)
            act.wait_ge(*W.at("bonus_in"))
            for i in range(4):
                act.wait_ge(*banks.ready(f"kn{i}"))
                act.activation(ar["kk"][:, 512 * i:512 * (i + 1)], banks[f"kn{i}"][:, :], ACT.Sqrt).then_inc(*banks.release(f"kn{i}"))
            act.wait_ge(*banks.emptied("kn3"))
            act.nop().then_inc(*X.mark("kk_norm"))
            rows_of_v(1)
            act.wait_ge(*W.at("args"))
            act.activation(ar["e1"], ar["cum"], ACT.Exp)
            act.activation(ar["e3"], ar["e3"], ACT.Exp).then_inc(*X.mark("exp"))
            act.wait_ge(*W.at("kk"))
            act.activation(ar["e2"], ar["cum"], ACT.Exp, scale=-1.0).then_inc(*X.mark("exp2"))
            evacuate("g", w_["g"], ACT.Silu, X.mark("g"))
            act.wait_ge(*W.at("e3_used"))
            for c in range(NC):
                for half in range(2):
                    act.wait_ge(*banks.ready(f"kbt{c}{half}"))
                    act.activation(kbrow[:, 4 * half:4 * half + 4, c, :], chunks(banks[f"kbt{c}{half}"][:, :], 4), ACT.Copy,
                                   scale=con(("sign_even", "sign_odd")[c % 2])).then_inc(*banks.release(f"kbt{c}{half}"))
            for q in range(2):
                for level in range(6):
                    for h4 in range(4):
                        act.wait_ge(*banks.ready(f"x{q}_{level}_{h4}"))
                        if 0 < level < 5:
                            act.wait_ge(*banks.ready(f"xt{q}_{level}_{h4}"))
                        act.activation(xm[:, 4 * h4:4 * h4 + 4, :], chunks(banks[f"x{q}_{level}_{h4}"][:, :], 4), ACT.Copy)\
                           .then_inc(*banks.release(f"x{q}_{level}_{h4}"))
            for c in range(NC):
                rows = slice(64, 128) if c % 2 == 0 else slice(0, 64)
                act.wait_ge(*banks.ready(f"w{c}1"))
                act.activation(wsb[rows, 512:1024], banks[f"w{c}1"][rows, :], ACT.Copy).then_inc(*banks.release(f"w{c}1"))
                act.wait_ge(*banks.ready(f"u{c}1"))
                act.activation(vu[rows, c, 512:1024], banks[f"u{c}1"][rows, :], ACT.Copy).then_inc(*banks.release(f"u{c}1"))
                act.wait_ge(*banks.ready(f"yr{c}"))
                act.activation(chunks(w_["lw"], 8)[:, :, c * C:(c + 1) * C], chunks(banks[f"yr{c}"][:, :], 8), ACT.Copy)\
                   .then_inc(*banks.release(f"yr{c}"))
            act.wait_ge(*W.at("centred"))
            act.activation(tmp[1], tmp[0], ACT.Square).then_inc(*X.mark("centred_sq"))
            act.wait_ge(*banks.ready("gvar"))
            act.activation(gn_root[:], banks["gvar"][:, 0:32], ACT.Sqrt, scale=1.0 / 64, bias=gn_eps[:, 0:1]).then_inc(*banks.release("gvar"))
            evacuate("ro", tmp[0], ACT.Copy)
            act.wait_ge(*banks.emptied("ro3"))
            act_squares(tmp[1], tmp[0])
            act_rms(7, T)
            act.wait_ge(*Y.at("lam_sum"))
            act.activation(z["le"], z["ls"], ACT.Exp).then_inc(*Z.mark("lam_exp"))

            def squares(src):
                act_squares(sq4, src)

            def ple(l):
                evacuate(f"pe{l}_", z["eb"], ACT.Copy)
                evacuate(f"pg{l}_", z["gb"], ACT.Sigmoid)
                act.wait_ge(*Y.at(f"ge{l}"))
                squares(z["gb"])
                act_rms((8, 11)[l], T)

            ple(0)
            act.wait_ge(*Y.at("x3"))
            squares(xt[:])
            act_rms(9, T)
            evacuate("kk", z["kt"], ACT.Copy, Z.mark("k"))
            for j in range(2):
                for t in range(TT):
                    act.wait_ge(*banks.ready(f"vv{j}{t}"))
                    act.activation(z["v"][:, t * D + 512 * j:t * D + 512 * (j + 1)], banks[f"vv{j}{t}"][:, :], ACT.Copy)\
                       .then_inc(*banks.release(f"vv{j}{t}"))
            for i in range(4):
                act.wait_ge(*banks.ready(f"qq{i}"))
                act.activation(z["qt"][:, 512 * i:512 * (i + 1)], banks[f"qq{i}"][:, :], ACT.Copy, scale=0.125).then_inc(*banks.release(f"qq{i}"))
            act.wait_ge(*banks.emptied("qq3"))
            act.nop().then_inc(*Z.mark("q"))

            def gate(i):
                act.wait_ge(*banks.ready(f"gg{i}"))
                act.activation(z["gate"][:, 512 * i:512 * (i + 1)], banks[f"gg{i}"][:, :], ACT.Silu).then_inc(*banks.release(f"gg{i}"))

            gate(0)
            for hh in range(8):
                if hh in (3, 5, 7):
                    gate((hh - 1) // 2)
                act.wait_ge(*Y.at(f"ds{hh}"))
                for c in range(2):
                    for q, (lo, hi) in enumerate(((0, P), (P, 3 * P))):
                        i = 4 * hh + 2 * c + q
                        ins = act.activation(dprob[:, hh, c, lo:hi], dprob[:, hh, c, lo:hi], ACT.Exp, bias=z["nmx"][:, i:i + 1],
                                             accum_out=z["sums"][:, i:i + 1])
                ins.then_inc(*Z.mark(f"dx{hh}"))
            evacuate("do", z["ot"], ACT.Copy)
            act.wait_ge(*banks.emptied("do3"))
            act.activation(sq4, z["ot"], ACT.Square).then_inc(*Z.mark("o_sq"))
            act.wait_ge(*banks.ready("on"))
            act.activation(z["ort"], banks["on"][:, 0:16], ACT.Sqrt, scale=1.0 / P, bias=z["eps"]).then_inc(*banks.release("on"))
            evacuate("bo", z["gb"], ACT.Copy)
            act.wait_ge(*banks.emptied("bo3"))
            squares(z["gb"])
            act_rms(10, T)
            ple(1)

        @block.vector
        def _(dve):
            link = lambda ins: dve_steps.link(dve, ins)

            def taps(out, src, weight, n, count):
                at = {}
                for k in range(n):
                    for c in range(count):
                        window = src[:, c, k:k + T]
                        if k == 0:
                            ins = dve.tensor_scalar(out[:, c, :], window, weight(c, k), None, ALU.mult)
                        else:
                            dve.wait_ge(dve_steps.sem, at[c])
                            ins = dve.scalar_tensor_tensor(out=out[:, c, :], in0=window, scalar=weight(c, k), in1=out[:, c, :],
                                                           op0=ALU.mult, op1=ALU.add)
                        if k == n - 1 and c == count - 1:
                            return ins
                        at[c] = dve_steps.step(ins)

            def modulate(out, src, scale, shift, buf):
                link(dve.tensor_tensor(buf, src, rst[:, 0:T].unsqueeze(1).to_broadcast([P, DC, T]), ALU.mult))
                for c in range(DC):
                    ins = dve.tensor_scalar(out[:, c, :], buf[:, c, :], scale[:, c:c + 1], shift[:, c:c + 1], ALU.mult, ALU.add)
                return ins

            dve.memset(xbc[:, :, 0:3], 0.0)
            dve.wait_ge(params_loaded, 32)
            dve.memset(u[:, :, 0:30], 0.0).then_inc(*V.mark("zeros"))
            dve.wait_ge(*A.at("cond"))
            ada_sum(dve, dve_steps, 0)
            ada_sum(dve, dve_steps, 1)
            dve_rms(0, T)
            ada_sum(dve, dve_steps, 2)
            ada_sum(dve, dve_steps, 3)
            dve.wait_ge(*banks.ready("mod"))
            mod = s["mod"]
            dve.tensor_tensor(mod[:, 0:16], banks["mod"][:, 0:16], par("ada_b", 0, 16), ALU.add).then_inc(*banks.release("mod"))
            dve.wait_ge(*banks.emptied("mod"))
            link(dve.scalar_tensor_tensor(out=s["gmix"], in0=mod[:, 8:16], scalar=1.0, in1=par("norm_mix_g"),
                                          op0=ALU.add, op1=ALU.mult))
            modulate(h, xv, s["gmix"], mod[:, 0:8], conv).then_inc(*V.mark("h"))
            ada_sum(dve, dve_steps, 4)
            ada_sum(dve, dve_steps, 5)
            for i in range(4):
                dve.wait_ge(*banks.emptied(f"xbc{i}"))
            dve.wait_ge(*V.at("h"))
            taps(conv, xbc, lambda c, k: par("ssd_conv_w", 4 * c + k, 1), 4, 8).then_inc(*V.mark("xconv"))
            spx = chunks(s["spx"], 2)
            for t in range(TT):
                dve.wait_ge(*banks.emptied(f"e{t}"))
                dve.tensor_tensor(spx[:, t, 0:8], ebuf[:, t, 260:268], par("ssd_dt_bias"), ALU.add)
                ins = dve.scalar_tensor_tensor(out=spx[:, t, 8:12], in0=ebuf[:, t, 256:260], scalar=-1.0, in1=par("fox_f_bias"),
                                               op0=ALU.mult, op1=ALU.subtract)
            link(ins)
            dve.scalar_tensor_tensor(out=s["spa"], in0=s["spx"], scalar=-1.0, in1=s["spx"], op0=ALU.mult, op1=ALU.max)\
               .then_inc(*V.mark("spa"))
            link(dve.tensor_scalar(s["spm"], s["spx"], 0.0, None, ALU.max))
            dve.wait_ge(*A.at("spu"))
            link(dve.tensor_scalar(s["spw"], s["spu"], 2.0, None, ALU.add))
            link(dve.reciprocal(s["spr"], s["spw"]))
            link(dve.tensor_tensor(s["spl"], s["spu"], s["spr"], ALU.mult))
            link(dve.tensor_tensor(s["spd"], s["spl"], s["spl"], ALU.mult))
            link(dve.tensor_scalar(s["spw"], s["spd"], 1.0 / 15, None, ALU.mult))
            for odd in (13, 11, 9, 7, 5, 3):
                link(dve.scalar_tensor_tensor(out=s["spw"], in0=s["spw"], scalar=1.0 / odd, in1=s["spd"], op0=ALU.add, op1=ALU.mult))
            link(dve.scalar_tensor_tensor(out=s["spr"], in0=s["spw"], scalar=1.0, in1=s["spl"], op0=ALU.add, op1=ALU.mult))
            link(dve.scalar_tensor_tensor(out=s["sp"], in0=s["spr"], scalar=2.0, in1=s["spm"], op0=ALU.mult, op1=ALU.add))
            dve.wait_ge(*A.at("ea"))
            sp, cumin = chunks(s["sp"], 2), chunks(s["cumin"], 2)
            dve.scalar_tensor_tensor(out=cumin[:, :, 0:8], in0=sp[:, :, 0:8], scalar=-1.0,
                                     in1=s["ea"].unsqueeze(1).to_broadcast([P, 2, 8]), op0=ALU.mult, op1=ALU.mult)
            dve.tensor_copy(cumin[:, :, 8:12], sp[:, :, 8:12]).then_inc(*V.mark("cumin"))
            dve.wait_ge(*banks.emptied("glu_b"))
            dve.wait_ge(*banks.ready("glu_a"))
            dve.tensor_tensor(u[:, :, 30:30 + T], chunks(banks["glu_a"][:, :], 2), chunks(m["sg"], 2), ALU.mult)\
               .then_inc(*banks.release("glu_a"))
            dve.wait_ge(*banks.emptied("glu_a"))
            dve.nop().then_inc(*V.mark("u_gated"))
            dve.wait_ge(*banks.ready("acs_rows"))
            link(dve.tensor_scalar(s["nacs"], banks["acs_rows"][:, 0:16], -1.0, None, ALU.mult))
            dve.tensor_copy(s["nq"], banks["acs_rows"][:, 16:24]).then_inc(*banks.release("acs_rows"))
            for half in range(2):
                dve.wait_ge(*banks.ready(f"acs0{half}"))
                end = chunks(banks[f"acs0{half}"][:, :], 4)[:, :, P - 1]
                ins = dve.tensor_tensor(s["tdiff"][:, 4 * half:4 * half + 4], end, s["nacs"][:, 4 * half:4 * half + 4], ALU.add)
            ins.then_inc(*V.mark("tdiff"))
            for t in range(TT):
                for half in range(2):
                    dve.wait_ge(*banks.ready(f"acs{t}{half}"))
                    if t:
                        dve.wait_ge(*A.at("cexp"))
                    for j in range(4):
                        hh = 4 * half + j
                        ins = dve.tensor_scalar(decay[:, t, hh, :], banks[f"acs{t}{half}"][:, j * P:(j + 1) * P],
                                                s["nacs"][:, 8 * t + hh:8 * t + hh + 1], 0.0, ALU.add, ALU.min)
                    ins.then_inc(*banks.release(f"acs{t}{half}"))
            dve.wait_ge(*banks.emptied("acs11"))
            dve.nop().then_inc(*V.mark("args"))
            for half in range(2):
                dve.wait_ge(*banks.ready(f"ncum{half}"))
                for j in range(2):
                    hd, b = 2 * half + j, banks[f"ncum{half}"][:, j * T:(j + 1) * T]
                    link(dve.tensor_tensor(prob[:, hd, 0:P], b[:, 0:P], con("causal"), ALU.add))
                    link(dve.tensor_copy(prob[:, hd, P:2 * P], b[:, 0:P]))
                    ins = dve.tensor_tensor(prob[:, hd, 2 * P:3 * P], b[:, P:T], con("causal"), ALU.add)
                    if j == 0:
                        link(ins)
                ins.then_inc(*banks.release(f"ncum{half}"))
            dve.wait_ge(*V.at("u_gated"))
            lx = chunks(m["sg"], 2)
            link(taps(lx, u, lambda c, k: par("cm_conv_w", 31 * c + k, 1), 31, 2))
            for c in range(2):
                ins = dve.tensor_scalar(lx[:, c, :], lx[:, c, :], par("cm_conv_b", c, 1), None, ALU.add)
            ins.then_inc(*V.mark("conv"))
            for t in range(TT):
                dve.wait_ge(*banks.ready(f"xrow{t}"))
                dve.tensor_tensor(xdt[:, t, :].rearrange("p (h i) -> p h i", h=8), chunks(banks[f"xrow{t}"][:, :], 8),
                                  sp[:, t, 0:8].unsqueeze(2).to_broadcast([P, 8, 64]), ALU.mult)\
                   .then_inc(*banks.release(f"xrow{t}"))
            dve.wait_ge(*banks.emptied("xrow0"))
            dve.wait_ge(*A.at("dte"))
            dve.tensor_tensor(chunks(m["xde"], 8), chunks(xdt[:, 0, :], 8),
                              s["dte"].unsqueeze(2).to_broadcast([P, 8, 64]), ALU.mult).then_inc(*V.mark("xde"))
            dve.wait_ge(*banks.ready("cb"))
            dve.tensor_tensor(chunks(m["cb"], 4), chunks(banks["cb"][:, :], 4),
                              con("tri").unsqueeze(1).to_broadcast([P, 4, P]), ALU.mult).then_inc(*banks.release("cb"))
            dve.wait_ge(*banks.emptied("cb"))
            dve.wait_ge(*A.at("decay"))
            for t in range(TT):
                for g in range(2):
                    block_ = decay[:, t, 4 * g:4 * g + 4, :]
                    ins = dve.tensor_tensor(block_, block_, cb[:, t, g, :].unsqueeze(1).to_broadcast([P, 4, P]), ALU.mult)
            ins.then_inc(*V.mark("decay"))
            dve.wait_ge(*A.at("silu_conv"))
            for g in range(2):
                block_ = cexp[:, 4 * g:4 * g + 4, :]
                ins = dve.tensor_tensor(block_, block_, conv[:, 6 + g, P:T].unsqueeze(1).to_broadcast([P, 4, P]), ALU.mult)
            ins.then_inc(*V.mark("cexp"))
            dve.wait_ge(*banks.ready("st"))
            dve.tensor_copy(m["st"], banks["st"][:, :]).then_inc(*banks.release("st"))
            for hd in range(4):
                dve.wait_ge(*banks.ready(f"s{hd}"))
                for q, (lo, hi) in enumerate(((0, P), (P, 3 * P))):
                    ins = dve.scalar_tensor_tensor(out=prob[:, hd, lo:hi], in0=banks[f"s{hd}"][:, lo:hi],
                                                   scalar=s["nq"][:, 4 * q + hd:4 * q + hd + 1], in1=prob[:, hd, lo:hi],
                                                   op0=ALU.subtract, op1=ALU.add)
                ins.then_inc(*banks.release(f"s{hd}"))
                dve.wait_ge(*banks.emptied(f"s{hd}"))
                for q, (lo, hi) in enumerate(((0, P), (P, 3 * P))):
                    ins = dve.reduce_max(s["mx"][:, 2 * hd + q:2 * hd + q + 1], prob[:, hd, lo:hi], AX.X)
            link(ins)
            dve.tensor_scalar(s["nmx"], s["mx"][:, 0:8], -1.0, None, ALU.mult).then_inc(*V.mark("scores"))
            dve.wait_ge(*A.at("exp"))
            link(dve.reciprocal(s["rs"], s["sums"]))
            for hd in range(4):
                for q, (lo, hi) in enumerate(((0, P), (P, 3 * P))):
                    i = 2 * hd + q
                    ins = dve.tensor_scalar(prob[:, hd, lo:hi], prob[:, hd, lo:hi], s["rs"][:, i:i + 1], None, ALU.mult)
            ins.then_inc(*V.mark("probs"))
            for hd in range(4):
                dve.wait_ge(*banks.ready(f"pt{hd}"))
                dve.tensor_copy(ptr[:, hd, :], banks[f"pt{hd}"][:, 0:3 * P]).then_inc(*banks.release(f"pt{hd}"))
            for i in range(2):
                dve.wait_ge(*banks.ready(f"y{i}"))
                for j in range(2):
                    c = 2 * i + j
                    ins = dve.scalar_tensor_tensor(out=y[:, c, :], in0=conv[:, c, :], scalar=par("ssd_d", c, 1),
                                                   in1=banks[f"y{i}"][:, j * T:(j + 1) * T], op0=ALU.mult, op1=ALU.add)
                ins.then_inc(*banks.release(f"y{i}"))
                dve.wait_ge(*banks.emptied(f"y{i}"))
                dve.wait_ge(*banks.emptied(f"z{i}"))
                half = slice(512 * i, 512 * i + 512)
                ins = dve.tensor_tensor(m["y"][:, half], m["y"][:, half], m["zs"][:, half], ALU.mult)
                if i == 0:
                    link(ins)
            ins.then_inc(*V.mark("y_gated"))
            dve.wait_ge(*banks.ready("ln_mean"))
            lnx = chunks(m["lnx"], 2)
            dve.tensor_scalar(var[:, 0:T], banks["ln_mean"][:, 0:T], 1.0 / 256, None, ALU.mult).then_inc(*banks.release("ln_mean"))
            dve.wait_ge(*banks.emptied("ln_mean"))
            dve.tensor_tensor(lnx, lx, var[:, 0:T].unsqueeze(1).to_broadcast([P, 2, T]), ALU.subtract)\
               .then_inc(*V.mark("ln_centred"))
            dve_rms(1, T)
            dve.tensor_tensor(lnx, lnx, rst[:, 0:T].unsqueeze(1).to_broadcast([P, 2, T]), ALU.mult).then_inc(*V.mark("ln_norm"))
            dve_rms(2, 2 * T, V.at("ln_norm"))
            for c in range(4):
                ins = dve.scalar_tensor_tensor(out=y[:, c, :], in0=y[:, c, :], scalar=par("ssd_norm_g", c, 1),
                                               in1=rst[:, (c // 2) * T:(c // 2 + 1) * T], op0=ALU.mult, op1=ALU.mult)
            ins.then_inc(*V.mark("y_ssd"))
            dve_rms(3, T, V.at("y_ssd"))
            for c in range(2):
                ins = dve.scalar_tensor_tensor(out=y[:, 4 + c, :], in0=y[:, 4 + c, :], scalar=par("fox_norm_g", c, 1),
                                               in1=rst[:, 0:T], op0=ALU.mult, op1=ALU.mult)
            ins.then_inc(*V.mark("y_fox"))
            dve.wait_ge(ada_reduced, ADA)
            link(dve.tensor_tensor(mod[:, 16:48], mod_bank[:, 0:32], par("ada_b", 16, 32), ALU.add))
            for i in range(4):
                dve.wait_ge(*banks.ready(f"wo{i}"))
                for j in range(2):
                    c = 2 * i + j
                    ins = dve.scalar_tensor_tensor(out=xv[:, c, :], in0=banks[f"wo{i}"][:, j * T:(j + 1) * T],
                                                   scalar=mod[:, 16 + c:17 + c], in1=xv[:, c, :], op0=ALU.mult, op1=ALU.add)
                ins.then_inc(*banks.release(f"wo{i}"))
            for i in range(4):
                dve.wait_ge(*banks.emptied(f"wo{i}"))
            dve.scalar_tensor_tensor(out=s["gffn"], in0=mod[:, 32:40], scalar=1.0, in1=par("norm_ffn_g"),
                                     op0=ALU.add, op1=ALU.mult).then_inc(*V.mark("x1"))
            dve_rms(4, T)
            dve.wait_ge(*V.at("x1"))
            modulate(h, xv, s["gffn"], mod[:, 24:32], zq).then_inc(*V.mark("h2"))
            dve.wait_ge(*V.at("h2"))
            v = lambda n, k=2: mo[n].rearrange("p (t j) -> p t j", t=k)
            rl = v("rl")
            dve.wait_ge(*banks.ready("router"))
            dve.tensor_tensor(rl, chunks(banks["router"][:, 0:72], 2), par("b_router").unsqueeze(1).to_broadcast([P, 2, 36]),
                              ALU.add).then_inc(*banks.release("router"))
            dve.wait_ge(*banks.emptied("router"))
            iota = con("iota")

            def first_max(values, best, diff, index_, hot, n, mark=None):
                link(dve.tensor_reduce(mo[best], values, AX.X, ALU.max))
                ins = dve.tensor_tensor(v(diff), values, mo[best].unsqueeze(2).to_broadcast([P, 2, n]), ALU.subtract)
                if mark:
                    ins.then_inc(*R.mark(mark))
                    dve.wait_ge(*R.at(mark))
                else:
                    link(ins)
                t_ = "gt" if n == 4 else "et"
                link(dve.tensor_scalar(v(t_), v(diff), 0.0, 64.0, ALU.is_lt, ALU.mult))
                link(dve.tensor_tensor(v(t_), v(t_), iota[:, 0:n].unsqueeze(1).to_broadcast([P, 2, n]), ALU.add))
                link(dve.tensor_reduce(mo[index_], v(t_), AX.X, ALU.min))
                link(dve.tensor_tensor(hot, iota[:, 0:n].unsqueeze(1).to_broadcast([P, 2, n]),
                                       mo[index_].unsqueeze(2).to_broadcast([P, 2, n]), ALU.is_equal))

            first_max(rl[:, :, 0:4], "gm", "gd", "gi", v("ohg"), 4, "gd")
            ep = mo["ep"].rearrange("p (t g j) -> p t g j", t=2, g=4)
            for t in range(TT):
                ins = dve.tensor_tensor(ep[:, t], rl[:, t, 4:36].rearrange("p (g j) -> p g j", g=4),
                                        v("ohg")[:, t, :].unsqueeze(2).to_broadcast([P, 4, 8]), ALU.mult)
            link(ins)
            for t in range(TT):
                ins = dve.tensor_reduce(v("el")[:, t, :], ep[:, t].rearrange("p g j -> p j g"), AX.X, ALU.add)
            link(ins)
            oh8 = mo["oh8"].rearrange("p (k t j) -> p k t j", k=2, t=2)
            first_max(v("el"), "m1", "ed", "ei", oh8[:, 0], 8)
            link(dve.scalar_tensor_tensor(out=v("el2"), in0=oh8[:, 0], scalar=-1e30, in1=v("el"), op0=ALU.mult, op1=ALU.add))
            first_max(v("el2"), "m2", "ed", "ei", oh8[:, 1], 8)
            dve.tensor_tensor(mo["md"], mo["m2"], mo["m1"], ALU.subtract).then_inc(*R.mark("md"))
            oh = mo["oh"].rearrange("p (k t g j) -> p k t g j", k=2, t=2, g=4)
            for k in range(2):
                for t in range(TT):
                    ins = dve.tensor_tensor(oh[:, k, t], v("ohg")[:, t, :].unsqueeze(2).to_broadcast([P, 4, 8]),
                                            oh8[:, k, t, :].unsqueeze(1).to_broadcast([P, 4, 8]), ALU.mult)
            link(ins)
            ohk = mo["oh"].rearrange("p (k n) -> p k n", k=2)
            dve.tensor_tensor(mo["hit"], ohk[:, 0], ohk[:, 1], ALU.add).then_inc(*R.mark("hits"))
            dve.wait_ge(*banks.ready("pos"))
            cnt = banks["pos"][:, 64:96]
            link(dve.tensor_scalar(mo["x"], cnt, float(SLOTS), None, ALU.is_gt))
            for n in (2, 3):
                link(dve.scalar_tensor_tensor(out=mo["x"], in0=cnt, scalar=float(n * SLOTS), in1=mo["x"], op0=ALU.is_gt, op1=ALU.add))
            link(dve.tensor_tensor_scan(out=mo["incl"], data0=ones[:, 0:32], data1=mo["x"], initial=0.0, op0=ALU.mult, op1=ALU.add))
            link(dve.tensor_tensor(mo["excl"], mo["incl"], mo["x"], ALU.subtract))
            prod = v("prod")

            def pick(out, table, shape_over_kt=None):
                for k in range(2):
                    ins = dve.tensor_tensor(prod[:, k, :].rearrange("p (t n) -> p t n", t=2),
                                            ohk[:, k, :].rearrange("p (t n) -> p t n", t=2), table, ALU.mult)
                link(ins)
                return dve.tensor_reduce(mo[out], mo["prod"].rearrange("p (a n) -> p a n", a=4), AX.X, ALU.add)

            pick("pos", chunks(banks["pos"][:, 0:64], 2)).then_inc(*banks.release("pos"))
            dve.wait_ge(*banks.emptied("pos"))
            link(pick("e", iota.unsqueeze(1).to_broadcast([P, 2, 32])))
            link(pick("ov", mo["excl"].unsqueeze(1).to_broadcast([P, 2, 32])))
            link(dve.tensor_scalar(mo["q"], mo["pos"], float(SLOTS), None, ALU.is_ge))
            link(dve.tensor_copy(mo["g0"], mo["q"]))
            for n in (2, 3):
                link(dve.scalar_tensor_tensor(out=mo["q"], in0=mo["pos"], scalar=float(n * SLOTS), in1=mo["q"], op0=ALU.is_ge, op1=ALU.add))
            link(dve.scalar_tensor_tensor(out=mo["slot"], in0=mo["q"], scalar=-float(SLOTS), in1=mo["pos"], op0=ALU.mult, op1=ALU.add))
            link(dve.scalar_tensor_tensor(out=mo["blk"], in0=mo["ov"], scalar=float(EXPERTS - 1), in1=mo["q"], op0=ALU.add, op1=ALU.add))
            link(dve.tensor_tensor(mo["blk"], mo["blk"], mo["e"], ALU.subtract))
            link(dve.tensor_tensor(mo["blk"], mo["blk"], mo["g0"], ALU.mult))
            link(dve.tensor_tensor(mo["blk"], mo["blk"], mo["e"], ALU.add))
            for i in range(TOP * TT):
                dve.tensor_scalar(chunks(mo["hot_slot"], 4)[:, i, :], con("slot_no"), mo["slot"][:, i:i + 1], None, ALU.is_equal)
                ins = dve.tensor_scalar(chunks(mo["hot_block"], 4)[:, i, :], con("block_no"), mo["blk"][:, i:i + 1],
                                        con("token")[:, i % TT:i % TT + 1], ALU.is_equal, ALU.mult)
            ins.then_inc(*R.mark("lists"))
            link(dve.scalar_tensor_tensor(out=mo["row"], in0=mo["blk"], scalar=float(SLOTS), in1=mo["slot"], op0=ALU.mult, op1=ALU.add))
            link(dve.tensor_copy(row_at[:], mo["row"]))
            dve.wait_ge(*banks.ready("lists"))
            dve.tensor_scalar(mo["listf"], banks["lists"][:, 0:LIST], 2.0, con("half"), ALU.mult, ALU.add).then_inc(*banks.release("lists"))
            dve.wait_ge(*banks.emptied("lists"))
            dve.tensor_copy(gather_at[:], mo["listf"]).then_inc(*R.mark("gather_at"))
            cmp = mo["cmp"].rearrange("p (j n) -> p j n", j=7)
            for j in range(SPARE):
                ins = dve.tensor_scalar(cmp[:, j, :], mo["incl"], float(j), None, ALU.is_le)
            link(ins)
            link(dve.tensor_reduce(mo["info"][:, 1:8], cmp, AX.X, ALU.add))
            link(dve.tensor_scalar(mo["info"][:, 1:8], mo["info"][:, 1:8], float(EXPERTS - 1), None, ALU.min))
            link(dve.tensor_copy(mo["info"][:, 0:1], mo["incl"][:, 31:32]))
            dve.tensor_copy(info[:], mo["info"]).then_inc(*R.mark("info"))
            dve.wait_ge(*S.at("ge"))
            link(dve.tensor_reduce(mo["gs"], v("ge"), AX.X, ALU.add))
            dve.wait_ge(*S.at("e2"))
            link(dve.tensor_scalar(mo["md"], mo["e2"], 1.0, None, ALU.add))
            link(dve.tensor_tensor(mo["gs"], mo["gs"], mo["md"], ALU.mult))
            link(dve.reciprocal(mo["w"][:, 0:2], mo["gs"]))
            dve.tensor_tensor(mo["w"][:, 2:4], mo["w"][:, 0:2], mo["e2"], ALU.mult).then_inc(*R.mark("weights"))

            def expert(e, p_, stored=None):
                dve.wait_ge(silu_done, e + 1)
                dve.tensor_tensor(hid[p_], psum[2 + p_][:, T:2 * T], sg_[p_], ALU.mult).then_inc(hid_done, 1)
                dve.wait_ge(ht_done, e + 1)
                dve.tensor_copy(ht[p_], psum[4][:, 0:T]).then_inc(ht_copied, 1)
                dve.wait_ge(y_done, e + 1)
                if stored:
                    dve.wait_ge(*stored)
                dve.tensor_copy(ys[p_], psum[5 + p_][:, :]).then_inc(y_copied, 1)

            def main(e, p_):
                stored = None if isinstance(e, int) else (y_stored[p_], 16 * (e - p_))
                expert(e, p_, stored)

            expert_loop(dve, main)
            for p_ in range(2):
                dve.wait_ge(y_stored[p_], 16 * EXPERTS)
            spare_loop(dve, lambda j: expert(EXPERTS + j, 0))
            yg = mo["yg"].rearrange("p (k t n) -> p k t n", k=2, t=2)
            for t in range(TT):
                dve.wait_ge(rows_gathered[t], 32)
                link(dve.tensor_scalar(yg[:, 0, t, :], yg[:, 0, t, :], mo["w"][:, t:t + 1], None, ALU.mult))
                dve.scalar_tensor_tensor(out=mo["comb"][:, t * D:(t + 1) * D], in0=yg[:, 1, t, :], scalar=mo["w"][:, 2 + t:3 + t],
                                         in1=yg[:, 0, t, :], op0=ALU.mult, op1=ALU.add).then_inc(*R.mark(f"comb{t}"))
            for t in range(TT):
                for half in range(2):
                    dve.wait_ge(*banks.ready(f"moe{t}{half}"))
                    for c in range(4):
                        cc = 4 * half + c
                        ins = dve.scalar_tensor_tensor(out=xv[:, cc, t * P:(t + 1) * P], in0=banks[f"moe{t}{half}"][:, c * P:(c + 1) * P],
                                                       scalar=mod[:, 40 + cc:41 + cc], in1=xv[:, cc, t * P:(t + 1) * P],
                                                       op0=ALU.mult, op1=ALU.add)
                    ins.then_inc(*banks.release(f"moe{t}{half}"))
                    dve.wait_ge(*banks.emptied(f"moe{t}{half}"))
            dve.nop().then_inc(*R.mark("x2"))
            dve_rms(5, T)
            for c in range(DC):
                ins = dve.scalar_tensor_tensor(out=xv[:, c, :], in0=xv[:, c, :], scalar=par("final_norm_g", c, 1), in1=rst[:, 0:T],
                                               op0=ALU.mult, op1=ALU.mult)
            ins.then_inc(*R.mark("final"))
            dve.wait_ge(*R.at("final"))
            dve.memset(gn_eps[:], 64e-5)
            full = work[:, 0:2056].rearrange("p (c t) -> p c t", c=DC)
            link(dve.memset(full[:, :, 0:1], 0.0))
            xn, dx = full[:, :, 1:T + 1], chunks(w_["dx"], 8)
            dve_rms(6, T)
            for c in range(DC):
                ins = dve.scalar_tensor_tensor(out=xn[:, c, :], in0=xv[:, c, :], scalar=par("norm_pre_2", c, 1), in1=rst[:, 0:T],
                                               op0=ALU.mult, op1=ALU.mult)
            ins.then_inc(*W.mark("xn"))
            dve.wait_ge(*W.at("xn"))
            link(dve.tensor_tensor(dx, full[:, :, 0:T], xn, ALU.subtract))
            link(dve.tensor_scalar(one_ka[:], par("a_k_a_2"), -1.0, 1.0, ALU.mult, ALU.add))
            mix = [chunks(w_["mix"][:, 2048 * i:2048 * (i + 1)], 8) for i in range(2)]

            def blend(i, which, after=None):
                if after:
                    dve.wait_ge(weights_used, POST_USED + after)
                for c in range(DC):
                    ins = dve.scalar_tensor_tensor(out=mix[i % 2][:, c, :], in0=dx[:, c, :], scalar=par("a_mu_2", 8 * which + c, 1),
                                                   in1=xn[:, c, :], op0=ALU.mult, op1=ALU.add)
                ins.then_inc(*W.mark(f"mix{i}"))

            blend(0, 4)
            blend(1, 5)
            dve.wait_ge(*banks.ready("lora0"))
            blend(2, 0)
            dve.wait_ge(*banks.ready("lora1"))
            blend(3, 1)
            L, lw, kk = ar["cum"], w_["lw"], ar["kk"]
            dve.wait_ge(*X.at("sigw"))
            link(dve.tensor_scalar(lw, lw, -0.6065306597126334, None, ALU.mult))
            link(dve.memset(ar["e2"], 1.0))
            link(dve.memset(ar["e2"].rearrange("p (c s) -> p c s", s=C)[:, :, 0:1], 0.0))
            link(dve.tensor_tensor_scan(out=L, data0=ar["e2"], data1=lw, initial=0.0, op0=ALU.mult, op1=ALU.add))
            blend(4, 2, 3)
            rr, kk_, aa = chunks(w_["r"], 8), chunks(w_["k"], 8), chunks(ar["a"], 8)
            dve.wait_ge(*X.at("k"))
            dve.wait_ge(*X.at("siga"))
            kkr = chunks(ar["e2"], 8)
            for c in range(DC):
                ins = dve.tensor_scalar(kkr[:, c, :], kk_[:, c, :], par("a_k_k_2", c, 1), None, ALU.mult)
            link(ins)
            dve.tensor_tensor(ar["e1"], ar["e2"], ar["e2"], ALU.mult).then_inc(*W.mark("kk_sq"))
            ta = chunks(ar["kk"], 8)
            for c in range(DC):
                ins = dve.tensor_scalar(ta[:, c, :], aa[:, c, :], par("a_k_a_2", c, 1), one_ka[:, c:c + 1], ALU.mult, ALU.add)
            link(ins)
            link(dve.tensor_tensor(w_["k"], w_["k"], ar["kk"], ALU.mult))
            dve.wait_ge(*X.at("r"))
            for c in range(DC):
                ins = dve.scalar_tensor_tensor(out=chunks(ar["e3"], 8)[:, c, :], in0=rr[:, c, :], scalar=par("a_r_k_2", c, 1), in1=kk_[:, c, :],
                                               op0=ALU.mult, op1=ALU.mult)
            ins.then_inc(*W.mark("bonus_in"))
            blend(5, 3, 5)
            dve.wait_ge(*banks.ready("bonus3"))
            dve.tensor_tensor(ar["e3"], L, lw, ALU.subtract).then_inc(*W.mark("args"))
            dve.wait_ge(*W.at("args"))
            for i in range(4):
                dve.tensor_copy(lw[:, 512 * i:512 * (i + 1)], banks[f"bonus{i}"][:, :]).then_inc(*banks.release(f"bonus{i}"))
            dve.wait_ge(*X.at("kk_norm"))
            link(dve.tensor_scalar(kk, kk, 1e-12, None, ALU.max))
            link(dve.reciprocal(kk, kk))
            dve.tensor_tensor(kk, kk, ar["e2"], ALU.mult).then_inc(*W.mark("kk"))
            dve.wait_ge(*W.at("kk"))
            link(dve.tensor_tensor(ar["a"], ar["a"], kk, ALU.mult))
            dve.wait_ge(*X.at("exp"))
            four = lambda ap: ap.rearrange("p (h c s) -> p h c s", h=HP, c=NC)
            two = lambda ap, e: ap.rearrange("p (h c e s) -> p h c e s", h=HP, c=2, e=2)[:, :, :, e, :]
            kb2 = work[:, 0:4096].rearrange("p (h c e k s) -> p h c e k s", h=HP, c=2, e=2, k=2)
            dve.tensor_copy(pc[:].rearrange("p (h c) -> p h c", h=HP), four(ar["e1"])[:, :, :, C - 1])
            dve.wait_ge(*X.at("exp2"))
            dve.wait_ge(*W.at("mix5"))
            for e in range(2):
                dve.tensor_tensor(kb2[:, :, :, e, e, :], two(w_["k"], e), two(ar["e2"], e), ALU.mult)
                ins = dve.tensor_tensor(kb2[:, :, :, e, 1 - e, :], two(ar["a"], e), two(ar["e2"], e), ALU.mult)
            ins.then_inc(*W.mark("kb"))
            dve.wait_ge(*W.at("kb"))
            for i in range(4):
                dve.wait_ge(*banks.emptied(f"bonus{i}"))
            dve.tensor_copy(w_["k"], lw)
            dve.wait_ge(weights_used, POST_USED + 9)
            dve.tensor_tensor(kr[:, :, :, 0, :], four(kk), four(ar["e3"]), ALU.mult).then_inc(*W.mark("e3_used"))
            dve.tensor_tensor(kr[:, :, :, 1, :], four(w_["r"]), four(ar["e1"]), ALU.mult).then_inc(*W.mark("kr"))
            dve.wait_ge(*W.at("kr"))
            for half in range(2):
                for c in range(NC):
                    for hd in range(2):
                        name = f"sc{half}{c}{hd}"
                        dve.wait_ge(*banks.ready(name))
                        out = sc_[:, 8 * half:8 * half + 8, c, :].rearrange("p (j e) n -> p j e n", e=2)[:, :, hd, :]
                        dve.tensor_tensor(out, chunks(banks[name][:, :], 4),
                                          con(("rwkv_even", "rwkv_odd")[c % 2]).unsqueeze(1).to_broadcast([P, 4, P]), ALU.mult)\
                           .then_inc(*banks.release(name))
            for half in range(2):
                for c in range(NC):
                    for hd in range(2):
                        dve.wait_ge(*banks.emptied(f"sc{half}{c}{hd}"))

            def blocks_of(q):
                dve.tensor_copy(xmt[0:64, :, 0:64], sc_[0:64, :, 2 * q + 1, 0:64])
                dve.tensor_copy(xmt[64:128, :, 64:128], sc_[64:128, :, 2 * q, 0:64]).then_inc(*W.mark(f"xmt{q}"))

            dve.wait_ge(corners_zero, 1)
            blocks_of(0)
            for q in range(2):
                dve.wait_ge(*W.at(f"xmt{q}"))
                dve.tensor_tensor(inv, xmt, ident.unsqueeze(1).to_broadcast([P, 16, P]), ALU.add).then_inc(*W.mark(f"inv{q}"))
                dve.wait_ge(*W.at(f"inv{q}"))
                for level in range(1, 6):
                    if level < 5:
                        for h4 in range(4):
                            dve.wait_ge(*banks.ready(f"xt{q}_{level}_{h4}"))
                            dve.tensor_copy(xmt[:, 4 * h4:4 * h4 + 4, :], chunks(banks[f"xt{q}_{level}_{h4}"][:, :], 4))\
                               .then_inc(*banks.release(f"xt{q}_{level}_{h4}"))
                    elif q == 0:
                        dve.wait_ge(*banks.ready("x0_5_3"))
                        for h4 in range(4):
                            dve.wait_ge(*banks.emptied(f"xt0_4_{h4}"))
                        blocks_of(1)
                    for h4 in range(4):
                        dve.wait_ge(*banks.ready(f"inv{q}_{level}_{h4}"))
                        block_ = inv[:, 4 * h4:4 * h4 + 4, :]
                        dve.tensor_tensor(block_, block_, chunks(banks[f"inv{q}_{level}_{h4}"][:, :], 4), ALU.add)\
                           .then_inc(*banks.release(f"inv{q}_{level}_{h4}"))
                for h4 in range(4):
                    dve.wait_ge(*banks.emptied(f"inv{q}_5_{h4}"))
                dve.tensor_copy(sc_[0:64, :, 2 * q + 1, 0:64], inv[0:64, :, 0:64])
                link(dve.tensor_copy(sc_[64:128, :, 2 * q, 0:64], inv[64:128, :, 64:128]))
            dve.memset(state, 0.0).then_inc(*W.mark("placed"))
            dve.wait_ge(*W.at("placed"))
            pcv = pc[:].rearrange("p (h c) -> p h c", h=HP)
            for c in range(NC):
                rows = slice(64, 128) if c % 2 == 0 else slice(0, 64)
                dve.wait_ge(*banks.ready(f"w{c}0"))
                dve.tensor_copy(wsb[rows, 0:512], banks[f"w{c}0"][rows, :]).then_inc(*banks.release(f"w{c}0"))
                dve.wait_ge(*banks.ready(f"u{c}0"))
                dve.tensor_copy(vu[rows, c, 0:512], banks[f"u{c}0"][rows, :]).then_inc(*banks.release(f"u{c}0"))
                if c < NC - 1:
                    dve.wait_ge(*banks.ready(f"yr{c}"))
                    for half in range(2):
                        for hd in range(2):
                            r = slice(64 * hd, 64 * hd + 64)
                            st = state[r, 4 * half:4 * half + 4, 64 * hd:64 * hd + 64]
                            new = chunks(banks[f"ds{c}{half}"][r, :], 4)[:, :, 64 * hd:64 * hd + 64]
                            ins = dve.tensor_tensor(st, st, new, ALU.add)
                            if hd == 0:
                                link(ins)
                        ins.then_inc(*banks.release(f"ds{c}{half}"))
                        dve.wait_ge(*banks.emptied(f"ds{c}{half}"))
                    for hd in range(2):
                        r = slice(64 * hd, 64 * hd + 64)
                        st = state[r, :, 64 * hd:64 * hd + 64]
                        ins = dve.tensor_tensor(st, st, pcv[r, :, c].unsqueeze(2).to_broadcast([64, HP, 64]), ALU.mult)
                    ins.then_inc(*W.mark(f"st{c}"))
                    dve.wait_ge(*W.at(f"st{c}"))
            dve.nop().then_inc(*W.mark(f"st{NC - 1}"))
            bonus = w_["k"]
            vt = w_["r"]
            for c in range(NC):
                dve.wait_ge(*banks.ready(f"vt{c}"))
                part = slice(c * C, (c + 1) * C)
                dve.tensor_tensor(chunks(vt, 8)[:, :, part], chunks(banks[f"vt{c}"][:, :], 8), chunks(bonus, 8)[:, :, part], ALU.mult)\
                   .then_inc(*banks.release(f"vt{c}"))
            yv = w_["lw"]
            for i in range(4):
                part = slice(512 * i, 512 * (i + 1))
                dve.wait_ge(*banks.ready(f"gmean{i}"))
                dve.scalar_tensor_tensor(out=tmp[0][:, part], in0=banks[f"gmean{i}"][:, :], scalar=-1.0 / 64, in1=yv[:, part],
                                         op0=ALU.mult, op1=ALU.add).then_inc(*banks.release(f"gmean{i}"))
            dve.wait_ge(*banks.emptied("gmean3"))
            dve.nop().then_inc(*W.mark("centred"))
            dve.wait_ge(*X.at("g"))
            for c in range(DC):
                part = slice(c * T, (c + 1) * T)
                dve.scalar_tensor_tensor(out=tmp[3][:, part], in0=tmp[0][:, part], scalar=par("a_lnx_g_2", c, 1), in1=w_["g"][:, part],
                                         op0=ALU.mult, op1=ALU.mult)
                ins = dve.scalar_tensor_tensor(out=vt[:, part], in0=vt[:, part], scalar=par("a_lnx_b_2", c, 1), in1=w_["g"][:, part],
                                               op0=ALU.add, op1=ALU.mult)
            link(ins)
            dve.wait_ge(*banks.emptied("gvar"))
            link(dve.reciprocal(gn_rstd[:], gn_root[:]))
            dve.tensor_copy(tmp[0].rearrange("p (h n) -> p h n", n=64), gn_rstd[:].unsqueeze(2).to_broadcast([P, 32, 64]))\
               .then_inc(*W.mark("gn_rstd"))
            for i in range(4):
                part = slice(512 * i, 512 * (i + 1))
                dve.wait_ge(*banks.ready(f"gb{i}"))
                dve.tensor_tensor(yv[:, part], tmp[3][:, part], banks[f"gb{i}"][:, :], ALU.mult).then_inc(*banks.release(f"gb{i}"))
                dve.wait_ge(*banks.emptied(f"gb{i}"))
                ins = dve.tensor_tensor(yv[:, part], yv[:, part], vt[:, part], ALU.add)
            ins.then_inc(*W.mark("y"))

            def add_normed(k, buf, gain, at):
                dve_rms(k, T)
                link(dve.tensor_tensor(chunks(buf, 8), chunks(buf, 8), rst[:, 0:T].unsqueeze(1).to_broadcast([P, DC, T]), ALU.mult))
                for c in range(DC):
                    ins = dve.scalar_tensor_tensor(out=xv[:, c, :], in0=buf[:, c * T:(c + 1) * T], scalar=par(gain, at + c, 1),
                                                   in1=xv[:, c, :], op0=ALU.mult, op1=ALU.add)
                return ins

            add_normed(7, tmp[0], "norm_post_2", 0).then_inc(*W.mark("attn_in"))
            dve.wait_ge(*W.at("attn_in"))
            lam = par("b_lambda_2").rearrange("p (a b n) -> p a b n", a=2, b=2)
            link(dve.tensor_tensor(chunks(z["lp"], 2), lam[:, :, 0, :], lam[:, :, 1, :], ALU.mult))
            dve.memset(z["eps"], 1e-5)
            dve.tensor_scalar(z["sub"], par("b_subln_2"), 1.0 - lam_init, None, ALU.mult)
            m3 = chunks(z["mask3"], 3)
            dve.memset(m3[:, 1, :], 0.0)
            dve.tensor_copy(m3[:, 0, :], con("causal"))
            link(dve.tensor_copy(m3[:, 2, :], con("causal")))

            def lam_sum():
                dve.tensor_reduce(z["ls"], chunks(z["lp"], 2), AX.X, ALU.add).then_inc(*Y.mark("lam_sum"))

            def ple(l, mark):
                for i in range(4):
                    dve.wait_ge(*banks.emptied(f"pe{l}_{i}"))
                    dve.wait_ge(*banks.emptied(f"pg{l}_{i}"))
                dve.tensor_tensor(z["gb"], z["gb"], z["eb"], ALU.mult).then_inc(*Y.mark(f"ge{l}"))
                add_normed((8, 11)[l], z["gb"], "ple_norm_2", 8 * l).then_inc(*Y.mark(mark))
                dve.wait_ge(*Y.at(mark))

            lam_sum()
            dve.wait_ge(*Z.at("lam_exp"))
            link(dve.tensor_tensor(z["nlam"], z["le"][:, 1:2], z["le"][:, 0:1], ALU.subtract))
            link(dve.tensor_scalar(z["nlam"], z["nlam"], -lam_init, None, ALU.add))
            ple(0, "x3")
            dve_rms(9, T)
            for name, gain, at in (("hkv", "kv_norm_2", 0), ("hq", "norm_pre_2", 8)):
                for c in range(DC):
                    ins = dve.scalar_tensor_tensor(out=z[name][:, c * T:(c + 1) * T], in0=xv[:, c, :], scalar=par(gain, at + c, 1),
                                                   in1=rst[:, 0:T], op0=ALU.mult, op1=ALU.mult)
                ins.then_inc(*Y.mark(name))
            for name, banks_of, ready in (("kt", "kr", "k"), ("qt", "qr", "q")):
                dve.wait_ge(*Z.at(ready))
                for i in range(4):
                    dve.wait_ge(*banks.ready(f"{banks_of}{i}"))
                    dve.tensor_tensor(chunks(z["eb"], 8)[:, 2 * i:2 * i + 2, :], chunks(banks[f"{banks_of}{i}"][:, :], 2),
                                      con("sin").unsqueeze(1).to_broadcast([P, 2, T]), ALU.mult).then_inc(*banks.release(f"{banks_of}{i}"))
                link(dve.tensor_tensor(chunks(z[name], 8), chunks(z[name], 8), con("cos").unsqueeze(1).to_broadcast([P, 8, T]), ALU.mult))
                for i in range(4):
                    dve.wait_ge(*banks.emptied(f"{banks_of}{i}"))
                dve.tensor_tensor(z[name], z[name], z["eb"], ALU.add).then_inc(*Y.mark(name))
                dve.wait_ge(*Y.at(name))

            def combine(hh):
                dve.wait_ge(*Z.at(f"dx{hh}"))
                link(dve.reciprocal(z["rs"][:, 4 * hh:4 * hh + 4], z["sums"][:, 4 * hh:4 * hh + 4]))
                link(dve.tensor_scalar(z["rs"][:, 4 * hh + 2:4 * hh + 4], z["rs"][:, 4 * hh + 2:4 * hh + 4], z["nlam"], None, ALU.mult))
                spans = ((0, P), (P, 3 * P))
                for q, (lo, hi) in enumerate(spans):
                    ins = dve.tensor_scalar(dprob[:, hh, 1, lo:hi], dprob[:, hh, 1, lo:hi], z["rs"][:, 4 * hh + 2 + q:4 * hh + 3 + q], None, ALU.mult)
                link(ins)
                for q, (lo, hi) in enumerate(spans):
                    ins = dve.scalar_tensor_tensor(out=dprob[:, hh, 0, lo:hi], in0=dprob[:, hh, 0, lo:hi],
                                                   scalar=z["rs"][:, 4 * hh + q:4 * hh + q + 1], in1=dprob[:, hh, 1, lo:hi],
                                                   op0=ALU.mult, op1=ALU.add)
                return ins

            def turned(hh):
                dve.wait_ge(*banks.ready(f"at{hh}"))
                dve.tensor_copy(dat[:, hh, :], banks[f"at{hh}"][:, 0:3 * P]).then_inc(*banks.release(f"at{hh}"))

            for hh in range(8):
                for c in range(2):
                    dve.wait_ge(*banks.ready(f"d{hh}{c}"))
                    dve.tensor_tensor(dprob[:, hh, c, :], banks[f"d{hh}{c}"][:, 0:3 * P], z["mask3"], ALU.add)\
                       .then_inc(*banks.release(f"d{hh}{c}"))
                for c in range(2):
                    dve.wait_ge(*banks.emptied(f"d{hh}{c}"))
                    for q, (lo, hi) in enumerate(((0, P), (P, 3 * P))):
                        i = 4 * hh + 2 * c + q
                        ins = dve.reduce_max(z["mx"][:, i:i + 1], dprob[:, hh, c, lo:hi], AX.X)
                link(ins)
                dve.tensor_scalar(z["nmx"][:, 4 * hh:4 * hh + 4], z["mx"][:, 4 * hh:4 * hh + 4], -1.0, None, ALU.mult).then_inc(*Y.mark(f"ds{hh}"))
                if hh:
                    combine(hh - 1).then_inc(*Y.mark(f"da{hh - 1}"))
                if hh > 1:
                    turned(hh - 2)
            combine(7).then_inc(*Y.mark("da7"))
            turned(6)
            turned(7)
            for i in range(4):
                dve.wait_ge(*banks.emptied(f"gg{i}"))
            dve.wait_ge(*Z.at("o_sq"))
            link(dve.scalar_tensor_tensor(out=z["eb"], in0=z["ot"], scalar=z["sub"], in1=z["gate"], op0=ALU.mult, op1=ALU.mult))
            dve.wait_ge(*banks.emptied("on"))
            dve.reciprocal(z["ors"], z["ort"]).then_inc(*Y.mark("o_rstd"))
            for i in range(4):
                part = slice(512 * i, 512 * (i + 1))
                dve.wait_ge(*banks.ready(f"ob{i}"))
                dve.tensor_tensor(z["ot"][:, part], z["eb"][:, part], banks[f"ob{i}"][:, :], ALU.mult).then_inc(*banks.release(f"ob{i}"))
            add_normed(10, z["gb"], "norm_post_2", 8).then_inc(*Y.mark("x4"))
            dve.wait_ge(*Y.at("x4"))
            ple(1, "x5")

        @block.gpsimd
        def _(pool):
            pool.wait_ge(*A.at("cond"))
            pool.wait_ge(ada_summed, ADA_DVE)
            for j in range(ADA_DVE, ADA):
                ada_sum(pool, pool_steps, j)
            pool.wait_ge(*V.at("h2"))
            pool.memset(mo["yg"], 0.0).then_inc(yg_zero, 1)

            def gather(block_, p_, done):
                pool.indirect_dma_start(out=xg[p_], out_offset=None, in_=a["hrow"],
                                        in_offset=bass.IndirectOffsetOnAxis(ap=gather_at[:, block_:block_ + 1], axis=0))\
                    .then_inc(done, 16)

            pool.wait_ge(*R.at("gather_at"))
            pool.wait_ge(h_stored, 16)
            for e in range(EXPERTS):
                if e >= 2:
                    pool.wait_ge(xt_done, e - 1)
                gather(e, e % 2, gathered[e % 2])
            for p_ in range(2):
                pool.wait_ge(y_stored[p_], 16 * EXPERTS)
            spare = pool.value_load(info[0:1, 0:1], min_val=0, max_val=SPARE)
            with pool.If(spare > 0):
                for j in range(SPARE):
                    if j:
                        pool.wait_ge(spare_stored, 32 * j)
                    gather(EXPERTS + j, 0, spare_gathered)
                pool.wait_ge(spare_stored, 32 * SPARE)
            pool.wait_ge(yrow_cleared, 16)
            for t in range(TT):
                for k in range(TOP):
                    out = mo["yg"][:, (k * TT + t) * D:(k * TT + t + 1) * D]
                    pool.indirect_dma_start(out=out, out_offset=None, in_=a["yrow"],
                                            in_offset=bass.IndirectOffsetOnAxis(ap=row_at[:, k * TT + t:k * TT + t + 1], axis=0))\
                        .then_inc(rows_gathered[t], 16)
            pool.wait_ge(*R.at("final"))
            for c in range(NC):
                rows = slice(64, 128) if c % 2 == 0 else slice(0, 64)
                ins = pool.memset(vu[rows, c, :], 0.0)
            ins.then_inc(vu_zero, 1)
            pool.wait_ge(*banks.ready("sc131"))
            pool.memset(xmt[0:64, :, 64:128], 0.0)
            pool.memset(xmt[64:128, :, 0:64], 0.0).then_inc(corners_zero, 1)

        @block.sync
        def _(sp):
            sp.dma_start(prm[:], a["params"]).then_inc(params_loaded, 16)
            sp.dma_start(cst[:], a["tables"]).then_inc(params_loaded, 16)
            sp.dma_start(xt[:], a["x"]).then_inc(x_loaded, 16)
            for n, (name, parts) in enumerate(tiles):
                if n >= RING:
                    sp.wait_ge(*tile_used(n - RING))
                for at, pitch, view in parts:
                    width = view.shape[2]
                    dst = ring[:, slot_of[name] * SLOT:slot_of[name] * SLOT + pitch * DC].rearrange("p (c n) -> p c n", c=DC)[:, :, at:at + width]
                    sp.dma_start(dst, view).then_inc(slot_loaded[slot_of[name]], 16)
            def load_expert(e, p_, which=range(3)):
                for k in which:
                    name = ("w_gate", "w_up", "w_down")[k]
                    dst = ring[:, expert_slots[p_][k] * SLOT:(expert_slots[p_][k] + 1) * SLOT]
                    if isinstance(e, int):
                        sp.wait_ge(*tile_used(MOE_TILE + 3 * e + k - RING))
                    else:
                        sp.wait_ge(weights_used, 3 * e + (MOE_USED + k - RING + 1))
                    load_matrix(name, e, dst, slot_loaded[expert_slots[p_][k]])

            def load_matrix(name, e, dst, done):
                w = a[name][0][bass.ds(e, 1)].rearrange("e (c p) n -> p (e c) n", p=P)
                sp.dma_start(dst.rearrange("p (c n) -> p c n", n=w.shape[2]), w).then_inc(done, 16)

            def store_rows(e, p_, done):
                rows = a["yrow"].rearrange("(b s) n -> b s n", s=SLOTS)[bass.ds(e, 1)].rearrange("b s n -> (b s) n")
                for half in range(2):
                    sp.dma_start(rows[:, half * 512:(half + 1) * 512], ys[p_][64 * half:64 * half + 64, :]).then_inc(done, 16)

            load_expert(0, 0)
            load_expert(1, 1, range(2))
            sp.wait_ge(yg_zero, 1)
            spare_rows = a["yrow"].rearrange("(b p) n -> b (p n)", p=SLOTS)[EXPERTS:EXPERTS + SPARE].rearrange("b (q n) -> q b n", q=P)
            sp.dma_start(spare_rows, mo["yg"][:, 0:SPARE * 512].rearrange("p (b n) -> p b n", b=SPARE)).then_inc(yrow_cleared, 16)
            for t in range(TT):
                for half in range(2):
                    sp.wait_ge(*banks.emptied(f"hrow{t}{half}"))
            sp.dma_start(a["hrow"].rearrange("(t p two) n -> p t (two n)", t=TT, two=2), chunks(m["conv"], 2)).then_inc(h_stored, 16)
            load_expert(1, 1, (2,))
            with sp.Fori(0, EXPERTS // 2 - 1) as i:
                for p_ in range(2):
                    load_expert(2 * i + 2 + p_, p_)
                    sp.wait_ge(y_copied, 2 * i + p_ + 1)
                    store_rows(2 * i + p_, p_, y_stored[p_])
            for p_ in range(2):
                sp.wait_ge(y_copied, EXPERTS - 1 + p_)
                store_rows(EXPERTS - 2 + p_, p_, y_stored[p_])
            for p_ in range(2):
                sp.wait_ge(y_stored[p_], 16 * EXPERTS)
            sp.wait_ge(*R.at("info"))
            spare = sp.value_load(info[0:1, 0:1], min_val=0, max_val=SPARE)
            with sp.If(spare > 0):
                sp.wait_ge(yrow_cleared, 16)
                sp.wait_ge(weights_used, MOE_USED + 3 * EXPERTS)
                for j in range(SPARE):
                    if j:
                        sp.wait_ge(spare_used, 3 * j)
                    owner = sp.value_load(info[0:1, 1 + j:2 + j], min_val=0, max_val=EXPERTS - 1)
                    for k, name in enumerate(("w_gate", "w_up", "w_down")):
                        load_matrix(name, owner, ring[:, (3 + k) * SLOT:(4 + k) * SLOT], spare_loaded)
                    sp.wait_ge(y_copied, EXPERTS + j + 1)
                    store_rows(EXPERTS + j, 0, spare_stored)
                sp.wait_ge(spare_stored, 32 * SPARE)
            for t in range(TT):
                sp.wait_ge(rows_gathered[t], 32)
            for n, (name, parts) in enumerate(post):
                if name == "ple_w0":
                    sp.wait_ge(*W.at("centred"))
                    sp.dma_start(z["pt"], a["p"]).then_inc(pt_loaded, 16)
                sp.wait_ge(weights_used, POST_USED + n - 2)
                for at, size, rows, c, view in parts:
                    base = slot_of[name] * SLOT + at
                    dst = ring[0:rows, base:base + size].rearrange("p (c n) -> p c n", c=c)
                    sp.dma_start(dst, view).then_inc(slot_loaded[slot_of[name]], 16)
            sp.wait_ge(*Y.at("x5"))
            sp.dma_start(a["out"], xt[:]).then_inc(out_written, 16)
            sp.wait_ge(out_written, 16)


def tables():
    p, q = np.arange(P)[:, None], np.arange(P)[None, :]
    t = {}
    t["ident"] = p == q
    t["tri"] = p <= q
    t["tri_strict"] = p < q
    t["ones"] = np.ones((P, P))
    t["block_ones"] = (p // 64) == (q // 64)
    mask = np.where(q < 64, (p % 64) < (q % 64), (p % 64) <= (q % 64))
    t["rwkv_even"] = mask * np.where(p < 64, 1.0, -1.0)
    t["rwkv_odd"] = mask * np.where(p < 64, -1.0, 1.0)
    t["causal"] = np.where(q <= p, 0.0, -1e30)
    rot = np.zeros((P, P))
    for i in range(P):
        if i % 64 < 8:
            rot[i + 8, i] = -1.0
        elif i % 64 < 16:
            rot[i - 8, i] = 1.0
    t["rot"] = rot
    inv = (np.float32(500000.0) ** (-np.arange(0, 16, 2, dtype=np.float32) / np.float32(16))).astype(np.float32)
    ang = (np.arange(T, dtype=np.float32)[None, :] * inv[np.arange(P) % 8][:, None]).astype(np.float32)
    turned = (p % 64) < 16
    t["cos"] = np.where(turned, np.cos(ang), 1.0)
    t["sin"] = np.where(turned, np.sin(ang), 0.0)
    t["iota"] = np.broadcast_to(np.arange(32)[None, :], (P, 32))
    t["token"] = p + P * np.arange(2)[None, :]
    t["half"] = p // 64
    t["eps"] = np.full((P, 1), 1e-6)
    t["slot_no"] = np.broadcast_to(np.arange(P)[None, :] % SLOTS, (P, P))
    t["block_no"] = np.broadcast_to(np.arange(LIST)[None, :], (P, LIST))
    t["sign_even"] = np.where(p < 64, 1.0, -1.0)
    t["sign_odd"] = np.where(p < 64, -1.0, 1.0)
    return np.ascontiguousarray(np.concatenate([np.asarray(t[n], np.float32) for n, _ in CONST], 1))


def parameters(i):
    def col(a):
        a = a.reshape(-1, P)
        return a.T

    def taps(w):
        k, n = w.shape
        return w.reshape(k, n // P, P).transpose(2, 1, 0).reshape(P, -1)

    def row(a):
        return np.broadcast_to(a.reshape(1, -1), (P, a.size))

    one = {"ssd_conv_w": taps(i["ssd_conv_w"][0]), "cm_conv_w": taps(i["cm_conv_w"][0]),
           "ssd_d": col(np.repeat(i["ssd_d"][0], 64)),
           "ssd_dt_bias": row(i["ssd_dt_bias"]), "ssd_a_log": row(i["ssd_a_log"]), "fox_f_bias": row(i["fox_f_bias"]),
           "b_router": row(np.concatenate([i["b_router_group"][0], i["b_router_expert"][0]])),
           "b_lambda_2": row(i["b_lambda_2"])}
    return np.ascontiguousarray(np.concatenate([one[n] if n in one else col(i[n]) for n, _ in PARAM], 1))


def transposed(x):
    return np.ascontiguousarray(x.reshape(T, -1, P).transpose(2, 1, 0).reshape(P, -1))


WEIGHTS = ["ada_w", "w_in", "w_out", "w_router_group", "w_router_expert", "w_gate", "w_up", "w_down",
           "a_w_in_2", "a_w1_2", "a_w2_2", "a_a1_2", "a_a2_2", "a_w_out_2", "kv_w_2", "b_w_in_2", "b_w_out_2",
           "ple_w_2", "ple_gate_2"]


def scratch(nc):
    return {"hrow": nc.dram_tensor("hrow_scratch", (2 * T, D // 2), F32).ap(),
            "yrow": nc.dram_tensor("yrow_scratch", ((EXPERTS + SPARE) * SLOTS, D), F32).ap()}


def kernel(**inputs):
    import concourse.bacc as _bacc
    from concourse.bass_utils import run_bass_kernel_spmd as _run

    i = {n: np.asarray(v) for n, v in inputs.items()}
    nc = _bacc.Bacc("TRN2", target_bir_lowering=False, num_devices=1)
    given = {"params": parameters(i), "tables": tables(), "x": transposed(i["x"][0]),
             "p": np.concatenate([transposed(i["p_2"][0, 0]), transposed(i["p_2"][1, 0])], 1)}
    given.update({n: np.ascontiguousarray(i[n]) for n in WEIGHTS})
    a = {n: nc.dram_tensor(f"in_{n}", v.shape, F32, kind="ExternalInput").ap() for n, v in given.items()}
    a["out"] = nc.dram_tensor("out_x", (P, DC * T), F32, kind="ExternalOutput").ap()
    a.update(scratch(nc))
    program(nc, a)
    r = _run(nc, [{f"in_{n}": v for n, v in given.items()}], core_ids=[0])
    return np.ascontiguousarray(r.results[0]["out_x"].reshape(P, DC, T).transpose(2, 1, 0).reshape(1, T, D))
```
